# Optimizing a Trainium2 kernel written in Bass

```python
import jax, jax.numpy as jnp
from jax import lax
import numpy as np

D_MODEL = 1024
BATCH = 1
SEQ = 1024
DEPTH = 1
DEC_BATCH = 8
DEC_SEQ = 1
PAST_LEN = 8192
PAGE_SIZE = 128

D_CONV = D_MODEL // 2
CONV_W = 31
D_GMLP = D_MODEL // 2
GMLP_HEADS = 8
GMLP_HEAD_DIM = D_GMLP // GMLP_HEADS
CHUNK = 128
IN_W = 2 * D_CONV + 2 * D_GMLP + 2 * D_MODEL
PEER_HEADS = 8
N_KEYS = 128
N_EXPERTS = N_KEYS * N_KEYS
D_KEY = 256
TOPK = 16
PEER_BLOCK = 128
EPS = 1e-6

kernel_name = "hybrid_conv_gmlp_peer_adaln_step"

def rmsnorm(x, g):
    xf = x.astype(jnp.float32)
    y = xf * lax.rsqrt(jnp.mean(xf * xf, axis=-1, keepdims=True) + EPS)
    return (y * g.astype(jnp.float32)).astype(x.dtype)

def layernorm(x, g, b):
    xf = x.astype(jnp.float32)
    mu = jnp.mean(xf, axis=-1, keepdims=True)
    var = jnp.mean(jnp.square(xf - mu), axis=-1, keepdims=True)
    y = (xf - mu) * lax.rsqrt(var + EPS)
    return (y * g.astype(jnp.float32) + b.astype(jnp.float32)).astype(x.dtype)

def causal_dwconv(full, w, b):
    y = lax.conv_general_dilated(full, w[:, None, :], window_strides=(1,), padding="VALID",
                                 dimension_numbers=("NWC", "WIO", "NWC"),
                                 feature_group_count=full.shape[-1])
    return y + b

def chunk_spatial_gate(v, w_s, b_s):
    n, s, _ = v.shape
    L = min(CHUNK, s)
    vh = v.reshape(n, s // L, L, GMLP_HEADS, GMLP_HEAD_DIM)
    mask = jnp.tril(jnp.ones((L, L), dtype=bool))
    wm = jnp.where(mask[None], w_s[:, :L, :L], jnp.zeros((), w_s.dtype))
    sg = jnp.einsum("hij,ncjhd->ncihd", wm, vh) + b_s[:, :L].T[None, None, :, :, None]
    return sg.reshape(n, s, D_GMLP)

def peer_block(xb, w_q, k1, k2, u_tab, v_tab):
    tb = xb.shape[0]
    half = D_KEY // 2
    q = (xb @ w_q).reshape(tb, PEER_HEADS, D_KEY)
    s1 = jnp.einsum("thd,nd->thn", q[..., :half], k1)
    s2 = jnp.einsum("thd,nd->thn", q[..., half:], k2)
    sc1, i1 = lax.top_k(s1, TOPK)
    sc2, i2 = lax.top_k(s2, TOPK)
    cand = (sc1[..., :, None] + sc2[..., None, :]).reshape(tb, PEER_HEADS, TOPK * TOPK)
    cid = (i1[..., :, None] * N_KEYS + i2[..., None, :]).reshape(tb, PEER_HEADS, TOPK * TOPK)
    top, pos = lax.top_k(cand, TOPK)
    eid = jnp.take_along_axis(cid, pos, axis=-1).reshape(tb, PEER_HEADS * TOPK)
    g = jax.nn.softmax(top.astype(jnp.float32), axis=-1).astype(xb.dtype).reshape(tb, PEER_HEADS * TOPK)
    act = jax.nn.gelu(jnp.einsum("tnd,td->tn", u_tab[eid], xb), approximate=False)
    return jnp.einsum("tn,tnd->td", g * act, v_tab[eid])

def peer(xn, w_q, k1, k2, u_tab, v_tab):
    n, s, d = xn.shape
    tot = n * s
    nb = -(-tot // PEER_BLOCK)
    t = jnp.pad(xn.reshape(tot, d), ((0, nb * PEER_BLOCK - tot), (0, 0))).reshape(nb, PEER_BLOCK, d)
    out = lax.map(lambda xb: peer_block(xb, w_q, k1, k2, u_tab, v_tab), t)
    return out.reshape(nb * PEER_BLOCK, d)[:tot].reshape(n, s, d)

def layer(x, c, hist, w_ada, b_ada, g_mix, w_in, w_dw, b_dw, g_cn, b_cn, w_conv_out,
          g_v, b_v, w_s, b_s, w_gmlp_out, w_out, g_ffn, w_q, k1, k2, u_tab, v_tab):
    mod = jax.nn.silu(c) @ w_ada + b_ada
    sh1, sc1, gt1, sh2, sc2, gt2 = [m[:, None, :] for m in jnp.split(mod, 6, axis=-1)]
    n = rmsnorm(x, g_mix) * (1 + sc1) + sh1
    z = n @ w_in
    a_lin, a_gate, u, v, g_a, g_b = jnp.split(
        z, [D_CONV, 2 * D_CONV, 2 * D_CONV + D_GMLP, 2 * D_CONV + 2 * D_GMLP,
            2 * D_CONV + 2 * D_GMLP + D_MODEL], axis=-1)
    a = a_lin * jax.nn.sigmoid(a_gate)
    full = jnp.concatenate([hist, a], axis=1)
    new_hist = full[:, full.shape[1] - (CONV_W - 1):]
    a = jax.nn.silu(layernorm(causal_dwconv(full, w_dw, b_dw), g_cn, b_cn)) @ w_conv_out
    v = layernorm(v, g_v, b_v)
    b_br = (u * chunk_spatial_gate(v, w_s, b_s)) @ w_gmlp_out
    m = jax.nn.sigmoid(g_a) * a + jax.nn.sigmoid(g_b) * b_br
    x = x + gt1 * (m @ w_out)
    n2 = rmsnorm(x, g_ffn) * (1 + sc2) + sh2
    x = x + gt2 * peer(n2, w_q, k1, k2, u_tab, v_tab)
    return x, new_hist, v

def setup_inputs(seed: int = 0) -> dict:
    key = jax.random.key(seed)
    ks = jax.random.split(key, 32)

    def nrm(k, shape, scale):
        return scale * jax.random.normal(k, shape, jnp.float32)

    L = DEPTH
    return {
        "x_prompt": nrm(ks[0], (BATCH, SEQ, D_MODEL), 1.0),
        "x_sample": nrm(ks[1], (DEC_BATCH, DEC_SEQ, D_MODEL), 1.0),
        "state_conv": nrm(ks[2], (DEPTH, DEC_BATCH, CONV_W - 1, D_CONV), 0.5),
        "c_prompt": nrm(ks[3], (BATCH, D_MODEL), 1.0),
        "c_sample": nrm(ks[4], (DEC_BATCH, D_MODEL), 1.0),
        "w_ada": nrm(ks[5], (L, D_MODEL, 6 * D_MODEL), 0.5 * D_MODEL ** -0.5),
        "b_ada": nrm(ks[6], (L, 6 * D_MODEL), 0.02),
        "g_mix": 1.0 + nrm(ks[7], (L, D_MODEL), 0.05),
        "w_in": nrm(ks[8], (L, D_MODEL, IN_W), D_MODEL ** -0.5),
        "w_dw": nrm(ks[9], (L, CONV_W, D_CONV), CONV_W ** -0.5),
        "b_dw": nrm(ks[10], (L, D_CONV), 0.02),
        "g_cn": 1.0 + nrm(ks[11], (L, D_CONV), 0.05),
        "b_cn": nrm(ks[12], (L, D_CONV), 0.02),
        "w_conv_out": nrm(ks[13], (L, D_CONV, D_MODEL), D_CONV ** -0.5),
        "g_v": 1.0 + nrm(ks[14], (L, D_GMLP), 0.05),
        "b_v": nrm(ks[15], (L, D_GMLP), 0.02),
        "w_s": nrm(ks[16], (L, GMLP_HEADS, CHUNK, CHUNK), CHUNK ** -0.5),
        "b_s": 1.0 + nrm(ks[17], (L, GMLP_HEADS, CHUNK), 0.1),
        "w_gmlp_out": nrm(ks[18], (L, D_GMLP, D_MODEL), D_GMLP ** -0.5),
        "w_out": nrm(ks[19], (L, D_MODEL, D_MODEL), D_MODEL ** -0.5),
        "g_ffn": 1.0 + nrm(ks[20], (L, D_MODEL), 0.05),
        "w_q": nrm(ks[21], (L, D_MODEL, PEER_HEADS * D_KEY), D_MODEL ** -0.5),
        "k1": nrm(ks[22], (L, N_KEYS, D_KEY // 2), (D_KEY // 2) ** -0.5),
        "k2": nrm(ks[23], (L, N_KEYS, D_KEY // 2), (D_KEY // 2) ** -0.5),
        "u_tab": nrm(ks[24], (L, N_EXPERTS, D_MODEL), D_MODEL ** -0.5),
        "v_tab": nrm(ks[25], (L, N_EXPERTS, D_MODEL), (PEER_HEADS * TOPK) ** -0.5),
        "g_final": 1.0 + nrm(ks[26], (D_MODEL,), 0.05),
    }

def reference(x_prompt, x_sample, state_conv, c_prompt, c_sample, w_ada, b_ada, g_mix, w_in,
              w_dw, b_dw, g_cn, b_cn, w_conv_out, g_v, b_v, w_s, b_s, w_gmlp_out, w_out,
              g_ffn, w_q, k1, k2, u_tab, v_tab, g_final):
    hp, hs = x_prompt, x_sample
    hist_p, hist_s, v_s = [], [], []
    for l in range(DEPTH):
        lp = (w_ada[l], b_ada[l], g_mix[l], w_in[l], w_dw[l], b_dw[l], g_cn[l], b_cn[l],
              w_conv_out[l], g_v[l], b_v[l], w_s[l], b_s[l], w_gmlp_out[l], w_out[l],
              g_ffn[l], w_q[l], k1[l], k2[l], u_tab[l], v_tab[l])
        zero_hist = jnp.zeros((x_prompt.shape[0], CONV_W - 1, D_CONV), x_prompt.dtype)
        hp, hp_hist, _ = layer(hp, c_prompt, zero_hist, *lp)
        hs, hs_hist, hs_v = layer(hs, c_sample, state_conv[l], *lp)
        hist_p.append(hp_hist)
        hist_s.append(hs_hist)
        v_s.append(hs_v)
    y_prompt = rmsnorm(hp, g_final)
    y_sample = rmsnorm(hs, g_final)
    return (y_prompt, y_sample, jnp.stack(hist_p), jnp.stack(hist_s), jnp.stack(v_s))


_drawn_inputs = setup_inputs


def setup_inputs(seed=0):
    import zlib

    import numpy as np

    out = dict(_drawn_inputs(seed))
    spreads = {}
    factors = {'b_dw': 8.0,
     'g_cn': 8.0,
     'b_cn': 8.0,
     'b_v': 2.855,
     'b_s': 3.538,
     'g_ffn': 8.0,
     'w_q': 4.125,
     'k1': 4.097,
     'k2': 4.193,
     'u_tab': 4.589,
     'v_tab': 4.108}
    for name, (base, spread) in spreads.items():
        noise = np.random.default_rng([zlib.crc32(name.encode()), seed]).standard_normal(out[name].shape)
        drawn = base * np.exp(spread * noise) if base else spread * noise
        out[name] = __import__('jax').numpy.asarray(drawn.astype(out[name].dtype))
    for name, factor in factors.items():
        out[name] = (out[name] * factor).astype(out[name].dtype)
    return out
```

```python
from contextlib import ExitStack

import numpy as np

import concourse.bass as bass
from concourse import mybir

D = 1024
NP = 1024
NS = 8
NT = NP + NS
P = 128
KC = D // P
DC = 512
CC = DC // P
W = 31
NB = NP // P
NBT = NB + 1
TG = NT // 3
NG = 3
LAST = NP - 2 * TG
H = 8
HD = 64
NCH = 2 * H
TOP = 16
NKEY = 128
EPS = 1e-6
ROWS = [16, 8, 5, 4, 3, 2, 2, 2] + [1] * 8
NC = sum(ROWS)
LOW = -3.0e38
NSLOT = H * TOP
RING = 4
PIECE = 2048
EBUF = 8


def build(nc, t):
    f32, u32 = mybir.dt.float32, mybir.dt.uint32
    ALU, ACT, AX = mybir.AluOpType, mybir.ActivationFunctionType, mybir.AxisListType
    ctx = ExitStack()
    with ctx:
        def sb(name, shape, dt=f32):
            return ctx.enter_context(nc.sbuf_tensor(name, shape, dt))

        def sem(name):
            return ctx.enter_context(nc.semaphore(name))

        def part(area, at, *shape):
            n = 1
            for k in shape:
                n *= k
            names = "abc"[:len(shape)]
            spec = "p (%s) -> p %s" % (" ".join(names), " ".join(names))
            return area[:, at:at + n].rearrange(spec, **dict(zip(names, shape)))

        arena = sb("arena", [P, 2 * NBT * D])
        x_tm = part(arena, 0, NBT, D)
        A_W = NP + W - 1
        aT = part(arena, 0, CC, A_W)
        yT = part(arena, CC * A_W, CC, NT)
        v_tm = part(arena, CC * (A_W + NT), NBT, DC)
        uT = part(arena, CC * (A_W + NT) + NBT * DC, CC, NT)
        rowv = part(arena, CC * (A_W + 2 * NT) + NBT * DC, 2, DC)
        x1 = part(arena, 0, NBT, D)
        n2 = part(arena, NBT * D, NBT, D)
        big = sb("big", [P, 2 * KC * NT + RING * PIECE])
        MT0, RING0 = KC * NT, 2 * KC * NT
        nT = part(big, 0, KC, NT)
        mT = part(big, MT0, KC, NT)
        xs_1 = part(big, MT0, 2, D)
        ring = part(big, RING0, RING, PIECE)
        cand = part(big, 0, NBT * H, NC)
        cid = part(big, NBT * H * NC, NBT * H, NC)
        qbuf = part(big, MT0, 2, NT)
        tmp4 = part(big, MT0 + 2 * NT, 2, 4, NKEY)
        v16 = part(big, MT0 + 2 * NT + 8 * NKEY, NBT, NCH, TOP)
        i16 = part(big, MT0 + 2 * NT + 8 * NKEY + NBT * NCH * TOP, NBT, NCH, TOP).bitcast(u32)
        i16f = part(big, MT0, NBT, NCH, TOP)
        crep = part(big, MT0 + NBT * NCH * TOP, H, NC)
        eq = part(big, RING0, H, TOP, NC)
        posf = part(big, RING0 + H * TOP * NC, NBT * H, TOP)
        pos = posf.bitcast(u32)
        rows = part(big, 0, EBUF, 2 * D)
        gfin = big[:, RING0:RING0 + D]
        w1 = sb("w1", [P, 9 * TG])
        sig, sq, prod, rbc = (part(w1, 2 * i * TG, k, TG) for i, k in ((0, 2), (1, 2), (2, 2), (3, 3)))
        conv_s = w1[:, 6 * TG:6 * TG + CC * NS * W].rearrange("p (c s k) -> p c s k", c=CC, s=NS)
        sgt = part(w1, 4 * TG, CC, P)
        xs = part(w1, 0, 2, D)
        gts = w1[0:NS, 2 * D:3 * D]
        w2 = sb("w2", [P, 2 * NBT * NSLOT + 4 * P])
        full_s = part(w2, 0, CC, NS * W).rearrange("p c (s k) -> p c s k", k=W)
        wsT = part(w2, CC * NS * W, H, P)
        bs = part(w2, CC * NS * W + H * P, CC, P)
        eid = part(w2, 0, NBT, NSLOT)
        gate = part(w2, NBT * NSLOT, NBT, NSLOT)
        diag = part(w2, 2 * NBT * NSLOT, 4, P)

        ident = sb("ident", [P, P])
        zero = sb("zero", [P, P])
        onesm = sb("onesm", [P, P])
        eye8 = sb("eye8", [P, NS, NS])
        iota = sb("iota", [P, NC])
        cT = sb("cT", [P, KC, 1 + NS])
        sigc = sb("sigc", [P, KC, 1 + NS])
        bada = sb("bada", [P, 48])
        gmix = sb("gmix", [P, KC])
        gffn = sb("gffn", [P, KC])
        mod = sb("mod", [P, 48, 1 + NS])
        scale1 = sb("scale1", [P, KC, 1 + NS])
        scale2 = sb("scale2", [P, KC, 1 + NS])
        wdw = sb("wdw", [P, CC, W])
        cvec = sb("cvec", [P, 3, CC])
        w00 = sb("w00", [P, CC])
        keys = sb("keys", [P, 2, NKEY])
        gt = sb("gt", [P, D])
        ms, root, rs, tm = (sb(n, [P, NBT]) for n in ("ms", "root", "rs", "tm"))
        ms2, root2, rs2, tm2 = (sb(n, [P, NBT]) for n in ("ms2", "root2", "rs2", "tm2"))
        bnst = sb("bnst", [P, 6])
        mv = sb("mv", [P, NBT, 2])
        vroot = sb("vroot", [P, NBT])
        eps = sb("eps", [P, 1])
        smx = sb("smx", [P, NBT * H])
        act = sb("act", [P, 4])
        gel = sb("gel", [P, 4])
        idx = sb("idx", [P, 16], u32)
        idxs = sb("idxs", [P, NS], u32)
        gsT = sb("gsT", [P, NS])
        wmask = sb("wmask", [P, NS, NS])
        sT = part(w1, 0, 2, 32)

        ps = ctx.enter_context(nc.psum_tensor("ps", [P, 8, 512], f32))

        def bank2(b):
            return ps[:, b:b + 2, :].rearrange("p b n -> p (b n)")

        names = """c_in small_in x_in x_again gfin_in consts masked sigmoid_c silu ada_mm
            sum_sq mean_sq1 root1 xs_ready xT_mm nT_done gate_mm lin_mm sig_a a_done v_mm v_stat v_root v_done
            u_mm u_done sg_mm sg_done conv mean_mm yc sq_act var_mm std_act yn_done sig_y y_done
            gb_mm ob_mm sig_b mb_done ga_mm oa_mm sig_g m_done gt_mm gt_done wo_mm x1_done sum_sq2 mean_sq2
            root_2 xs2 t2_mm n2T_done t2b_mm n2_done q_mm q_done s_mm s_done sel_done
            sm_diff sm_exp routes dve_chain pool_chain dots gelu weights experts_used acc_done x2_part x2_done
            xb_mm s_dots s_gelu s_weights s_acc eT_mm idx_ready idxs_ready sum_sq3 mean_sq3 root3
            y_ready out_y out_hist out_v ada_used""".split()
        S = {n: sem(n) for n in names}
        s_piece = [sem(f"piece{i}") for i in range(RING)]
        s_row = [sem(f"rows{i}") for i in range(EBUF)]

        def width(b):
            return P if b < NB else NS

        def cols(b):
            return slice(b * P, b * P + width(b))

        w_in, pieces = t["w_in"], []
        for i in range(24):
            pieces.append(("ada", t["w_ada"], i, "ada_used", i + 1))
        for half in range(2):
            pieces.append(("ag", w_in, 2 + half, "lin_mm", 2 * NG * (half + 1)))
            pieces.append(("al", w_in, half, "lin_mm", 2 * NG * (half + 1)))
        for half in range(2):
            pieces.append(("v", w_in, 6 + half, "v_mm", NBT))
        for half in range(2):
            pieces.append(("u", w_in, 4 + half, "u_mm", 2 * NG * (half + 1)))
        for base, wout, done in ((12, t["w_gmlp_out"], "ob_mm"), (8, t["w_conv_out"], "oa_mm")):
            for col in range(4):
                if col % 2 == 0:
                    pieces.append(("out", wout, col // 2, done, 2 * NG * (col + 2)))
                pieces.append(("gate", w_in, base + col, done, 2 * NG * (col + 1)))
        for i in range(4):
            pieces.append(("wo", t["w_out"], i, "wo_mm", NBT))
        for i in range(8):
            pieces.append(("wq", t["w_q"], i, "q_mm", 2 * NG * (i + 1)))

        def piece(n):
            k = CC if pieces[n][0] == "out" else KC
            return ring[:, n % RING, :].rearrange("p (k n) -> p k n", k=k)

        block = ctx.enter_context(nc.Block())

        @block.sync
        def _(sp):
            for name, dst in (("cT", cT), ("bada", bada), ("gmix", gmix), ("gffn", gffn)):
                sp.dma_start(dst[:], t[name]).then_inc(S["c_in"], 16)
            for b in range(NBT):
                w = width(b)
                sp.dma_start(x_tm[0:w, b, :], t["x"][b * P:b * P + w, :]).then_inc(S["x_in"], 16)

            def load(n):
                kind, src, col, done, count = pieces[n]
                if n >= RING:
                    done, count = pieces[n - RING][3:]
                    sp.wait_ge(S[done], count)
                w = 512 if kind == "out" else 256
                sp.dma_start(piece(n), src[:, col * w:(col + 1) * w].rearrange("(k p) n -> p k n", p=P)
                             ).then_inc(s_piece[n % RING], 16)

            for n in range(8):
                load(n)
            sp.dma_start(wdw[:], t["w_dw"]).then_inc(S["small_in"], 16)
            sp.dma_start(cvec[:], t["cvec"]).then_inc(S["small_in"], 16)
            sp.dma_start(keys[:], t["keys"]).then_inc(S["small_in"], 16)
            sp.dma_start(wsT, t["wsT"]).then_inc(S["small_in"], 16)
            for c in range(CC):
                sp.dma_start(full_s[:, c, :, 0:W - 1], t["state_T"][:, c, :, :]).then_inc(S["small_in"], 16)
            for h in range(H):
                at = slice(HD * (h % 2), HD * (h % 2) + HD)
                sp.dma_start(bs[at, h // 2, :], t["b_s"][h:h + 1, :].broadcast_to([HD, P])).then_inc(S["small_in"], 16)
                sp.dma_start(w00[at, h // 2:h // 2 + 1], t["w_s00"][h:h + 1, :].broadcast_to([HD, 1])
                             ).then_inc(S["small_in"], 16)
            for i, name in enumerate(("g_v", "b_v")):
                sp.dma_start(rowv[:, i, :], t[name].broadcast_to([P, DC])).then_inc(S["small_in"], 16)
            first_wo = [n for n, p in enumerate(pieces) if p[0] == "wo"][0]
            for n in range(8, len(pieces)):
                if n == first_wo - 4:
                    sp.wait_ge(S["a_done"], CC * NG)
                    sp.dma_start(t["out_hist_p"], aT[:, :, NP:NP + W - 1]).then_inc(S["out_hist"], 16)
                    for c in range(CC):
                        sp.dma_start(t["out_hist_s"][:, c, :, :], full_s[:, c, :, 1:W]).then_inc(S["out_hist"], 16)
                    sp.wait_ge(S["v_done"], NBT)
                    sp.dma_start(t["out_v"], v_tm[0:NS, NB, :]).then_inc(S["out_v"], 16)
                    sp.wait_ge(S["ob_mm"], KC * NG)
                    sp.wait_ge(S["out_v"], 16)
                    for b in range(NBT):
                        w = width(b)
                        sp.dma_start(n2[0:w, b, :], t["x"][b * P:b * P + w, :]).then_inc(S["x_again"], 16)
                load(n)
            sp.wait_ge(S["sel_done"], NBT)
            sp.dma_start(gfin, t["g_final"].broadcast_to([P, D])).then_inc(S["gfin_in"], 16)
            sp.wait_ge(S["out_hist"], 16 * (1 + CC))

        SMALL_IN = 16 * (4 + CC + 2 * H + 2)

        @block.tensor
        def _(pe):
            def arrived(n):
                pe.wait_ge(s_piece[n % RING], 16 * (n // RING + 1))

            def tiles(n, col, g, out, src=nT, k=KC):
                for c in range(k):
                    mm = nc.tensor.matmul(out, piece(n)[:, c, col:col + P], src[:, c, g * TG:(g + 1) * TG],
                                          start=(c == 0), stop=(c == k - 1))
                return mm

            pe.wait_ge(S["silu"], 1)
            for n in range(24):
                arrived(n)
                for j in range(2):
                    at = (2 * n + j) * (1 + NS)
                    for c in range(KC):
                        mm = nc.tensor.matmul(ps[:, 0, at:at + 1 + NS], piece(n)[:, c, j * P:(j + 1) * P],
                                              cT[:, c, :], start=(c == 0), stop=(c == KC - 1))
                mm.then_inc(S["ada_used"], 1)
            pe.wait_ge(S["consts"], 1)
            for b in range(NBT):
                w = width(b)
                pe.wait_ge(S["xs_ready"], b + 1)
                if b >= 2:
                    pe.wait_ge(S["nT_done"], b - 1)
                for c in range(KC):
                    at = bank2(2 + 2 * (b % 2))[:, c * P:c * P + w]
                    mm = nc.tensor.transpose(at, xs_1[0:w, b % 2, c * P:(c + 1) * P], ident[0:w, 0:w])
                mm.then_inc(S["xT_mm"], 1)
            n = 24
            pe.wait_ge(S["nT_done"], NBT)
            for half in range(2):
                arrived(n)
                arrived(n + 1)
                for j in range(2):
                    for g in range(NG):
                        i = (2 * half + j) * NG + g
                        if i >= 4:
                            pe.wait_ge(S["a_done"], i - 3)
                        tiles(n, j * P, g, ps[:, 2 * (i % 4), 0:TG]).then_inc(S["gate_mm"], 1)
                        tiles(n + 1, j * P, g, ps[:, 2 * (i % 4) + 1, 0:TG]).then_inc(S["lin_mm"], 1)
                n += 2
            arrived(n)
            arrived(n + 1)
            pe.wait_ge(S["a_done"], CC * NG)
            for b in range(NBT):
                w = width(b)
                if b >= 4:
                    pe.wait_ge(S["v_done"], b - 3)
                for half in range(2):
                    for c in range(KC):
                        mm = nc.tensor.matmul(ps[0:w, b % 4, half * 256:(half + 1) * 256], nT[:, c, cols(b)],
                                              piece(n + half)[:, c, :], start=(c == 0), stop=(c == KC - 1))
                mm.then_inc(S["v_mm"], 1)
            n += 2
            for half in range(2):
                arrived(n)
                for j in range(2):
                    for g in range(NG):
                        i = (2 * half + j) * NG + g
                        if i >= 4:
                            pe.wait_ge(S["u_done"], i - 3)
                        tiles(n, j * P, g, ps[:, 4 + i % 4, 0:TG]).then_inc(S["u_mm"], 1)
                n += 1
            pe.wait_ge(S["v_done"], NBT)
            pe.wait_ge(S["masked"], 1)
            for b in range(NB):
                if b >= 2:
                    pe.wait_ge(S["sg_done"], b - 1)
                for c in range(CC):
                    mm = nc.tensor.matmul(bank2(2 * (b % 2))[:, 256 * c:256 * (c + 1)], v_tm[:, b, c * P:(c + 1) * P],
                                          wsT[:, 2 * c:2 * c + 2, :].rearrange("p h i -> p (h i)"), start=True, stop=True)
                mm.then_inc(S["sg_mm"], 1)
            pe.wait_ge(S["sg_done"], NB)
            for c in range(CC):
                mm = nc.tensor.transpose(ps[:, 0, c * NS:(c + 1) * NS], v_tm[0:NS, NB, c * P:(c + 1) * P],
                                         ident[0:NS, 0:NS])
            mm.then_inc(S["sg_mm"], 1)
            pe.wait_ge(S["sg_done"], NB + 1)
            pe.wait_ge(S["u_done"], CC * NG)

            def branch(n, src, gate_sem, out_sem, done):
                for col in range(4):
                    if col % 2 == 0:
                        no = n
                        arrived(no)
                        n += 1
                    arrived(n)
                    for j in range(2):
                        for g in range(NG):
                            i = (2 * col + j) * NG + g
                            if i >= 4:
                                pe.wait_ge(S[done], i - 3)
                            tiles(n, j * P, g, ps[:, 2 * (i % 4), 0:TG]).then_inc(S[gate_sem], 1)
                            tiles(no, (col % 2) * 256 + j * P, g, ps[:, 2 * (i % 4) + 1, 0:TG], src, CC
                                  ).then_inc(S[out_sem], 1)
                    n += 1
                return n

            n = branch(n, uT, "gb_mm", "ob_mm", "mb_done")
            pe.wait_ge(S["conv"], CC * W + 1)
            pe.wait_ge(S["mb_done"], KC * NG)
            for g in range(NG):
                for c in range(CC):
                    mm = nc.tensor.matmul(ps[:, g, 0:TG], onesm[:], yT[:, c, g * TG:(g + 1) * TG],
                                          start=(c == 0), stop=(c == CC - 1))
                mm.then_inc(S["mean_mm"], 1)
            for g in range(NG):
                for c in range(CC):
                    i = g * CC + c
                    pe.wait_ge(S["sq_act"], i + 1)
                    nc.tensor.matmul(ps[:, 3 + g, 0:TG], onesm[:], sq[:, i % 2, :],
                                     start=(c == 0), stop=(c == CC - 1)).then_inc(S["var_mm"], 1)
            pe.wait_ge(S["y_done"], CC * NG)
            n = branch(n, yT, "ga_mm", "oa_mm", "m_done")
            pe.wait_ge(S["m_done"], KC * NG)

            def spread(k):
                for c in range(KC):
                    nc.tensor.matmul(bank2(4)[:, c * P:(c + 1) * P], mod[:, k * KC + c, 0:1].broadcast_to([P, P]),
                                     ident[:], start=True, stop=True)
                    mm = nc.tensor.transpose(bank2(6)[0:NS, c * P:(c + 1) * P], mod[:, k * KC + c, 1:1 + NS], ident[:])
                mm.then_inc(S["gt_mm"], 1)

            spread(2)
            for i in range(4):
                arrived(n + i)

            def project(b):
                w = width(b)
                if b >= 2:
                    pe.wait_ge(S["x1_done"], b - 1)
                for i in range(4):
                    for c in range(KC):
                        mm = nc.tensor.matmul(bank2(2 * (b % 2))[0:w, i * 256:(i + 1) * 256], mT[:, c, cols(b)],
                                              piece(n + i)[:, c, :], start=(c == 0), stop=(c == KC - 1))
                mm.then_inc(S["wo_mm"], 1)

            def turn(b):
                w = width(b)
                pe.wait_ge(S["xs2"], b + 1)
                if b == 0:
                    pe.wait_ge(S["gt_done"], 2)
                else:
                    pe.wait_ge(S["n2T_done"], b)
                for c in range(KC):
                    mm = nc.tensor.transpose(bank2(4)[:, c * P:c * P + w], xs[0:w, b % 2, c * P:(c + 1) * P],
                                             ident[0:w, 0:w])
                mm.then_inc(S["t2_mm"], 1)
                pe.wait_ge(S["n2T_done"], b + 1)
                if b >= 1:
                    pe.wait_ge(S["n2_done"], b)
                for c in range(KC):
                    mm = nc.tensor.transpose(bank2(6)[0:w, c * P:(c + 1) * P], nT[:, c, cols(b)], ident[:])
                mm.then_inc(S["t2b_mm"], 1)

            for b in range(NBT):
                project(b)
                if b >= 1:
                    turn(b - 1)
            turn(NBT - 1)
            n += 4
            pe.wait_ge(S["n2_done"], NBT)
            pe.wait_ge(S["x1_done"], NBT)
            spread(5)
            pe.wait_ge(S["gt_done"], 4)

            def query(ch):
                if ch % 2 == 0:
                    arrived(n + ch // 2)
                for g in range(NG):
                    if ch >= 2:
                        pe.wait_ge(S["q_done"], (ch - 2) * NG + g + 1)
                    tiles(n + ch // 2, (ch % 2) * P, g, ps[:, 3 * (ch % 2) + g, 0:TG]).then_inc(S["q_mm"], 1)

            def score(ch):
                pe.wait_ge(S["q_done"], (ch + 1) * NG)
                for third in range(3):
                    i = ch * 3 + third
                    if i >= 2:
                        pe.wait_ge(S["s_done"], i - 1)
                    for b in range(4 * third, min(4 * third + 4, NBT)):
                        w = width(b)
                        mm = nc.tensor.matmul(ps[0:w, 6 + i % 2, (b % 4) * P:(b % 4 + 1) * P],
                                              qbuf[:, ch % 2, cols(b)], keys[:, ch % 2, :], start=True, stop=True)
                    mm.then_inc(S["s_mm"], 1)

            for ch in range(NCH):
                query(ch)
                if ch >= 1:
                    score(ch - 1)
            score(NCH - 1)

            pe.wait_ge(S["s_done"], NCH * 3)
            pe.sem_inc(S["experts_used"], 4)

            def values(bank, q, group):
                pe.wait_ge(S["weights"], group + 1)
                for s in range(2):
                    for half in range(2):
                        mm = nc.tensor.matmul(ps[:, bank + half, :], diag[:, (2 * q + s) % 4, :],
                                              rows[:, (2 * q + s) % EBUF, D + 512 * half:D + 512 * (half + 1)],
                                              start=False, stop=False)
                mm.then_inc(S["experts_used"], 1)

            with pe.Fori(0, NB // 2) as pair:
                for par in range(2):
                    bank = 2 * par
                    pe.wait_ge(S["x2_done"], pair * 2 + par + 1)
                    for half in range(2):
                        nc.tensor.matmul(ps[:, bank + half, :], zero[:], zero[:, 0:1].broadcast_to([P, 512]),
                                         start=True, stop=False)
                    with pe.Fori(0, 8) as m:
                        for q in range(8):
                            values(bank, q, (pair * 2 + par) * 64 + m * 8 + q)
                    for half in range(2):
                        mm = nc.tensor.matmul(ps[:, bank + half, :], zero[:], zero[:, 0:1].broadcast_to([P, 512]),
                                              start=False, stop=True)
                    mm.then_inc(S["acc_done"], 1)
            for s in range(NS):
                if s >= 1:
                    pe.wait_ge(S["s_dots"], s)
                for half in range(2):
                    mm = nc.tensor.matmul(ps[:, 6 + half, :], ident[0:NS, s:s + 1].broadcast_to([NS, P]),
                                          n2[0:NS, NB, 512 * half:512 * (half + 1)], start=True, stop=True)
                mm.then_inc(S["xb_mm"], 1)
                pe.wait_ge(S["s_weights"], s + 1)
                if s == 0:
                    pe.wait_ge(S["x2_done"], 2 + NB - 1)
                for half in range(2):
                    mm = nc.tensor.matmul(ps[0:NS, half, :], wmask[:, s, :],
                                          rows[:, s, D + 512 * half:D + 512 * (half + 1)],
                                          start=(s == 0), stop=(s == NS - 1))
            mm.then_inc(S["s_acc"], 1)

        @block.scalar
        def _(act_):
            ac = nc.scalar
            act_.wait_ge(S["c_in"], 64)
            ac.activation(sigc[:], cT[:], ACT.Sigmoid).then_inc(S["sigmoid_c"], 1)
            act_.wait_ge(S["consts"], 1)
            act_.wait_ge(S["x_in"], 16 * NBT)
            for b in range(NBT):
                w = width(b)
                ac.activation(big[0:w, b * D:(b + 1) * D], x_tm[0:w, b, :], ACT.Square,
                              accum_out=ms[0:w, b:b + 1]).then_inc(S["sum_sq"], 1)
            act_.wait_ge(S["mean_sq1"], 1)
            ac.activation(root[:], ms[:], ACT.Sqrt).then_inc(S["root1"], 1)
            for i in range(CC * NG):
                act_.wait_ge(S["gate_mm"], i + 1)
                if i >= 2:
                    act_.wait_ge(S["a_done"], i - 1)
                ac.activation(sig[:, i % 2, :], ps[:, 2 * (i % 4), 0:TG], ACT.Sigmoid).then_inc(S["sig_a"], 1)
            for b in range(NBT):
                w = width(b)
                act_.wait_ge(S["v_stat"], b + 1)
                ac.activation(vroot[0:w, b:b + 1], mv[0:w, b, 1:2], ACT.Sqrt, bias=eps[0:w, :]).then_inc(S["v_root"], 1)
            for i in range(CC * NG):
                c, g = i // NG, i % NG
                act_.wait_ge(S["u_mm"], i + 1)
                ac.activation(uT[:, c, g * TG:(g + 1) * TG], ps[:, 4 + i % 4, 0:TG], ACT.Copy).then_inc(S["u_done"], 1)
            for i in range(KC * NG):
                act_.wait_ge(S["gb_mm"], i + 1)
                if i >= 2:
                    act_.wait_ge(S["mb_done"], i - 1)
                ac.activation(sig[:, i % 2, :], ps[:, 2 * (i % 4), 0:TG], ACT.Sigmoid).then_inc(S["sig_b"], 1)
            for i in range(CC * NG):
                g, c = i // CC, i % CC
                act_.wait_ge(S["yc"], i + 1)
                if i >= 2:
                    act_.wait_ge(S["var_mm"], i - 1)
                ac.activation(sq[:, i % 2, :], yT[:, c, g * TG:(g + 1) * TG], ACT.Square).then_inc(S["sq_act"], 1)
            act_.wait_ge(S["var_mm"], CC * NG)
            for g in range(NG):
                ac.activation(rbc[:, g, :], ps[:, 3 + g, 0:TG], ACT.Sqrt, bias=eps[:]).then_inc(S["std_act"], 1)
            for i in range(CC * NG):
                g, c = i // CC, i % CC
                act_.wait_ge(S["yn_done"], i + 1)
                if i >= 2:
                    act_.wait_ge(S["y_done"], i - 1)
                elif i == 0:
                    act_.wait_ge(S["mb_done"], KC * NG)
                ac.activation(sig[:, i % 2, :], yT[:, c, g * TG:(g + 1) * TG], ACT.Sigmoid, scale=cvec[:, 1, c:c + 1],
                              bias=cvec[:, 2, c:c + 1]).then_inc(S["sig_y"], 1)
            for i in range(KC * NG):
                act_.wait_ge(S["ga_mm"], i + 1)
                if i >= 2:
                    act_.wait_ge(S["m_done"], i - 1)
                elif i == 0:
                    act_.wait_ge(S["y_done"], CC * NG)
                ac.activation(sig[:, i % 2, :], ps[:, 2 * (i % 4), 0:TG], ACT.Sigmoid).then_inc(S["sig_g"], 1)

            def spread():
                ac.activation(gt[:], bank2(4), ACT.Copy).then_inc(S["gt_done"], 1)
                ac.activation(gts, bank2(6)[0:NS, :], ACT.Copy).then_inc(S["gt_done"], 1)

            def n2_back(b):
                w = width(b)
                act_.wait_ge(S["t2b_mm"], b + 1)
                ac.activation(n2[0:w, b, :], bank2(6)[0:w, :], ACT.Copy).then_inc(S["n2_done"], 1)

            act_.wait_ge(S["gt_mm"], 1)
            act_.wait_ge(S["m_done"], KC * NG)
            spread()
            for b in range(NBT):
                w = width(b)
                act_.wait_ge(S["x1_done"], b + 1)
                if b >= 2:
                    act_.wait_ge(S["t2_mm"], b - 1)
                ac.activation(xs[0:w, b % 2, :], x1[0:w, b, :], ACT.Square, accum_out=ms2[0:w, b:b + 1]
                              ).then_inc(S["sum_sq2"], 1)
                act_.wait_ge(S["mean_sq2"], b + 1)
                ac.activation(root2[0:w, b:b + 1], ms2[0:w, b:b + 1], ACT.Sqrt).then_inc(S["root_2"], 1)
                if b >= 1:
                    n2_back(b - 1)
            n2_back(NBT - 1)
            act_.wait_ge(S["gt_mm"], 2)
            act_.wait_ge(S["x1_done"], NBT)
            spread()
            for i in range(NCH * NG):
                ch, g = i // NG, i % NG
                act_.wait_ge(S["q_mm"], i + 1)
                if ch == 0:
                    act_.wait_ge(S["wo_mm"], NBT)
                if ch >= 2:
                    act_.wait_ge(S["s_mm"], (ch - 1) * 3)
                ac.activation(qbuf[:, ch % 2, g * TG:(g + 1) * TG], ps[:, 3 * (ch % 2) + g, 0:TG], ACT.Copy
                              ).then_inc(S["q_done"], 1)
            act_.wait_ge(S["sm_diff"], 1)
            ac.activation(gate, gate, ACT.Exp).then_inc(S["sm_exp"], 1)
            with act_.Fori(0, NB) as b:
                with act_.Fori(0, 32) as m:
                    for q in range(2):
                        act_.wait_ge(S["dots"], b * 64 + m * 2 + q + 1)
                        ac.activation(gel[:, 2 * q:2 * q + 2], act[:, 2 * q:2 * q + 2], ACT.Gelu).then_inc(S["gelu"], 1)
            for s in range(NS):
                act_.wait_ge(S["s_dots"], s + 1)
                ac.activation(gel[:, s % 4:s % 4 + 1], act[:, s % 4:s % 4 + 1], ACT.Gelu).then_inc(S["s_gelu"], 1)
            act_.wait_ge(S["x2_done"], 2 + NBT)
            for b in range(NBT):
                w = width(b)
                ac.activation(big[0:w, b * D:(b + 1) * D], x1[0:w, b, :], ACT.Square, accum_out=ms[0:w, b:b + 1]
                              ).then_inc(S["sum_sq3"], 1)
            act_.wait_ge(S["mean_sq3"], 1)
            ac.activation(root[:], ms[:], ACT.Sqrt).then_inc(S["root3"], 1)
            for b in range(NBT):
                w = width(b)
                act_.wait_ge(S["y_ready"], b + 1)
                act_.dma_start(t["out_y"][b * P:b * P + w, :], x1[0:w, b, :]).then_inc(S["out_y"], 16)
            act_.wait_ge(S["out_y"], 16 * NBT)

        @block.gpsimd
        def _(pool):
            gp = nc.gpsimd
            k = [0]

            def link(ins):
                k[0] += 1
                ins.then_inc(S["pool_chain"], 1)
                pool.wait_ge(S["pool_chain"], k[0])

            gp.memset(ident[:], 0.0)
            gp.memset(zero[:], 0.0)
            gp.memset(onesm[:], 1.0 / DC)
            gp.memset(ms[:], 1.0)
            gp.memset(eps[:], EPS)
            gp.iota(iota[:], [[1, NC]], base=0, channel_multiplier=0, allow_small_or_imprecise_dtypes=True)
            link(gp.memset(eye8[:], 0.0))
            gp.affine_select(out=eye8[:], in_=eye8[:], compare_op=ALU.not_equal, fill=1.0, base=0,
                             pattern=[[1, NS], [-1, NS]], channel_multiplier=0)
            gp.affine_select(out=ident[:], in_=ident[:], compare_op=ALU.not_equal, fill=1.0, base=0,
                             pattern=[[-1, P]], channel_multiplier=1).then_inc(S["consts"], 1)
            pool.wait_ge(S["small_in"], SMALL_IN)
            gp.affine_select(out=wsT, in_=wsT, compare_op=ALU.is_ge, fill=0.0, base=0,
                             pattern=[[0, H], [1, P]], channel_multiplier=-1).then_inc(S["masked"], 1)
            pool.wait_ge(S["routes"], 1)
            slots = eid.rearrange("p b n -> p (b n)")
            gp.tensor_copy(idx[:, 0:2], slots[:, 0:2]).then_inc(S["idx_ready"], 1)
            with pool.Fori(0, NB * NSLOT // 16) as m:
                for q in range(8):
                    group = m * 8 + q
                    pool.wait_ge(S["idx_ready"], group + 1)
                    pool.wait_ge(S["experts_used"], group + 1)
                    nxt = 2 * ((q + 1) % 8)
                    gp.tensor_copy(idx[:, nxt:nxt + 2], slots[:, bass.ds(group * 2 + 2, 2)]
                                   ).then_inc(S["idx_ready"], 1)
                    for s in range(2):
                        r = (2 * q + s) % EBUF
                        gp.indirect_dma_start(
                            rows[:, r, :], None, t["experts"],
                            bass.IndirectOffsetOnAxis(ap=idx[:, 2 * q + s:2 * q + s + 1], axis=0)
                        ).then_inc(s_row[r], 16)
            pool.wait_ge(S["idxs_ready"], 1)
            pool.wait_ge(S["experts_used"], 64 * NB + 4)
            for s in range(NS):
                gp.indirect_dma_start(rows[:, s, :], None, t["experts"],
                                      bass.IndirectOffsetOnAxis(ap=idxs[:, s:s + 1], axis=0)).then_inc(s_row[s], 16)

        @block.vector
        def _(dve):
            v = nc.vector
            k = [0]

            def link(ins):
                k[0] += 1
                ins.then_inc(S["dve_chain"], 1)
                dve.wait_ge(S["dve_chain"], k[0])

            def rsqrt(sq_, root_, out, tmp):
                link(v.reciprocal(out, root_))
                link(v.tensor_tensor(tmp, out, out, ALU.mult))
                link(v.tensor_tensor(tmp, tmp, sq_, ALU.mult))
                link(v.tensor_scalar(tmp, tmp, -0.5, 1.5, ALU.mult, ALU.add))
                link(v.tensor_tensor(out, out, tmp, ALU.mult))

            dve.wait_ge(S["sigmoid_c"], 1)
            v.tensor_tensor(cT[:], cT[:], sigc[:], ALU.mult).then_inc(S["silu"], 1)
            dve.wait_ge(S["sum_sq"], NBT)
            v.tensor_scalar(ms[:], ms[:], 1.0 / D, EPS, ALU.mult, ALU.add).then_inc(S["mean_sq1"], 1)
            dve.wait_ge(S["root1"], 1)
            rsqrt(ms[:], root[:], rs[:], tm[:])

            def scaled(b):
                w = width(b)
                if b >= 2:
                    dve.wait_ge(S["xT_mm"], b - 1)
                v.tensor_scalar(xs_1[0:w, b % 2, :], x_tm[0:w, b, :], rs[0:w, b:b + 1], None, ALU.mult
                                ).then_inc(S["xs_ready"], 1)

            def modulate(b, bank, scale, shift, done):
                if b < NB:
                    for c in range(KC):
                        last = v.tensor_scalar(nT[:, c, cols(b)], bank2(bank)[:, c * P:(c + 1) * P],
                                               scale[:, c, 0:1], mod[:, shift * KC + c, 0:1], ALU.mult, ALU.add)
                else:
                    src = bank2(bank).rearrange("p (c t) -> p c t", c=KC)[:, :, 0:NS]
                    link(v.tensor_tensor(nT[:, :, cols(b)], src, scale[:, :, 1:1 + NS], ALU.mult))
                    last = v.tensor_tensor(nT[:, :, cols(b)], nT[:, :, cols(b)],
                                           mod[:, shift * KC:(shift + 1) * KC, 1:1 + NS], ALU.add)
                last.then_inc(S[done], 1)

            scaled(0)
            scaled(1)
            dve.wait_ge(S["ada_used"], 24)
            link(v.tensor_tensor(mod[:], ps[:, 0, 0:48 * (1 + NS)].rearrange("p (k n) -> p k n", k=48),
                                 bada[:].unsqueeze(2).broadcast_to([P, 48, 1 + NS]), ALU.add))
            for sc, g, kk in ((scale1, gmix, 1), (scale2, gffn, 4)):
                last = v.scalar_tensor_tensor(out=sc[:], in0=mod[:, kk * KC:(kk + 1) * KC, :], scalar=1.0,
                                              in1=g[:].unsqueeze(2).broadcast_to([P, KC, 1 + NS]),
                                              op0=ALU.add, op1=ALU.mult)
            link(last)
            for b in range(NBT):
                dve.wait_ge(S["xT_mm"], b + 1)
                modulate(b, 2 + 2 * (b % 2), scale1, 0, "nT_done")
                if b + 2 < NBT:
                    scaled(b + 2)
            dve.wait_ge(S["small_in"], SMALL_IN)
            v.memset(aT[:, :, 0:W - 1], 0.0)
            for i in range(CC * NG):
                c, g = i // NG, i % NG
                dve.wait_ge(S["sig_a"], i + 1)
                dve.wait_ge(S["lin_mm"], i + 1)
                lin = ps[:, 2 * (i % 4) + 1, :]
                w = TG if g < NG - 1 else LAST
                last = v.tensor_tensor(aT[:, c, W - 1 + g * TG:W - 1 + g * TG + w], lin[:, 0:w], sig[:, i % 2, 0:w], ALU.mult)
                if g == NG - 1:
                    last = v.tensor_tensor(full_s[:, c, :, W - 1:W], lin[:, LAST:TG].unsqueeze(2),
                                           sig[:, i % 2, LAST:TG].unsqueeze(2), ALU.mult)
                last.then_inc(S["a_done"], 1)
            dve.wait_ge(S["a_done"], CC * NG)
            link(v.tensor_tensor(conv_s, full_s, wdw[:].unsqueeze(2).broadcast_to([P, CC, NS, W]), ALU.mult))
            link(v.tensor_reduce(yT[:, :, NP:NT], conv_s, AX.X, ALU.add))
            v.tensor_tensor(yT[:, :, NP:NT], yT[:, :, NP:NT], cvec[:, 0, :].unsqueeze(2).broadcast_to([P, CC, NS]),
                            ALU.add).then_inc(S["conv"], 1)

            taps = [0]

            def conv(count):
                for n in range(taps[0], min(taps[0] + count, CC * W)):
                    kk, c = n // CC, n % CC
                    y = yT[:, c, 0:NP]
                    if kk == 0:
                        ins = v.tensor_scalar(y, aT[:, c, 0:NP], wdw[:, c, 0:1], cvec[:, 0, c:c + 1], ALU.mult, ALU.add)
                    else:
                        dve.wait_ge(S["conv"], 1 + n - CC + 1)
                        ins = v.scalar_tensor_tensor(out=y, in0=aT[:, c, kk:kk + NP], scalar=wdw[:, c, kk:kk + 1],
                                                     in1=y, op0=ALU.mult, op1=ALU.add)
                    ins.then_inc(S["conv"], 1)
                    taps[0] += 1

            def v_stats(b):
                w = width(b)
                dve.wait_ge(S["v_mm"], b + 1)
                link(v.bn_stats(bnst[0:w, :], ps[0:w, b % 4, :]))
                v.bn_aggr(mv[0:w, b, :], bnst[0:w, :]).then_inc(S["v_stat"], 1)

            def v_norm(b):
                w = width(b)
                dve.wait_ge(S["v_root"], b + 1)
                link(v.reciprocal(vroot[0:w, b:b + 1], vroot[0:w, b:b + 1]))
                link(v.scalar_tensor_tensor(out=v_tm[0:w, b, :], in0=ps[0:w, b % 4, :], scalar=mv[0:w, b, 0:1],
                                            in1=rowv[0:w, 0, :], op0=ALU.subtract, op1=ALU.mult))
                v.scalar_tensor_tensor(out=v_tm[0:w, b, :], in0=v_tm[0:w, b, :], scalar=vroot[0:w, b:b + 1],
                                       in1=rowv[0:w, 1, :], op0=ALU.mult, op1=ALU.add).then_inc(S["v_done"], 1)

            for b in range(NBT):
                v_stats(b)
                conv(3)
                v_norm(b)
            for b in range(NB):
                dve.wait_ge(S["sg_mm"], b + 1)
                dve.wait_ge(S["u_done"], CC * NG) if b == 0 else dve.wait_ge(S["sg_done"], b)
                sg = bank2(2 * (b % 2)).rearrange("p (c n) -> p c n", c=CC)
                for hh in range(2):
                    at = slice(HD * hh, HD * hh + HD)
                    last = v.tensor_tensor(sgt[at, :, :], sg[at, :, P * hh:P * hh + P], bs[at, :, :], ALU.add)
                link(last)
                v.tensor_tensor(uT[:, :, cols(b)], uT[:, :, cols(b)], sgt, ALU.mult).then_inc(S["sg_done"], 1)
            dve.wait_ge(S["sg_mm"], NB + 1)
            dve.wait_ge(S["sg_done"], NB)
            vs = ps[:, 0, 0:CC * NS].rearrange("p (c s) -> p c s", c=CC)
            link(v.tensor_tensor(sgt[:, :, 0:NS], vs, w00[:].unsqueeze(2).broadcast_to([P, CC, NS]), ALU.mult))
            link(v.tensor_tensor(sgt[:, :, 0:NS], sgt[:, :, 0:NS], bs[:, :, 0:1].broadcast_to([P, CC, NS]), ALU.add))
            v.tensor_tensor(uT[:, :, NP:NT], uT[:, :, NP:NT], sgt[:, :, 0:NS], ALU.mult).then_inc(S["sg_done"], 1)
            for i in range(KC * NG):
                j, g = i // NG, i % NG
                dve.wait_ge(S["sig_b"], i + 1)
                dve.wait_ge(S["ob_mm"], i + 1)
                v.tensor_tensor(mT[:, j, g * TG:(g + 1) * TG], ps[:, 2 * (i % 4) + 1, 0:TG], sig[:, i % 2, :], ALU.mult
                                ).then_inc(S["mb_done"], 1)
                conv(4)
            conv(CC * W)
            for i in range(CC * NG):
                g, c = i // CC, i % CC
                dve.wait_ge(S["mean_mm"], g + 1)
                y = yT[:, c, g * TG:(g + 1) * TG]
                v.tensor_tensor(y, y, ps[:, g, 0:TG], ALU.subtract).then_inc(S["yc"], 1)

            def swish(i):
                g, c = i // CC, i % CC
                y = yT[:, c, g * TG:(g + 1) * TG]
                dve.wait_ge(S["sig_y"], i + 1)
                if i >= 2:
                    dve.wait_ge(S["y_done"], i - 1)
                link(v.tensor_scalar(prod[:, i % 2, :], y, cvec[:, 1, c:c + 1], cvec[:, 2, c:c + 1], ALU.mult, ALU.add))
                v.tensor_tensor(y, prod[:, i % 2, :], sig[:, i % 2, :], ALU.mult).then_inc(S["y_done"], 1)

            for i in range(CC * NG):
                g, c = i // CC, i % CC
                if c == 0:
                    dve.wait_ge(S["std_act"], g + 1)
                    link(v.reciprocal(rbc[:, g, :], rbc[:, g, :]))
                y = yT[:, c, g * TG:(g + 1) * TG]
                if i == 0:
                    dve.wait_ge(S["sq_act"], CC * NG)
                v.tensor_tensor(y, y, rbc[:, g, :], ALU.mult).then_inc(S["yn_done"], 1)
                if i >= 1:
                    swish(i - 1)
            swish(CC * NG - 1)

            def add_m(i):
                j, g = i // NG, i % NG
                m = mT[:, j, g * TG:(g + 1) * TG]
                dve.wait_ge(S["dve_chain"], chain_at[i])
                v.tensor_tensor(m, m, prod[:, i % 2, :], ALU.add).then_inc(S["m_done"], 1)

            chain_at = []
            for i in range(KC * NG):
                dve.wait_ge(S["sig_g"], i + 1)
                dve.wait_ge(S["oa_mm"], i + 1)
                if i >= 2:
                    dve.wait_ge(S["m_done"], i - 1)
                k[0] += 1
                chain_at.append(k[0])
                v.tensor_tensor(prod[:, i % 2, :], ps[:, 2 * (i % 4) + 1, 0:TG], sig[:, i % 2, :], ALU.mult
                                ).then_inc(S["dve_chain"], 1)
                if i >= 1:
                    add_m(i - 1)
            add_m(KC * NG - 1)

            def residual(b):
                w = width(b)
                dve.wait_ge(S["wo_mm"], b + 1)
                g = gt[:] if b < NB else gts
                link(v.tensor_tensor(x1[0:w, b, :], bank2(2 * (b % 2))[0:w, :], g, ALU.mult))
                v.tensor_tensor(x1[0:w, b, :], x1[0:w, b, :], n2[0:w, b, :], ALU.add).then_inc(S["x1_done"], 1)

            def norm2(b):
                w = width(b)
                dve.wait_ge(S["sum_sq2"], b + 1)
                v.tensor_scalar(ms2[0:w, b:b + 1], ms2[0:w, b:b + 1], 1.0 / D, EPS, ALU.mult, ALU.add
                                ).then_inc(S["mean_sq2"], 1)
                dve.wait_ge(S["root_2"], b + 1)
                rsqrt(ms2[0:w, b:b + 1], root2[0:w, b:b + 1], rs2[0:w, b:b + 1], tm2[0:w, b:b + 1])
                v.tensor_scalar(xs[0:w, b % 2, :], x1[0:w, b, :], rs2[0:w, b:b + 1], None, ALU.mult
                                ).then_inc(S["xs2"], 1)

            dve.wait_ge(S["gt_done"], 2)
            dve.wait_ge(S["x_again"], 16 * NBT)
            dve.wait_ge(S["out_hist"], 16 * (1 + CC))
            for b in range(NBT):
                residual(b)
                norm2(b)
                dve.wait_ge(S["t2_mm"], b + 1)
                modulate(b, 4, scale2, 3, "n2T_done")

            dve.wait_ge(S["wo_mm"], NBT)
            v.memset(v16[:, NB, :, :], 0.0)
            link(v.memset(i16[:, NB, :, :], 0))
            for ch in range(NCH):
                for third in range(3):
                    i = ch * 3 + third
                    dve.wait_ge(S["s_mm"], i + 1)
                    bl = range(4 * third, min(4 * third + 4, NBT))

                    def sc(b):
                        return ps[0:width(b), 6 + i % 2, (b % 4) * P:(b % 4 + 1) * P]

                    def rep(b):
                        return tmp4[0:width(b), i % 2, b % 4, :]

                    def top(x, b, half):
                        return x[0:width(b), b, ch, 8 * half:8 * half + 8]

                    for b in bl:
                        last = v.max(top(v16, b, 0), sc(b))
                    link(last)
                    for b in bl:
                        last = v.match_replace(rep(b), top(v16, b, 0), sc(b), LOW)
                    link(last)
                    for b in bl:
                        v.max_index(top(i16, b, 0), top(v16, b, 0), sc(b))
                        last = v.max(top(v16, b, 1), rep(b))
                    link(last)
                    for b in bl:
                        last = v.max_index(top(i16, b, 1), top(v16, b, 1), rep(b))
                    last.then_inc(S["s_done"], 1)
            dve.wait_ge(S["s_done"], NCH * 3)
            dve.wait_ge(S["s_mm"], NCH * 3)
            link(v.tensor_copy(i16f, i16))
            vv = v16.rearrange("p b (h f) k -> p (b h) f k", f=2)
            ii = i16f.rearrange("p b (h f) k -> p (b h) f k", f=2)
            at = 0
            for a in range(9):
                if a < 8:
                    n_ = ROWS[a]
                    first, second = (lambda x: x[:, :, 0, a:a + 1].broadcast_to([P, NBT * H, n_])), (lambda x: x[:, :, 1, 0:n_])
                else:
                    n_ = 8
                    first, second = (lambda x: x[:, :, 0, 8:16]), (lambda x: x[:, :, 1, 0:1].broadcast_to([P, NBT * H, n_]))
                v.tensor_tensor(cand[:, :, at:at + n_], first(vv), second(vv), ALU.add)
                last = v.scalar_tensor_tensor(out=cid[:, :, at:at + n_], in0=first(ii), scalar=float(NKEY),
                                              in1=second(ii), op0=ALU.mult, op1=ALU.add)
                at += n_
            link(last)
            dve.wait_ge(S["out_hist"], 16 * (1 + CC))

            def choose(b):
                for h in range(H):
                    last = v.max(gate[:, b, TOP * h:TOP * h + 8], cand[:, b * H + h, :])
                link(last)
                for h in range(H):
                    last = v.match_replace(crep[:, h, :], gate[:, b, TOP * h:TOP * h + 8], cand[:, b * H + h, :], LOW)
                link(last)
                for h in range(H):
                    v.max_index(pos[:, b * H + h, 0:8], gate[:, b, TOP * h:TOP * h + 8], cand[:, b * H + h, :])
                    last = v.max(gate[:, b, TOP * h + 8:TOP * h + 16], crep[:, h, :])
                link(last)
                for h in range(H):
                    last = v.max_index(pos[:, b * H + h, 8:16], gate[:, b, TOP * h + 8:TOP * h + 16], crep[:, h, :])
                link(last)
                link(v.tensor_copy(posf[:, b * H:(b + 1) * H, :], pos[:, b * H:(b + 1) * H, :]))

            def select(b):
                link(v.tensor_tensor(eq.rearrange("p h k n -> p (h k) n"),
                                     posf[:, b * H:(b + 1) * H, :].rearrange("p h k -> p (h k)").unsqueeze(2)
                                     .broadcast_to([P, H * TOP, NC]),
                                     iota[:].unsqueeze(1).broadcast_to([P, H * TOP, NC]), ALU.is_equal))
                link(v.tensor_tensor(eq, eq, cid[:, b * H:(b + 1) * H, :].unsqueeze(2).broadcast_to([P, H, TOP, NC]),
                                     ALU.mult))
                v.tensor_reduce(eid[:, b, :].rearrange("p (h k) -> p h k", h=H), eq, AX.X, ALU.add
                                ).then_inc(S["sel_done"], 1)

            for b in range(NBT):
                choose(b)
                select(b)
            gg = gate.rearrange("p b (h k) -> p (b h) k", k=TOP)
            link(v.tensor_copy(smx[:], gg[:, :, 0]))
            v.tensor_tensor(gg, gg, smx[:].unsqueeze(2).broadcast_to([P, NBT * H, TOP]), ALU.subtract
                            ).then_inc(S["sm_diff"], 1)
            dve.wait_ge(S["sm_exp"], 1)
            link(v.tensor_reduce(smx[:], gg, AX.X, ALU.add))
            link(v.reciprocal(smx[:], smx[:]))
            link(v.tensor_tensor(gg, gg, smx[:].unsqueeze(2).broadcast_to([P, NBT * H, TOP]), ALU.mult))
            dve.wait_ge(S["sel_done"], NBT)
            for r in range(4):
                at = slice(32 * r, 32 * r + 32)
                v.transpose(sT[at, 0, :], eid[0:32, NB, at])
                last = v.transpose(sT[at, 1, :], gate[0:32, NB, at])
            link(last)
            v.tensor_copy(idxs[:], sT[:, 0, 0:NS]).then_inc(S["idxs_ready"], 1)
            v.tensor_copy(gsT[:], sT[:, 1, 0:NS]).then_inc(S["routes"], 1)
            dve.sem_inc(S["x2_done"], 2)

            def dots(q, b, group):
                for s in range(2):
                    r = (2 * q + s) % EBUF
                    dve.wait_ge(s_row[r], 16 * (group[0] + q // 4) + 16)
                    last = v.scalar_tensor_tensor(out=rows[:, r, 0:D], in0=rows[:, r, 0:D], scalar=1.0, in1=n2[:, b, :],
                                                  op0=ALU.mult, op1=ALU.mult,
                                                  accum_out=act[:, (2 * q + s) % 4:(2 * q + s) % 4 + 1])
                last.then_inc(S["dots"], 1)

            def weights(q, b, slot, group):
                dve.wait_ge(S["gelu"], group + 1)
                dve.wait_ge(S["experts_used"], group + 3)
                for s in range(2):
                    j = (2 * q + s) % 4
                    last = v.tensor_scalar(diag[:, j, :], ident[:], gel[:, j:j + 1], gate[:, b, bass.ds(slot + s, 1)],
                                           ALU.mult, ALU.mult)
                last.then_inc(S["weights"], 1)

            def body(b, m, first, last_):
                for q in range(first, last_):
                    dots(q, b, [b * 16 + m * 2])
                    if q > 0:
                        weights(q - 1, b, m * 16 + 2 * (q - 1), b * 64 + m * 8 + q - 1)

            with dve.Fori(0, NB // 2) as pair:
                for par in range(2):
                    b = pair * 2 + par
                    dots(0, b, [b * 16])
                    with dve.Fori(0, 7) as m:
                        body(b, m, 1, 9)
                    body(b, 7, 1, 8)
                    weights(7, b, 7 * 16 + 14, b * 64 + 63)
                    dve.wait_ge(S["acc_done"], b + 1)
                    v.tensor_tensor(xs[:, 0, :], bank2(2 * par), gt[:], ALU.mult).then_inc(S["x2_part"], 1)
                    dve.wait_ge(S["x2_part"], b + 1)
                    v.tensor_tensor(x1[:, b, :], x1[:, b, :], xs[:, 0, :], ALU.add).then_inc(S["x2_done"], 1)
            for s in range(NS):
                dve.wait_ge(s_row[s], 16 * (NB * 128 // EBUF + 1))
                dve.wait_ge(S["xb_mm"], s + 1)
                v.scalar_tensor_tensor(out=rows[:, s, 0:D], in0=rows[:, s, 0:D], scalar=1.0, in1=bank2(6),
                                       op0=ALU.mult, op1=ALU.mult, accum_out=act[:, s % 4:s % 4 + 1]
                                       ).then_inc(S["s_dots"], 1)
                dve.wait_ge(S["s_gelu"], s + 1)
                v.tensor_scalar(wmask[:, s, :], eye8[:, s, :], gel[:, s % 4:s % 4 + 1], gsT[:, s:s + 1],
                                ALU.mult, ALU.mult).then_inc(S["s_weights"], 1)
            dve.wait_ge(S["s_acc"], 1)
            link(v.tensor_tensor(xs[0:NS, 0, :], bank2(0)[0:NS, :], gts, ALU.mult))
            v.tensor_tensor(x1[0:NS, NB, :], x1[0:NS, NB, :], xs[0:NS, 0, :], ALU.add).then_inc(S["x2_done"], 1)
            dve.wait_ge(S["sum_sq3"], NBT)
            v.tensor_scalar(ms[:], ms[:], 1.0 / D, EPS, ALU.mult, ALU.add).then_inc(S["mean_sq3"], 1)
            dve.wait_ge(S["root3"], 1)
            rsqrt(ms[:], root[:], rs[:], tm[:])
            dve.wait_ge(S["gfin_in"], 16)
            for b in range(NBT):
                w = width(b)
                v.scalar_tensor_tensor(out=x1[0:w, b, :], in0=x1[0:w, b, :], scalar=rs[0:w, b:b + 1],
                                       in1=gfin[0:w, :], op0=ALU.mult, op1=ALU.mult).then_inc(S["y_ready"], 1)


def kernel(**inputs):
    import concourse.bacc as bacc
    from concourse.bass_utils import run_bass_kernel_spmd

    a = {k: np.asarray(v) for k, v in inputs.items()}

    def cm(v):
        return v.reshape(-1, P).T

    ins = {
        "x": np.concatenate([a["x_prompt"][0], a["x_sample"][:, 0]], 0),
        "cT": np.concatenate([a["c_prompt"], a["c_sample"]], 0).T.reshape(KC, P, 1 + NS).transpose(1, 0, 2),
        "bada": cm(a["b_ada"][0]),
        "gmix": cm(a["g_mix"][0]),
        "gffn": cm(a["g_ffn"][0]),
        "w_dw": a["w_dw"][0].T.reshape(CC, P, W).transpose(1, 0, 2),
        "cvec": np.stack([cm(a["b_dw"][0]), cm(a["g_cn"][0]), cm(a["b_cn"][0])], 1),
        "keys": np.stack([a["k1"][0].T, a["k2"][0].T], 1),
        "wsT": a["w_s"][0].transpose(2, 0, 1),
        "state_T": a["state_conv"][0].transpose(2, 0, 1).reshape(CC, P, NS, W - 1).transpose(1, 0, 2, 3),
        "b_s": a["b_s"][0],
        "w_s00": a["w_s"][0][:, 0, 0:1],
        "g_v": a["g_v"],
        "b_v": a["b_v"],
        "g_final": a["g_final"][None],
        "w_ada": a["w_ada"][0],
        "w_in": a["w_in"][0],
        "w_conv_out": a["w_conv_out"][0],
        "w_gmlp_out": a["w_gmlp_out"][0],
        "w_out": a["w_out"][0],
        "w_q": a["w_q"][0],
        "experts": np.concatenate([a["u_tab"][0], a["v_tab"][0]], 1),
    }
    outs = {
        "out_y": (NT, D),
        "out_hist_p": (P, CC, W - 1),
        "out_hist_s": (P, CC, NS, W - 1),
        "out_v": (NS, DC),
    }
    nc = bacc.Bacc("TRN2", target_bir_lowering=False, num_devices=1)
    arrays, t = {}, {}
    for name, v in ins.items():
        v = np.ascontiguousarray(v)
        arrays[f"in_{name}"] = v
        t[name] = nc.dram_tensor(f"in_{name}", v.shape, mybir.dt.from_np(v.dtype), kind="ExternalInput").ap()
    for name, shape in outs.items():
        t[name] = nc.dram_tensor(name, shape, mybir.dt.float32, kind="ExternalOutput").ap()
    build(nc, t)
    got = run_bass_kernel_spmd(nc, [arrays], core_ids=[0]).results[0]
    y = got["out_y"]
    hist_p = got["out_hist_p"].transpose(2, 1, 0).reshape(1, 1, W - 1, DC)
    hist_s = got["out_hist_s"].transpose(2, 3, 1, 0).reshape(1, NS, W - 1, DC)
    return (y[:NP].reshape(1, NP, D), y[NP:].reshape(NS, 1, D), hist_p, hist_s, got["out_v"].reshape(1, NS, 1, DC))
```

```python
from contextlib import ExitStack

import numpy as np

import concourse.bass as bass
from concourse import mybir

D = 1024
NP = 1024
NS = 8
NT = NP + NS
P = 128
KC = D // P
DC = 512
CC = DC // P
W = 31
NB = NP // P
NBT = NB + 1
H = 8
HD = 64
NCH = 2 * H
TOP = 16
NKEY = 128
EPS = 1e-6
ROWS = [16, 8, 5, 4, 3, 2, 2, 2] + [1] * 8
NC = sum(ROWS)
LOW = -3.0e38
NSLOT = H * TOP
RING = 3
PIECE = 2048
NB1 = 4
GW = 520
RB1, RB2 = 6, 8
TICKS = NB1 * NSLOT
HEAVY = 3
FRONT_TICKS = 500
ROUTE_PIECES = 10
ROUTE_EXP = [2 * (ROUTE_PIECES * i + 6) for i in range(NB1 - 1)]


class Group:
    pass


def gap(n):
    for _ in range(n):
        yield


def build(nc, t):
    f32, u32 = mybir.dt.float32, mybir.dt.uint32
    ALU, ACT, AX = mybir.AluOpType, mybir.ActivationFunctionType, mybir.AxisListType
    ctx = ExitStack()
    with ctx:
        def sb(name, shape, dt=f32):
            return ctx.enter_context(nc.sbuf_tensor(name, shape, dt))

        def part(area, at, *shape):
            names = "abc"[:len(shape)]
            spec = "p (%s) -> p %s" % (" ".join(names), " ".join(names))
            return area[:, at:at + int(np.prod(shape))].rearrange(spec, **dict(zip(names, shape)))

        big = sb("big", [P, RB1 * 2 * D + KC * GW])
        rows = part(big, 0, RB2, 2 * D)
        nT = part(big, RB1 * 2 * D, KC, GW)
        mod_rows = big[0:1 + NS, 0:6 * D]
        gt1_a = big[:, 6 * D:7 * D]
        sq_a = part(big, 7 * D, NB1, D)
        mbuf = sb("mbuf", [P, KC * GW])
        mT = part(mbuf, 0, KC, GW)
        wring = sb("wring", [P, RING * PIECE])
        AW = 512 + W - 1
        arena = sb("arena", [P, CC * (AW + 2 * GW) + 5 * DC])
        aT = part(arena, 0, CC, AW)
        yT = part(arena, CC * AW, CC, GW)
        v_tm = part(arena, CC * (AW + GW), 5, DC)
        uT = part(arena, CC * (AW + GW) + 5 * DC, CC, GW)
        ysq = part(arena, CC * (AW + GW), CC, GW)
        x_first = part(arena, CC * AW, 5, D)
        eq = part(arena, CC * AW + 5 * D, 2, TOP, NC)
        xn2 = part(arena, 3768, 5, D)
        xn1 = sb("xn1", [P, NB1, D])
        v16 = part(arena, 0, 5, NCH, TOP)
        i16f = part(arena, 5 * NCH * TOP, 5, NCH, TOP)
        i16 = i16f.bitcast(u32)
        rep = part(arena, 10 * NCH * TOP, 4, NKEY)
        w1 = sb("w1", [P, 3600])
        sig, prod = part(w1, 0, 2, 512), part(w1, 1024, 2, 512)
        conv_s = w1[:, 2048:2048 + CC * NS * W].rearrange("p (c s k) -> p c s k", c=CC, s=NS)
        sgt = part(w1, 1024, CC, P)
        rbc = w1[:, 3072:3072 + GW]
        xs = part(w1, 0, 2, D)
        qbuf = part(w1, 0, 2, GW)
        qs = part(w1, 2 * GW, NCH, NS)
        rep_s = part(w1, 2 * GW + NCH * NS, 4, NKEY)
        gts = w1[0:NS, 2 * D:3 * D]
        w2 = sb("w2", [P, H * P + CC * P + 2 * DC])
        wsT = part(w2, 0, H, P)
        bs = part(w2, H * P, CC, P)
        rowv = part(w2, H * P + CC * P, 2, DC)
        gt1_b = w2[:, 0:D]
        full_s = sb("full_s", [P, CC, NS, W])
        hist = sb("hist", [P, CC, W - 1])
        eid = sb("eid", [P, NBT, NSLOT], u32)
        eid_s = sb("eid_s", [P, NSLOT])
        gate = sb("gate", [P, NBT, NSLOT])
        diag = sb("diag", [P, 4, P])
        gt2 = sb("gt2", [P, D])
        ident = sb("ident", [P, P])
        zero = sb("zero", [P, P])
        onesm = sb("onesm", [P, P])
        eye8 = sb("eye8", [P, NS, NS])
        iota = sb("iota", [P, NC])
        cT = sb("cT", [P, KC, 1 + NS])
        sigc = sb("sigc", [P, KC, 1 + NS])
        bada = sb("bada", [P, 48])
        gmix = sb("gmix", [P, KC])
        gffn = sb("gffn", [P, KC])
        mod = sb("mod", [P, 48, 1 + NS])
        scale1 = sb("scale1", [P, KC, 1 + NS])
        scale2 = sb("scale2", [P, KC, 1 + NS])
        wdw = sb("wdw", [P, CC, W])
        cvec = sb("cvec", [P, 3, CC])
        w00 = sb("w00", [P, CC])
        keys = sb("keys", [P, 2, NKEY])
        stat = sb("stat", [P, 4, NBT])
        bnst = sb("bnst", [P, 2, 6])
        mv = sb("mv", [P, NBT, 2])
        vroot = sb("vroot", [P, NBT])
        eps = sb("eps", [P, 1])
        smx = sb("smx", [P, 5 * H])
        act = sb("act", [P, 4])
        gel = sb("gel", [P, 4])
        idx = sb("idx", [P, 16], u32)
        idxs = sb("idxs", [P, NS], u32)
        gsT = sb("gsT", [P, NS])
        sT = sb("sT", [P, 2, 32])
        wmask = sb("wmask", [P, NS, NS])

        ps = ctx.enter_context(nc.psum_tensor("ps", [P, 8, 512], f32))

        def bank2(b):
            return ps[:, b:b + 2, :].rearrange("p b n -> p (b n)")

        def pair(i):
            return 2 + 2 * (i % 3)

        group_names = """x_in sum_sq mean_sq root xs_ready xT_mm nT_done gate_mm lin_mm sig_a a_done
            u_mm u_done v_mm v_stat v_root v_done sg_mm sg_done conv gb_mm ob_mm sig_b mb_done mean_mm yc sq_act
            var_mm std_act yn_done sig_y y_done ga_mm oa_mm sig_g m_done wo_mm x1_done gt_mm gt_done t2b_mm n2_done
            q_mm q_done s_mm s_done sm_diff sm_exp routes tables out_x1""".split()
        S = {f"{n}{g}": ctx.enter_context(nc.semaphore(f"{n}{g}")) for n in group_names for g in (1, 2)}
        for n in """c_in small_in gfin_in consts masked sigmoid_c silu ada_mm ada_row adaT_mm mod_done
                dve_chain pool_chain dots gelu weights rows_used acc_done acc_read hist_kept x_again
                xb_mm s_dots s_gelu s_weights s_acc idx_ready idxs_ready qs_mm
                x1_back x2_done fin_sq fin_ms fin_root y_ready out_y out_hist out_v""".split():
            S[n] = ctx.enter_context(nc.semaphore(n))
        s_piece = [ctx.enter_context(nc.semaphore(f"piece{i}")) for i in range(RING)]
        s_row = [ctx.enter_context(nc.semaphore(f"rows{i}")) for i in range(RB2)]
        fills = [len(range(r, TICKS, RB1)) if r < RB1 else 0 for r in range(RB2)]

        def width(b):
            return P if b < NB else NS

        def group(n, blocks, tg, xn, tables):
            g = Group()
            g.n, g.blocks, g.nb, g.tg, g.xn = n, blocks, len(blocks), tg, xn
            g.nt = sum(width(b) for b in blocks)
            g.ng = g.nt // tg
            g.np = 4 * P
            g.S = {k: S[f"{k}{n}"] for k in group_names}
            g.cand = part(tables, 0, g.nb * H, NC)
            g.cid = part(tables, g.nb * H * NC, g.nb * H, NC)
            g.posf = part(mbuf, 3200, g.nb * H, TOP) if n == 1 else part(mbuf, 0, g.nb * H, TOP)
            g.crep = part(mbuf, 3200 + 512, H, NC) if n == 1 else part(mbuf, 1024, H, NC)
            g.eq = eq if n == 1 else part(mbuf, 2048, 2, TOP, NC)
            g.sq = sq_a if n == 1 else None
            g.gt1 = gt1_a if n == 1 else gt1_b
            return g

        G1 = group(1, list(range(NB1)), 512, xn1, mbuf)
        G2 = group(2, list(range(NB1, NBT)), 260, xn2, wring)

        def cols(b):
            i = b % 4 if b < NB else 4
            return slice(i * P, i * P + width(b))

        def local(b):
            return b if b < NB1 else b - NB1

        w_in, pieces, first_piece = t["w_in"], [], {}
        for i in range(24):
            pieces.append(("ada", t["w_ada"], i, S["ada_mm"], i + 1))
        for g in (G1, G2):
            ng = g.ng
            first_piece[g.n] = len(pieces)
            for half in range(2):
                pieces.append(("in", w_in, 2 + half, g.S["lin_mm"], 2 * ng * (half + 1)))
                pieces.append(("in", w_in, half, g.S["lin_mm"], 2 * ng * (half + 1)))
            for half in range(2):
                pieces.append(("in", w_in, 4 + half, g.S["u_mm"], 2 * ng * (half + 1)))
            for half in range(2):
                pieces.append(("in", w_in, 6 + half, g.S["v_mm"], g.nb))
            for base, wout, done in ((12, t["w_gmlp_out"], "ob_mm"), (8, t["w_conv_out"], "oa_mm")):
                for col in range(4):
                    if col % 2 == 0:
                        pieces.append(("out", wout, col // 2, g.S[done], 2 * ng * (col + 2)))
                    pieces.append(("in", w_in, base + col, g.S[done], 2 * ng * (col + 1)))
            for i in range(4):
                pieces.append(("wo", t["w_out"], i, g.S["wo_mm"], g.nb * (i + 1)))
            for i in range(8):
                pieces.append(("wq", t["w_q"], i, g.S["q_mm"], 2 * ng * (i + 1)))

        def piece(n):
            k = CC if pieces[n][0] == "out" else KC
            return wring[:, (n % RING) * PIECE:(n % RING + 1) * PIECE].rearrange("p (k n) -> p k n", k=k)

        def norm_steps(g):
            yield from [1] * (g.nb + 7)
            yield from [2] * (2 * g.nb)

        def front_weights(g):
            for work, idle in ((4 * CC * g.ng, 5), (2 * CC * g.ng, 5), (4 * g.nb, 12), (2 * g.nb, 5),
                               (3 * KC * g.ng, 5), (2 * g.ng, 17), (3 * KC * g.ng, 7), (8 * g.nb, 3)):
                if work == 4 * CC * g.ng:
                    yield from norm_steps(g)
                    yield from [1] * 5
                yield from [HEAVY] * work
                yield from [1] * idle
            yield from norm_steps(g)
            yield from [1] * 5
            yield from [HEAVY] * (2 * g.nb)
            yield from [1] * 3
            yield from [HEAVY] * (NCH * (2 * g.ng + 1))
            yield from [1] * (2 * g.ng + 1) * 3
            yield from [1] * 4 + [2] * 36

        def interleave(peer, front):
            weights = list(front_weights(G2))
            total, spent, at = sum(weights), 0, 0
            for tick in range(TICKS):
                peer(tick)
                while at < len(weights) and spent < total * (tick + 1) / FRONT_TICKS:
                    spent += weights[at]
                    at += 1
                    next(front, None)
            for _ in front:
                pass

        taps_per_step = {g.n: -(-CC * W // (2 * CC * g.ng + 4 * g.nb + 3 * KC * g.ng)) for g in (G1, G2)}

        def x1_again(b):
            return mbuf[:, b * D:(b + 1) * D] if b < NB1 else wring[:, (b - NB1) * D:(b - NB1 + 1) * D]

        gfin = wring[:, 5 * D:6 * D]
        SMALL_IN = 16 * (4 + CC + 2 * H + 2)

        block = ctx.enter_context(nc.Block())

        @block.sync
        def _(sp):
            for name, dst in (("cT", cT), ("bada", bada), ("gmix", gmix), ("gffn", gffn)):
                sp.dma_start(dst[:], t[name]).then_inc(S["c_in"], 16)
            for b in G1.blocks:
                sp.dma_start(xn1[:, b, :], t["x"][b * P:(b + 1) * P, :]).then_inc(S["x_in1"], 16)

            def load(n):
                kind, src, col, _, _ = pieces[n]
                if n >= RING:
                    done, count = pieces[n - RING][3:]
                    sp.wait_ge(done, count)
                w = 512 if kind == "out" else 256
                sp.dma_start(piece(n), src[:, col * w:(col + 1) * w].rearrange("(k p) n -> p k n", p=P)
                             ).then_inc(s_piece[n % RING], 16)

            for n in range(8):
                load(n)
            sp.dma_start(wdw[:], t["w_dw"]).then_inc(S["small_in"], 16)
            sp.dma_start(cvec[:], t["cvec"]).then_inc(S["small_in"], 16)
            sp.dma_start(keys[:], t["keys"]).then_inc(S["small_in"], 16)
            sp.dma_start(wsT, t["wsT"]).then_inc(S["small_in"], 16)
            for c in range(CC):
                sp.dma_start(full_s[:, c, :, 0:W - 1], t["state_T"][:, c, :, :]).then_inc(S["small_in"], 16)
            for h in range(H):
                at = slice(HD * (h % 2), HD * (h % 2) + HD)
                sp.dma_start(bs[at, h // 2, :], t["b_s"][h:h + 1, :].broadcast_to([HD, P])).then_inc(S["small_in"], 16)
                sp.dma_start(w00[at, h // 2:h // 2 + 1], t["w_s00"][h:h + 1, :].broadcast_to([HD, 1])
                             ).then_inc(S["small_in"], 16)
            for i, name in enumerate(("g_v", "b_v")):
                sp.dma_start(rowv[:, i, :], t[name].broadcast_to([P, DC])).then_inc(S["small_in"], 16)

            def spill(g):
                sp.wait_ge(g.S["x1_done"], 4 * g.nb)
                for b in g.blocks:
                    w = width(b)
                    sp.dma_start(t["x1_rows"][b * P:b * P + w, :], g.xn[0:w, local(b), :]).then_inc(g.S["out_x1"], 16)

            for n in range(8, first_piece[2]):
                load(n)
                if pieces[n][0] == "wq" and pieces[n - 1][0] == "wo":
                    spill(G1)
            sp.wait_ge(S["oa_mm1"], KC * G1.ng)
            sp.wait_ge(S["s_done1"], NCH)
            sp.wait_ge(S["sq_act1"], 1)
            sp.wait_ge(S["tables1"], 1)
            for b in G2.blocks:
                w = width(b)
                sp.dma_start(x_first[0:w, local(b), :], t["x"][b * P:b * P + w, :]).then_inc(S["x_in2"], 16)
            first_wo = max(n for n, p in enumerate(pieces) if p[0] == "wo") - 3
            for n in range(first_piece[2], len(pieces)):
                if n == first_piece[2] + 11:
                    sp.wait_ge(S["a_done2"], CC * G2.ng)
                    sp.dma_start(t["out_hist_p"], aT[:, :, AW - W + 1:AW]).then_inc(S["out_hist"], 16)
                    for c in range(CC):
                        sp.dma_start(t["out_hist_s"][:, c, :, :], full_s[:, c, :, 1:W]).then_inc(S["out_hist"], 16)
                    sp.wait_ge(S["v_done2"], G2.nb)
                    sp.dma_start(t["out_v"], v_tm[0:NS, 4, :]).then_inc(S["out_v"], 16)
                if n == first_wo + 2:
                    sp.wait_ge(S["oa_mm2"], KC * G2.ng)
                    sp.wait_ge(S["out_v"], 16)
                    for b in G2.blocks:
                        w = width(b)
                        sp.dma_start(xn2[0:w, local(b), :], t["x"][b * P:b * P + w, :]).then_inc(S["x_again"], 16)
                if pieces[n][0] == "wq" and pieces[n - 1][0] == "wo":
                    load(n)
                    spill(G2)
                    continue
                load(n)
            sp.wait_ge(S["out_hist"], 16 * (1 + CC))
            sp.wait_ge(S["routes2"], G2.nb)
            for g, area in ((G1, None), (G2, None)):
                sp.wait_ge(g.S["out_x1"], 16 * g.nb)
            for b in range(NBT):
                w = width(b)
                sp.dma_start(x1_again(b)[0:w, :], t["x1_rows"][b * P:b * P + w, :]).then_inc(S["x1_back"], 16)
            sp.dma_start(gfin, t["g_final"].broadcast_to([P, D])).then_inc(S["gfin_in"], 16)

        @block.tensor
        def _(pe):
            mmul = nc.tensor.matmul

            def arrived(n):
                pe.wait_ge(s_piece[n % RING], 16 * (n // RING + 1))

            def ada_turn(n):
                pe.wait_ge(S["ada_row"], n + 1)
                for j in range(2):
                    at = (2 * n + j) * (1 + NS)
                    mm = nc.tensor.transpose(ps[:, 2, at:at + 1 + NS], mod_rows[:, (2 * n + j) * P:(2 * n + j + 1) * P],
                                             ident[0:1 + NS, 0:1 + NS])
                mm.then_inc(S["adaT_mm"], 1)

            pe.wait_ge(S["silu"], 1)
            pe.wait_ge(S["consts"], 1)
            for n in range(24):
                arrived(n)
                if n >= 4:
                    pe.wait_ge(S["ada_row"], n - 3)
                for c in range(KC):
                    mm = mmul(ps[0:1 + NS, 4 + n % 4, 0:256], cT[:, c, :], piece(n)[:, c, :],
                              start=(c == 0), stop=(c == KC - 1))
                mm.then_inc(S["ada_mm"], 1)
                if n >= 1:
                    ada_turn(n - 1)
            ada_turn(23)
            pe.wait_ge(S["mod_done"], 1)

            def front(g):
                s, tg, ng, nb = g.S, g.tg, g.ng, g.nb
                n = first_piece[g.n]

                def tiles(n, col, gi, out, done, src=nT, k=KC):
                    for c in range(k):
                        mm = mmul(out, piece(n)[:, c, col:col + P], src[:, c, gi * tg:(gi + 1) * tg],
                                  start=(c == 0), stop=(c == k - 1))
                        if c == k - 1:
                            mm.then_inc(done, 1)
                        if c % 4 == 3:
                            yield

                def norm(turn):
                    yield from gap(nb + 7)
                    for i, b in enumerate(g.blocks):
                        w = width(b)
                        pe.wait_ge(s["xs_ready"], turn * nb + i + 1)
                        if i >= 3:
                            pe.wait_ge(s["nT_done"], turn * nb + i - 2)
                        for c in range(KC):
                            mm = nc.tensor.transpose(bank2(pair(i))[:, c * P:c * P + w], xs[0:w, i % 2, c * P:(c + 1) * P],
                                                     ident[0:w, 0:w])
                        mm.then_inc(s["xT_mm"], 1)
                        yield from gap(2)

                yield from norm(0)
                yield from gap(5)
                pe.wait_ge(s["nT_done"], nb)
                for i in range(CC * ng):
                    c, gi = i // ng, i % ng
                    if i % (2 * ng) == 0:
                        arrived(n)
                        arrived(n + 1)
                    if i >= 3:
                        pe.wait_ge(s["a_done"], i - 2)
                    yield from tiles(n, (c % 2) * P, gi, ps[:, pair(i), 0:tg], s["gate_mm"])
                    yield from tiles(n + 1, (c % 2) * P, gi, ps[:, pair(i) + 1, 0:tg], s["lin_mm"])
                    if i % (2 * ng) == 2 * ng - 1:
                        n += 2
                yield from gap(5)
                pe.wait_ge(s["a_done"], CC * ng)
                for i in range(CC * ng):
                    c, gi = i // ng, i % ng
                    if i % (2 * ng) == 0:
                        arrived(n)
                    if i >= 6:
                        pe.wait_ge(s["u_done"], i - 5)
                    yield from tiles(n, (c % 2) * P, gi, ps[:, 2 + i % 6, 0:tg], s["u_mm"])
                    if i % (2 * ng) == 2 * ng - 1:
                        n += 1
                yield from gap(5)
                pe.wait_ge(s["u_done"], CC * ng)
                arrived(n)
                arrived(n + 1)
                for i, b in enumerate(g.blocks):
                    for half in range(2):
                        for c in range(KC):
                            mm = mmul(ps[0:width(b), 2 + i % 6, half * 256:(half + 1) * 256], nT[:, c, cols(b)],
                                      piece(n + half)[:, c, :], start=(c == 0), stop=(c == KC - 1))
                            if (half, c) == (1, KC - 1):
                                mm.then_inc(s["v_mm"], 1)
                            if c % 4 == 3:
                                yield
                n += 2
                yield from gap(12)
                pe.wait_ge(s["v_done"], nb)
                pe.wait_ge(S["masked"], 1)
                for i, b in enumerate(g.blocks):
                    if i >= 3:
                        pe.wait_ge(s["sg_done"], i - 2)
                    for c in range(CC):
                        if b < NB:
                            mm = mmul(bank2(pair(i))[:, 256 * c:256 * (c + 1)], v_tm[:, i, c * P:(c + 1) * P],
                                      wsT[:, 2 * c:2 * c + 2, :].rearrange("p h i -> p (h i)"), start=True, stop=True)
                        else:
                            mm = nc.tensor.transpose(ps[:, pair(i), c * NS:(c + 1) * NS], v_tm[0:NS, i, c * P:(c + 1) * P],
                                                     ident[0:NS, 0:NS])
                    mm.then_inc(s["sg_mm"], 1)
                    yield from gap(2)
                yield from gap(5)
                pe.wait_ge(s["sg_done"], nb)

                def branch(n, src, gate_sem, out_sem, done):
                    for i in range(KC * ng):
                        j, gi = i // ng, i % ng
                        if i % (4 * ng) == 0:
                            no = n
                            arrived(no)
                            n += 1
                        if i % (2 * ng) == 0:
                            arrived(n)
                        if i >= 3:
                            pe.wait_ge(s[done], i - 2)
                        yield from tiles(n, (j % 2) * P, gi, ps[:, pair(i), 0:tg], s[gate_sem])
                        yield from tiles(no, (j % 4) * P, gi, ps[:, pair(i) + 1, 0:tg], s[out_sem], src, CC)
                        if i % (2 * ng) == 2 * ng - 1:
                            n += 1
                    yield from gap(5)

                yield from branch(n, uT, "gb_mm", "ob_mm", "mb_done")
                n += 6
                pe.wait_ge(s["conv"], CC * W + (1 if g.n == 2 else 0))
                pe.wait_ge(s["mb_done"], KC * ng)
                for gi in range(ng):
                    for c in range(CC):
                        mm = mmul(ps[:, 2 + gi, 0:tg], onesm[:], yT[:, c, gi * tg:(gi + 1) * tg],
                                  start=(c == 0), stop=(c == CC - 1))
                    mm.then_inc(s["mean_mm"], 1)
                    yield
                yield from gap(6)
                pe.wait_ge(s["sq_act"], ng)
                for gi in range(ng):
                    for c in range(CC):
                        mm = mmul(ps[:, 4 + gi, 0:tg], onesm[:], ysq[:, c, gi * tg:(gi + 1) * tg],
                                  start=(c == 0), stop=(c == CC - 1))
                    mm.then_inc(s["var_mm"], 1)
                    yield
                yield from gap(6)
                yield from gap(5)
                pe.wait_ge(s["y_done"], CC)
                yield from branch(n, yT, "ga_mm", "oa_mm", "m_done")
                n += 6
                pe.wait_ge(s["m_done"], KC * ng)
                for k, bank in ((2, 2), (5, 4)) if g.n == 1 else ((2, None),):
                    for c in range(KC):
                        at = slice(c * P, (c + 1) * P)
                        mm = mmul(bank2(bank or 2)[:, at], mod[:, k * KC + c, 0:1].broadcast_to([P, P]), ident[:],
                                  start=True, stop=True)
                        if g.n == 2:
                            mm = nc.tensor.transpose(bank2(6)[0:NS, at], mod[:, k * KC + c, 1:1 + NS], ident[:])
                mm.then_inc(s["gt_mm"], 1)
                yield from gap(2)
                pe.wait_ge(s["gt_done"], 1)
                for i in range(4 * nb):
                    col, b = i // nb, g.blocks[i % nb]
                    w = width(b)
                    if i % nb == 0:
                        arrived(n + col)
                    if i >= 6:
                        pe.wait_ge(s["x1_done"], i - 5)
                    for c in range(KC):
                        mm = mmul(ps[0:w, 2 + i % 6, 0:256], mT[:, c, cols(b)], piece(n + col)[:, c, :],
                                  start=(c == 0), stop=(c == KC - 1))
                        if c == KC - 1:
                            mm.then_inc(s["wo_mm"], 1)
                        if c % 4 == 3:
                            yield
                n += 4
                yield from gap(3)
                pe.wait_ge(s["x1_done"], 4 * nb)
                yield from norm(1)
                yield from gap(5)
                pe.wait_ge(s["nT_done"], 2 * nb)
                for i, b in enumerate(g.blocks):
                    w = width(b)
                    if i >= 3:
                        pe.wait_ge(s["n2_done"], i - 2)
                    for c in range(KC):
                        mm = nc.tensor.transpose(bank2(pair(i))[0:w, c * P:(c + 1) * P], nT[:, c, cols(b)], ident[:])
                    mm.then_inc(s["t2b_mm"], 1)
                    yield from gap(2)
                yield from gap(3)
                pe.wait_ge(s["n2_done"], nb)
                for ch in range(NCH + 3):
                    if ch < NCH:
                        if ch % 2 == 0:
                            arrived(n + ch // 2)
                        if ch >= 2:
                            pe.wait_ge(s["q_done"], ch - 1)
                        for gi in range(ng):
                            yield from tiles(n + ch // 2, (ch % 2) * P, gi, ps[:, 2 + 2 * (ch % 2) + gi, 0:tg], s["q_mm"])
                    else:
                        yield from gap(2 * ng)
                    if ch >= 2 and ch - 2 < NCH:
                        k = ch - 2
                        pe.wait_ge(s["q_done"], k + 1)
                        if k >= 2:
                            pe.wait_ge(s["s_done"], k - 1)
                        for i in range(4):
                            mm = mmul(ps[:, 6 + k % 2, i * P:(i + 1) * P], qbuf[:, k % 2, i * P:(i + 1) * P],
                                      keys[:, k % 2, :], start=True, stop=True)
                        mm.then_inc(s["s_mm"], 1)
                    yield
                yield from gap(4)
                if g.n == 2:
                    pe.wait_ge(s["q_done"], NCH)
                    for ch in range(NCH):
                        mm = mmul(ps[0:NS, 2 + ch // 4, (ch % 4) * P:(ch % 4 + 1) * P], qs[:, ch, :], keys[:, ch % 2, :],
                                  start=True, stop=True)
                    mm.then_inc(S["qs_mm"], 1)
                    pe.wait_ge(s["s_done"], NCH)
                    for c in range(KC):
                        mm = nc.tensor.transpose(bank2(6)[0:NS, c * P:(c + 1) * P], mod[:, 5 * KC + c, 1:1 + NS], ident[:])
                    mm.then_inc(s["gt_mm"], 1)
                yield from gap(36)

            for _ in front(G1):
                pass

            def open_acc(b):
                if b >= 1:
                    pe.wait_ge(S["acc_read"], b)
                for half in range(2):
                    mmul(ps[:, half, :], zero[:], zero[:, 0:1].broadcast_to([P, 512]), start=True, stop=False)

            def close_acc():
                for half in range(2):
                    mm = mmul(ps[:, half, :], zero[:], zero[:, 0:1].broadcast_to([P, 512]), start=False, stop=True)
                mm.then_inc(S["acc_done"], 1)

            def value(j, r):
                for half in range(2):
                    mm = mmul(ps[:, half, :], diag[:, j, :], rows[:, r, D + 512 * half:D + 512 * (half + 1)],
                              start=False, stop=False)
                return mm

            def peer(tick):
                if tick == 0:
                    return
                n = tick - 1
                if n % NSLOT == 0:
                    open_acc(n // NSLOT)
                pe.wait_ge(S["weights"], n + 1)
                value(n % 4, n % RB1).then_inc(S["rows_used"], 1)
                if n % NSLOT == NSLOT - 1:
                    close_acc()

            interleave(peer, front(G2))
            peer(TICKS)
            with pe.Fori(0, NB - NB1) as bb:
                pe.wait_ge(S["acc_read"], bb + NB1)
                for half in range(2):
                    mmul(ps[:, half, :], zero[:], zero[:, 0:1].broadcast_to([P, 512]), start=True, stop=False)
                with pe.Fori(0, 8) as m:
                    for q in range(8):
                        pe.wait_ge(S["weights"], bb * 64 + m * 8 + (TICKS + q + 1))
                        value(2 * q % 4, 2 * q % RB2)
                        value((2 * q + 1) % 4, (2 * q + 1) % RB2).then_inc(S["rows_used"], 1)
                close_acc()
            def sample_x(k):
                if k >= 3:
                    pe.wait_ge(S["s_dots"], k - 2)
                for half in range(2):
                    mm = mmul(ps[:, pair(k) + half, :], ident[0:NS, k:k + 1].broadcast_to([NS, P]),
                              xn2[0:NS, 4, 512 * half:512 * (half + 1)], start=True, stop=True)
                mm.then_inc(S["xb_mm"], 1)

            for k in range(3):
                sample_x(k)
            pe.wait_ge(S["acc_read"], NB)
            for k in range(NS):
                pe.wait_ge(S["s_weights"], k + 1)
                for half in range(2):
                    mm = mmul(ps[0:NS, half, :], wmask[:, k, :], rows[:, k, D + 512 * half:D + 512 * (half + 1)],
                              start=(k == 0), stop=(k == NS - 1))
                if k + 3 < NS:
                    sample_x(k + 3)
            mm.then_inc(S["s_acc"], 1)

        @block.scalar
        def _(act_):
            ac = nc.scalar.activation
            act_.wait_ge(S["c_in"], 64)
            ac(sigc[:], cT[:], ACT.Sigmoid).then_inc(S["sigmoid_c"], 1)
            for n in range(24):
                act_.wait_ge(S["ada_mm"], n + 1)
                ac(mod_rows[:, n * 256:(n + 1) * 256], ps[0:1 + NS, 4 + n % 4, 0:256], ACT.Copy).then_inc(S["ada_row"], 1)

            def front(g):
                s, tg, ng, nb = g.S, g.tg, g.ng, g.nb
                if g.n == 2:
                    yield from gap(2)

                def norm(turn):
                    for i, b in enumerate(g.blocks):
                        w = width(b)
                        if g.n == 1:
                            x, out = xn1[0:w, i, :], g.sq[0:w, i, :]
                        else:
                            x = (x_first if turn == 0 else xn2)[0:w, i, :]
                            out = part(big, RB1 * 2 * D, 4, D)[0:w, i % 4, :]
                        if i == 0:
                            act_.wait_ge(S["consts"], 1)
                            act_.wait_ge(s["x_in"], 16 * nb)
                            if turn == 1:
                                act_.wait_ge(s["x1_done"], 4 * nb)
                        if i == 4:
                            act_.wait_ge(s["sum_sq"], turn * nb + 1)
                        ac(out, x, ACT.Square, accum_out=stat[0:w, 0, b:b + 1]).then_inc(s["sum_sq"], 1)
                        yield
                    yield from gap(2)
                    act_.wait_ge(s["mean_sq"], turn + 1)
                    lo, hi = g.blocks[0], g.blocks[-1] + 1
                    ac(stat[:, 1, lo:hi], stat[:, 0, lo:hi], ACT.Sqrt).then_inc(s["root"], 1)
                    yield from gap(5 + 2 * nb)

                if g.n == 2:
                    act_.wait_ge(S["q_mm1"], NCH * G1.ng)
                    act_.wait_ge(S["t2b_mm1"], G1.nb)
                yield from norm(0)
                yield from gap(5)
                for i in range(CC * ng):
                    yield from gap(3)
                    act_.wait_ge(s["gate_mm"], i + 1)
                    if i >= 2:
                        act_.wait_ge(s["a_done"], i - 1)
                    elif i == 0:
                        act_.wait_ge(s["xT_mm"], nb)
                    ac(sig[:, i % 2, 0:tg], ps[:, pair(i), 0:tg], ACT.Sigmoid).then_inc(s["sig_a"], 1)
                    yield
                yield from gap(5)
                if g.n == 2:
                    act_.wait_ge(S["routes1"], G1.nb)
                for i in range(CC * ng):
                    c, gi = i // ng, i % ng
                    yield
                    act_.wait_ge(s["u_mm"], i + 1)
                    ac(uT[:, c, gi * tg:(gi + 1) * tg], ps[:, 2 + i % 6, 0:tg], ACT.Copy).then_inc(s["u_done"], 1)
                    yield
                yield from gap(5)
                for i in range(nb + 2):
                    yield
                    if i >= 2:
                        b = g.blocks[i - 2]
                        w = width(b)
                        act_.wait_ge(s["v_stat"], i - 1)
                        ac(vroot[0:w, b:b + 1], mv[0:w, b, 1:2], ACT.Sqrt, bias=eps[0:w, :]).then_inc(s["v_root"], 1)
                    yield from gap(3)
                yield from gap(4 + 2 * nb + 5)

                def gates(gate_sem, sig_sem, done):
                    for i in range(KC * ng):
                        yield from gap(2)
                        act_.wait_ge(s[gate_sem], i + 1)
                        if i >= 2:
                            act_.wait_ge(s[done], i - 1)
                        ac(sig[:, i % 2, 0:tg], ps[:, pair(i), 0:tg], ACT.Sigmoid).then_inc(s[sig_sem], 1)
                        yield
                    yield from gap(5)

                yield from gates("gb_mm", "sig_b", "mb_done")
                yield from gap(ng + 3)
                act_.wait_ge(s["yc"], 1)
                if g.n == 2:
                    act_.wait_ge(S["out_v"], 16)
                for gi in range(ng):
                    at = slice(gi * tg, (gi + 1) * tg)
                    ac(ysq[:, :, at], yT[:, :, at], ACT.Square).then_inc(s["sq_act"], 1)
                    yield
                yield from gap(3)
                act_.wait_ge(s["var_mm"], ng)
                for gi in range(ng):
                    ac(rbc[:, gi * tg:(gi + 1) * tg], ps[:, 4 + gi, 0:tg], ACT.Sqrt, bias=eps[:]).then_inc(s["std_act"], 1)
                yield from gap(4)
                act_.wait_ge(s["yn_done"], 1)
                for c in range(CC):
                    ac(ysq[:, c, 0:g.nt], yT[:, c, 0:g.nt], ACT.Sigmoid, scale=cvec[:, 1, c:c + 1],
                       bias=cvec[:, 2, c:c + 1]).then_inc(s["sig_y"], 1)
                yield from gap(7)
                act_.wait_ge(s["mb_done"], KC * ng)
                yield from gates("ga_mm", "sig_g", "m_done")
                act_.wait_ge(s["gt_mm"], 1)
                if g.n == 1:
                    act_.wait_ge(S["adaT_mm"], 24)
                    ac(gt2[:], bank2(4), ACT.Copy)
                else:
                    act_.wait_ge(s["v_done"], nb)
                    act_.wait_ge(s["sg_done"], nb)
                    ac(gts, bank2(6)[0:NS, :], ACT.Copy)
                ac(g.gt1, bank2(2), ACT.Copy).then_inc(s["gt_done"], 1)
                yield from gap(2)
                yield from gap(8 * nb + 3)
                yield from norm(1)
                yield from gap(5)
                for i, b in enumerate(g.blocks):
                    w = width(b)
                    yield
                    act_.wait_ge(s["t2b_mm"], i + 1)
                    if i == 0:
                        act_.wait_ge(s["out_x1"], 16 * nb)
                    ac(g.xn[0:w, i, :], bank2(pair(i))[0:w, :], ACT.Copy).then_inc(s["n2_done"], 1)
                    yield
                yield from gap(3)
                for ch in range(NCH + 3):
                    yield from gap(2 * ng - 1)
                    if ch < NCH:
                        act_.wait_ge(s["q_mm"], ng * (ch + 1))
                        if ch >= 2:
                            act_.wait_ge(s["s_mm"], ch - 1)
                        for gi in range(ng):
                            last = ac(qbuf[:, ch % 2, gi * tg:(gi + 1) * tg], ps[:, 2 + 2 * (ch % 2) + gi, 0:tg], ACT.Copy)
                        if g.n == 2:
                            last = ac(qs[:, ch, :], ps[:, 3 + 2 * (ch % 2), tg - NS:tg], ACT.Copy)
                        last.then_inc(s["q_done"], 1)
                    yield from gap(2)
                yield from gap(8)
                if g.n == 2:
                    act_.wait_ge(s["gt_mm"], 2)
                    act_.wait_ge(s["x1_done"], 4 * nb)
                    ac(gts, bank2(6)[0:NS, :], ACT.Copy).then_inc(s["gt_done"], 1)
                yield from gap(27)
                next(g.numerators)
                yield from gap(5)

            def numerators(g):
                for i, b in enumerate(g.blocks):
                    act_.wait_ge(g.S["sm_diff"], i + 1)
                    ac(gate[:, b, :], gate[:, b, :], ACT.Exp).then_inc(g.S["sm_exp"], 1)
                    yield

            for g in (G1, G2):
                g.numerators = numerators(g)
            for _ in front(G1):
                pass

            def peer(tick):
                j = tick % 4
                act_.wait_ge(S["dots"], tick + 1)
                ac(gel[:, j:j + 1], act[:, j:j + 1], ACT.Gelu).then_inc(S["gelu"], 1)
                if tick in ROUTE_EXP:
                    next(G1.numerators)

            interleave(peer, front(G2))
            for bb in range(NB - NB1):
                def gelu(q, at):
                    act_.wait_ge(S["dots"], at + 1)
                    ac(gel[:, 2 * q:2 * q + 2], act[:, 2 * q:2 * q + 2], ACT.Gelu).then_inc(S["gelu"], 1)

                first = TICKS + bb * 64
                for q in range(8):
                    gelu(q % 2, first + q)
                next(G2.numerators)
                with act_.Fori(0, 28) as m:
                    for q in range(2):
                        gelu(q, m * 2 + (first + 8 + q))
            for k in range(NS):
                act_.wait_ge(S["s_dots"], k + 1)
                ac(gel[:, k % 4:k % 4 + 1], act[:, k % 4:k % 4 + 1], ACT.Gelu).then_inc(S["s_gelu"], 1)
            for b in range(NBT):
                w = width(b)
                act_.wait_ge(S["x2_done"], b + 1)
                ac(part(big, 0, NBT, D)[0:w, b, :], x1_again(b)[0:w, :], ACT.Square, accum_out=stat[0:w, 0, b:b + 1]
                   ).then_inc(S["fin_sq"], 1)
            act_.wait_ge(S["fin_ms"], 1)
            ac(stat[:, 1, :], stat[:, 0, :], ACT.Sqrt).then_inc(S["fin_root"], 1)
            for b in range(NBT):
                w = width(b)
                act_.wait_ge(S["y_ready"], b + 1)
                act_.dma_start(t["out_y"][b * P:b * P + w, :], x1_again(b)[0:w, :]).then_inc(S["out_y"], 16)
            act_.wait_ge(S["out_y"], 16 * NBT)

        @block.gpsimd
        def _(pool):
            gp = nc.gpsimd
            gp.memset(ident[:], 0.0)
            gp.memset(zero[:], 0.0)
            gp.memset(onesm[:], 1.0 / DC)
            gp.memset(stat[:], 1.0)
            gp.memset(eps[:], EPS)
            gp.iota(iota[:], [[1, NC]], base=0, channel_multiplier=0, allow_small_or_imprecise_dtypes=True)
            gp.memset(eye8[:], 0.0).then_inc(S["pool_chain"], 1)
            pool.wait_ge(S["pool_chain"], 1)
            gp.affine_select(out=eye8[:], in_=eye8[:], compare_op=ALU.not_equal, fill=1.0, base=0,
                             pattern=[[1, NS], [-1, NS]], channel_multiplier=0)
            gp.affine_select(out=ident[:], in_=ident[:], compare_op=ALU.not_equal, fill=1.0, base=0,
                             pattern=[[-1, P]], channel_multiplier=1).then_inc(S["consts"], 1)
            pool.wait_ge(S["small_in"], SMALL_IN)
            gp.affine_select(out=wsT, in_=wsT, compare_op=ALU.is_ge, fill=0.0, base=0,
                             pattern=[[0, H], [1, P]], channel_multiplier=-1).then_inc(S["masked"], 1)

            def fetch(r, index, done):
                gp.indirect_dma_start(rows[:, r, :], None, t["experts"],
                                      bass.IndirectOffsetOnAxis(ap=index, axis=0)).then_inc(done, 16)

            for n in range(TICKS):
                b, slot = n // NSLOT, n % NSLOT
                if slot == 0:
                    pool.wait_ge(S["routes1"], b + 1)
                if n >= RB1:
                    pool.wait_ge(S["rows_used"], n - RB1 + 1)
                fetch(n % RB1, eid[:, b, slot:slot + 1], s_row[n % RB1])
            pool.wait_ge(S["rows_used"], TICKS)
            pool.wait_ge(S["q_mm2"], NCH * G2.ng)
            pool.wait_ge(S["routes2"], 1)
            slots = eid[:].rearrange("p b n -> p (b n)")
            gp.tensor_copy(idx[:, 0:2], slots[:, NB1 * NSLOT:NB1 * NSLOT + 2]).then_inc(S["idx_ready"], 1)
            for bb in range(NB - NB1):
                def eight(m, last=False):
                    for q in range(8):
                        if last and q == 7:
                            pool.wait_ge(S["routes2"], bb + 2)
                        pool.wait_ge(S["idx_ready"], m * 8 + (bb * 64 + q + 1))
                        pool.wait_ge(S["rows_used"], m * 8 + (TICKS - RB2 // 2 + bb * 64 + q + 1))
                        nxt, at = 2 * ((q + 1) % 8), m * 16 + ((NB1 + bb) * NSLOT + 2 * q + 2)
                        gp.tensor_copy(idx[:, nxt:nxt + 2], slots[:, bass.ds(at, 2)]).then_inc(S["idx_ready"], 1)
                        for k in range(2):
                            r = (2 * q + k) % RB2
                            fetch(r, idx[:, 2 * q + k:2 * q + k + 1], s_row[r])

                with pool.Fori(0, 7) as m:
                    eight(m)
                eight(7, last=True)
            pool.wait_ge(S["idxs_ready"], 1)
            for k in range(NS):
                if k % 2 == 0:
                    pool.wait_ge(S["rows_used"], TICKS + 64 * (NB - NB1) - RB2 // 2 + k // 2 + 1)
                fetch(k, idxs[:, k:k + 1], s_row[k])

        @block.vector
        def _(dve):
            v = nc.vector
            k_ = [0]

            def link(ins):
                k_[0] += 1
                ins.then_inc(S["dve_chain"], 1)
                dve.wait_ge(S["dve_chain"], k_[0])

            def rsqrt(lo, hi):
                sq_, root_, out, tmp = (stat[:, i, lo:hi] for i in range(4))
                link(v.reciprocal(out, root_))
                link(v.tensor_tensor(tmp, out, out, ALU.mult))
                link(v.tensor_tensor(tmp, tmp, sq_, ALU.mult))
                link(v.tensor_scalar(tmp, tmp, -0.5, 1.5, ALU.mult, ALU.add))
                link(v.tensor_tensor(out, out, tmp, ALU.mult))

            dve.wait_ge(S["sigmoid_c"], 1)
            v.tensor_tensor(cT[:], cT[:], sigc[:], ALU.mult).then_inc(S["silu"], 1)
            dve.wait_ge(S["adaT_mm"], 24)
            link(v.tensor_tensor(mod[:], ps[:, 2, 0:48 * (1 + NS)].rearrange("p (k n) -> p k n", k=48),
                                 bada[:].unsqueeze(2).broadcast_to([P, 48, 1 + NS]), ALU.add))
            for sc, gg, kk in ((scale1, gmix, 1), (scale2, gffn, 4)):
                last = v.scalar_tensor_tensor(out=sc[:], in0=mod[:, kk * KC:(kk + 1) * KC, :], scalar=1.0,
                                              in1=gg[:].unsqueeze(2).broadcast_to([P, KC, 1 + NS]),
                                              op0=ALU.add, op1=ALU.mult)
            last.then_inc(S["mod_done"], 1)
            dve.wait_ge(S["mod_done"], 1)

            def front(g):
                s, tg, ng, nb = g.S, g.tg, g.ng, g.nb
                lo, hi = g.blocks[0], g.blocks[-1] + 1
                if g.n == 2:
                    yield from gap(4)

                def norm(turn):
                    scale, shift = ((scale1, 0), (scale2, 3))[turn]

                    def scaled(i):
                        w = width(g.blocks[i])
                        if i >= 2:
                            dve.wait_ge(s["xT_mm"], turn * nb + i - 1)
                        x = g.xn if g.n == 1 or turn == 1 else x_first
                        v.tensor_scalar(xs[0:w, i % 2, :], x[0:w, i, :], stat[0:w, 2, lo + i:lo + i + 1], None, ALU.mult
                                        ).then_inc(s["xs_ready"], 1)

                    yield from gap(nb - 1)
                    dve.wait_ge(s["sum_sq"], (turn + 1) * nb)
                    v.tensor_scalar(stat[:, 0, lo:hi], stat[:, 0, lo:hi], 1.0 / D, EPS, ALU.mult, ALU.add
                                    ).then_inc(s["mean_sq"], 1)
                    yield from gap(3)
                    dve.wait_ge(s["root"], turn + 1)
                    rsqrt(lo, hi)
                    yield
                    scaled(0)
                    scaled(1)
                    yield from gap(4)
                    for i, b in enumerate(g.blocks):
                        dve.wait_ge(s["xT_mm"], turn * nb + i + 1)
                        src = bank2(pair(i))
                        if b < NB:
                            for c in range(KC):
                                last = v.tensor_scalar(nT[:, c, cols(b)], src[:, c * P:(c + 1) * P],
                                                       scale[:, c, 0:1], mod[:, shift * KC + c, 0:1], ALU.mult, ALU.add)
                        else:
                            src = src.rearrange("p (c t) -> p c t", c=KC)[:, :, 0:NS]
                            link(v.tensor_tensor(nT[:, :, cols(b)], src, scale[:, :, 1:1 + NS], ALU.mult))
                            last = v.tensor_tensor(nT[:, :, cols(b)], nT[:, :, cols(b)],
                                                   mod[:, shift * KC:(shift + 1) * KC, 1:1 + NS], ALU.add)
                        last.then_inc(s["nT_done"], 1)
                        yield
                        if i + 2 < nb:
                            scaled(i + 2)
                        yield

                yield from norm(0)
                yield from gap(5)
                dve.wait_ge(S["small_in"], SMALL_IN)
                if g.n == 1:
                    v.memset(aT[:, :, 0:W - 1], 0.0)
                else:
                    v.tensor_copy(aT[:, :, 0:W - 1], hist[:])
                for i in range(CC * ng):
                    c, gi = i // ng, i % ng
                    yield from gap(3)
                    dve.wait_ge(s["sig_a"], i + 1)
                    dve.wait_ge(s["lin_mm"], i + 1)
                    lin = ps[:, pair(i) + 1, :]
                    w = min(tg, g.np - gi * tg)
                    last = v.tensor_tensor(aT[:, c, W - 1 + gi * tg:W - 1 + gi * tg + w], lin[:, 0:w], sig[:, i % 2, 0:w],
                                           ALU.mult)
                    if w < tg:
                        last = v.tensor_tensor(full_s[:, c, :, W - 1:W], lin[:, w:tg].unsqueeze(2),
                                               sig[:, i % 2, w:tg].unsqueeze(2), ALU.mult)
                    last.then_inc(s["a_done"], 1)
                    yield
                dve.wait_ge(s["a_done"], CC * ng)
                if g.n == 1:
                    v.tensor_copy(hist[:], aT[:, :, 512:512 + W - 1]).then_inc(S["hist_kept"], 1)
                else:
                    link(v.tensor_tensor(conv_s, full_s[:], wdw[:].unsqueeze(2).broadcast_to([P, CC, NS, W]), ALU.mult))
                    link(v.tensor_reduce(yT[:, :, 512:GW], conv_s, AX.X, ALU.add))
                    v.tensor_tensor(yT[:, :, 512:GW], yT[:, :, 512:GW], cvec[:, 0, :].unsqueeze(2).broadcast_to([P, CC, NS]),
                                    ALU.add).then_inc(s["conv"], 1)
                before = 1 if g.n == 2 else 0
                taps = [0]

                def conv(count):
                    for n in range(taps[0], min(taps[0] + count, CC * W)):
                        kk, c = n // CC, n % CC
                        y = yT[:, c, 0:512]
                        if kk == 0:
                            ins = v.tensor_scalar(y, aT[:, c, 0:512], wdw[:, c, 0:1], cvec[:, 0, c:c + 1], ALU.mult, ALU.add)
                        else:
                            dve.wait_ge(s["conv"], before + n - CC + 1)
                            ins = v.scalar_tensor_tensor(out=y, in0=aT[:, c, kk:kk + 512], scalar=wdw[:, c, kk:kk + 1],
                                                         in1=y, op0=ALU.mult, op1=ALU.add)
                        ins.then_inc(s["conv"], 1)
                        taps[0] += 1

                def conv_gap(n):
                    for _ in range(n):
                        conv(taps_per_step[g.n])
                        yield

                yield from gap(5)
                yield from conv_gap(2 * CC * ng)
                yield from gap(5)
                for i in range(nb + 2):
                    yield from conv_gap(1) if i < nb else gap(1)
                    if i >= 2:
                        b, j = g.blocks[i - 2], i - 2
                        w = width(b)
                        dve.wait_ge(s["v_root"], j + 1)
                        link(v.reciprocal(vroot[0:w, b:b + 1], vroot[0:w, b:b + 1]))
                        link(v.scalar_tensor_tensor(out=v_tm[0:w, j, :], in0=ps[0:w, 2 + j % 6, :], scalar=mv[0:w, b, 0:1],
                                                    in1=rowv[0:w, 0, :], op0=ALU.subtract, op1=ALU.mult))
                        v.scalar_tensor_tensor(out=v_tm[0:w, j, :], in0=v_tm[0:w, j, :], scalar=vroot[0:w, b:b + 1],
                                               in1=rowv[0:w, 1, :], op0=ALU.mult, op1=ALU.add).then_inc(s["v_done"], 1)
                    yield
                    yield from conv_gap(1) if i < nb else gap(1)
                    if i < nb:
                        w = width(g.blocks[i])
                        dve.wait_ge(s["v_mm"], i + 1)
                        link(v.bn_stats(bnst[0:w, i % 2, :], ps[0:w, 2 + i % 6, :]))
                        v.bn_aggr(mv[0:w, g.blocks[i], :], bnst[0:w, i % 2, :]).then_inc(s["v_stat"], 1)
                    yield
                yield from gap(4)
                dve.wait_ge(s["u_done"], CC * ng)
                for i, b in enumerate(g.blocks):
                    yield from conv_gap(1)
                    dve.wait_ge(s["sg_mm"], i + 1)
                    if i >= 1:
                        dve.wait_ge(s["sg_done"], i)
                    if b < NB:
                        sg = bank2(pair(i)).rearrange("p (c n) -> p c n", c=CC)
                        for hh in range(2):
                            at = slice(HD * hh, HD * hh + HD)
                            last = v.tensor_tensor(sgt[at, :, :], sg[at, :, P * hh:P * hh + P], bs[at, :, :], ALU.add)
                        link(last)
                        v.tensor_tensor(uT[:, :, cols(b)], uT[:, :, cols(b)], sgt, ALU.mult).then_inc(s["sg_done"], 1)
                    else:
                        vs = ps[:, pair(i), 0:CC * NS].rearrange("p (c s) -> p c s", c=CC)
                        link(v.tensor_tensor(sgt[:, :, 0:NS], vs, w00[:].unsqueeze(2).broadcast_to([P, CC, NS]), ALU.mult))
                        link(v.tensor_tensor(sgt[:, :, 0:NS], sgt[:, :, 0:NS], bs[:, :, 0:1].broadcast_to([P, CC, NS]), ALU.add))
                        v.tensor_tensor(uT[:, :, cols(b)], uT[:, :, cols(b)], sgt[:, :, 0:NS], ALU.mult
                                        ).then_inc(s["sg_done"], 1)
                    yield from conv_gap(1)
                yield from gap(5)
                if g.n == 2:
                    dve.wait_ge(S["routes1"], G1.nb)
                    dve.wait_ge(S["wo_mm1"], 4 * G1.nb)
                for i in range(KC * ng):
                    j, gi = i // ng, i % ng
                    yield from conv_gap(2)
                    dve.wait_ge(s["sig_b"], i + 1)
                    dve.wait_ge(s["ob_mm"], i + 1)
                    v.tensor_tensor(mT[:, j, gi * tg:(gi + 1) * tg], ps[:, pair(i) + 1, 0:tg], sig[:, i % 2, 0:tg], ALU.mult
                                    ).then_inc(s["mb_done"], 1)
                    yield from conv_gap(1)
                conv(CC * W)
                yield from gap(5)
                yield from gap(ng - 1)
                dve.wait_ge(s["mean_mm"], ng)
                for gi in range(ng):
                    y = yT[:, :, gi * tg:(gi + 1) * tg]
                    last = v.tensor_tensor(y, y, ps[:, 2 + gi, 0:tg].unsqueeze(1).broadcast_to([P, CC, tg]), ALU.subtract)
                last.then_inc(s["yc"], 1)
                yield from gap(ng + 6)
                dve.wait_ge(s["std_act"], ng)
                link(v.reciprocal(rbc[:, 0:g.nt], rbc[:, 0:g.nt]))
                dve.wait_ge(s["sq_act"], ng)
                v.tensor_tensor(yT[:, :, 0:g.nt], yT[:, :, 0:g.nt], rbc[:, 0:g.nt].unsqueeze(1).broadcast_to([P, CC, g.nt]),
                                ALU.mult).then_inc(s["yn_done"], 1)
                yield from gap(4)
                for c in range(CC):
                    dve.wait_ge(s["sig_y"], c + 1)
                    y = yT[:, c, 0:g.nt]
                    link(v.tensor_scalar(y, y, cvec[:, 1, c:c + 1], cvec[:, 2, c:c + 1], ALU.mult, ALU.add))
                    v.tensor_tensor(y, y, ysq[:, c, 0:g.nt], ALU.mult).then_inc(s["y_done"], 1)
                    yield
                yield from gap(4)

                chain_at = []

                def add_m(i):
                    j, gi = i // ng, i % ng
                    m = mT[:, j, gi * tg:(gi + 1) * tg]
                    dve.wait_ge(S["dve_chain"], chain_at[i])
                    v.tensor_tensor(m, m, prod[:, i % 2, 0:tg], ALU.add).then_inc(s["m_done"], 1)

                for i in range(KC * ng):
                    yield from gap(2)
                    dve.wait_ge(s["sig_g"], i + 1)
                    dve.wait_ge(s["oa_mm"], i + 1)
                    if i >= 2:
                        dve.wait_ge(s["m_done"], i - 1)
                    k_[0] += 1
                    chain_at.append(k_[0])
                    v.tensor_tensor(prod[:, i % 2, 0:tg], ps[:, pair(i) + 1, 0:tg], sig[:, i % 2, 0:tg], ALU.mult
                                    ).then_inc(S["dve_chain"], 1)
                    add_m(i)
                    yield
                yield from gap(5)
                yield from gap(2)
                dve.wait_ge(s["gt_done"], 1)
                if g.n == 2:
                    dve.wait_ge(S["x_again"], 16 * nb)
                for i in range(4 * nb):
                    col, b = i // nb, g.blocks[i % nb]
                    w = width(b)
                    at = slice(256 * col, 256 * (col + 1))
                    yield
                    dve.wait_ge(s["wo_mm"], i + 1)
                    if i >= 2:
                        dve.wait_ge(s["x1_done"], i - 1)
                    gt_ = g.gt1[:, at] if b < NB else gts[:, at]
                    x = g.xn[0:w, i % nb, at]
                    link(v.tensor_tensor(xs[0:w, i % 2, 0:256], ps[0:w, 2 + i % 6, 0:256], gt_, ALU.mult))
                    v.tensor_tensor(x, x, xs[0:w, i % 2, 0:256], ALU.add).then_inc(s["x1_done"], 1)
                    yield
                yield from gap(3)
                dve.wait_ge(s["x1_done"], 4 * nb)
                yield from norm(1)
                yield from gap(5)
                yield from gap(2 * nb + 3)
                if g.n == 2:
                    dve.wait_ge(S["out_hist"], 16 * (1 + CC))
                    v.memset(v16[:, 4, :, :], 0.0)
                    link(v.memset(i16[:, 4, :, :], 0))

                def top16(scores, out, w, reps):
                    def at(x, o, half):
                        return x[0:w, o[0], o[1], 8 * half:8 * half + 8]
                    for sc, o in zip(scores, out):
                        last = v.max(at(v16, o, 0), sc)
                    link(last)
                    yield
                    for n, (sc, o) in enumerate(zip(scores, out)):
                        last = v.match_replace(reps[0:w, n, :], at(v16, o, 0), sc, LOW)
                    link(last)
                    yield
                    for n, (sc, o) in enumerate(zip(scores, out)):
                        v.max_index(at(i16, o, 0), at(v16, o, 0), sc)
                        last = v.max(at(v16, o, 1), reps[0:w, n, :])
                    link(last)
                    yield
                    for n, o in enumerate(out):
                        last = v.max_index(at(i16, o, 1), at(v16, o, 1), reps[0:w, n, :])
                    last.then_inc(s["s_done"], 1)
                    yield

                for ch in range(NCH + 3):
                    if ch >= 3:
                        k = ch - 3
                        dve.wait_ge(s["s_mm"], k + 1)
                        if k >= 1:
                            dve.wait_ge(s["s_done"], k)
                        yield from top16([ps[:, 6 + k % 2, i * P:(i + 1) * P] for i in range(4)],
                                         [(i, k) for i in range(4)], P, rep)
                    else:
                        yield from gap(2 * ng)
                    yield
                yield from gap(4)
                if g.n == 2:
                    dve.wait_ge(S["qs_mm"], 1)
                    for c in range(4):
                        dve.wait_ge(s["s_done"], NCH + c)
                        yield from top16([ps[0:NS, 2 + c, i * P:(i + 1) * P] for i in range(4)],
                                         [(4, 4 * c + i) for i in range(4)], NS, rep_s)
                    dve.wait_ge(s["s_done"], NCH + 4)
                dve.wait_ge(s["s_done"], NCH)
                dve.wait_ge(s["s_mm"], NCH)
                if g.n == 2:
                    dve.wait_ge(s["q_mm"], NCH * ng)
                link(v.tensor_copy(i16f[:, 0:nb, :, :], i16[:, 0:nb, :, :]))
                vv = v16[:, 0:nb, :, :].rearrange("p b (h f) k -> p (b h) f k", f=2)
                ii = i16f[:, 0:nb, :, :].rearrange("p b (h f) k -> p (b h) f k", f=2)
                at = 0
                for a in range(9):
                    n_ = ROWS[a] if a < 8 else 8

                    def first(x):
                        return x[:, :, 0, a:a + 1].broadcast_to([P, nb * H, n_]) if a < 8 else x[:, :, 0, 8:16]

                    def second(x):
                        return x[:, :, 1, 0:n_] if a < 8 else x[:, :, 1, 0:1].broadcast_to([P, nb * H, n_])

                    v.tensor_tensor(g.cand[:, :, at:at + n_], first(vv), second(vv), ALU.add)
                    last = v.scalar_tensor_tensor(out=g.cid[:, :, at:at + n_], in0=first(ii), scalar=float(NKEY),
                                                  in1=second(ii), op0=ALU.mult, op1=ALU.add)
                    at += n_
                    if a == 8:
                        last.then_inc(s["tables"], 1)
                        dve.wait_ge(s["tables"], 1)
                    yield
                yield from route(g, 0)
                yield

            def route(g, i):
                s, b = g.S, g.blocks[i]
                best = gate[:, b, :].rearrange("p (h k) -> p h k", k=TOP)
                pos = g.posf.bitcast(u32)
                hs = range(H)
                for h in hs:
                    last = v.max(best[:, h, 0:8], g.cand[:, i * H + h, :])
                link(last)
                yield
                for h in hs:
                    last = v.match_replace(g.crep[:, h, :], best[:, h, 0:8], g.cand[:, i * H + h, :], LOW)
                link(last)
                yield
                for h in hs:
                    v.max_index(pos[:, i * H + h, 0:8], best[:, h, 0:8], g.cand[:, i * H + h, :])
                    last = v.max(best[:, h, 8:16], g.crep[:, h, :])
                link(last)
                yield
                for h in hs:
                    last = v.max_index(pos[:, i * H + h, 8:16], best[:, h, 8:16], g.crep[:, h, :])
                link(last)
                link(v.tensor_copy(g.posf[:, i * H:(i + 1) * H, :], pos[:, i * H:(i + 1) * H, :]))
                link(v.tensor_copy(smx[:, 0:H], best[:, :, 0]))
                v.tensor_tensor(best, best, smx[:, 0:H].unsqueeze(2).broadcast_to([P, H, TOP]), ALU.subtract
                                ).then_inc(s["sm_diff"], 1)
                yield
                for hp in range(4):
                    p_ = g.posf[:, i * H + 2 * hp:i * H + 2 * hp + 2, :]
                    c_ = g.cid[:, i * H + 2 * hp:i * H + 2 * hp + 2, :]
                    link(v.tensor_tensor(g.eq.rearrange("p h k n -> p (h k) n"),
                                         p_.rearrange("p h k -> p (h k)").unsqueeze(2).broadcast_to([P, 2 * TOP, NC]),
                                         iota[:].unsqueeze(1).broadcast_to([P, 2 * TOP, NC]), ALU.is_equal))
                    link(v.tensor_tensor(g.eq, g.eq, c_.unsqueeze(2).broadcast_to([P, 2, TOP, NC]), ALU.mult))
                    at = slice(2 * hp * TOP, (2 * hp + 2) * TOP)
                    link(v.tensor_reduce(eid_s[:, at].rearrange("p (h k) -> p h k", k=TOP), g.eq, AX.X, ALU.add))
                    if hp == 3:
                        link(v.tensor_copy(eid[:, b, :], eid_s[:]))
                    yield
                dve.wait_ge(s["sm_exp"], i + 1)
                link(v.tensor_reduce(smx[:, 0:H], best, AX.X, ALU.add))
                link(v.reciprocal(smx[:, 0:H], smx[:, 0:H]))
                yield
                v.tensor_tensor(best, best, smx[:, 0:H].unsqueeze(2).broadcast_to([P, H, TOP]), ALU.mult
                                ).then_inc(s["routes"], 1)
                dve.wait_ge(s["routes"], i + 1)
                yield

            for _ in front(G1):
                pass

            def dot(j, r, x, turn):
                dve.wait_ge(s_row[r], turn * 16 + 16)
                return v.scalar_tensor_tensor(out=rows[:, r, 0:D], in0=rows[:, r, 0:D], scalar=1.0, in1=x,
                                              op0=ALU.mult, op1=ALU.mult, accum_out=act[:, j:j + 1])

            def weight(j, gate_):
                return v.tensor_scalar(diag[:, j, :], ident[:], gel[:, j:j + 1], gate_, ALU.mult, ALU.mult)

            routing = (None for i in range(1, NB1) for _ in route(G1, i))

            def peer(tick):
                if tick < TICKS:
                    dot(tick % 4, tick % RB1, xn1[:, tick // NSLOT, :], tick // RB1).then_inc(S["dots"], 1)
                if tick >= 1:
                    n = tick - 1
                    b, slot = n // NSLOT, n % NSLOT
                    dve.wait_ge(S["gelu"], n + 1)
                    if n >= 4:
                        dve.wait_ge(S["rows_used"], n - 3)
                    weight(n % 4, gate[:, b, slot:slot + 1]).then_inc(S["weights"], 1)
                    if slot == NSLOT - 1:
                        dve.wait_ge(S["acc_done"], b + 1)
                        v.tensor_tensor(xn1[:, b, :], bank2(0), gt2[:], ALU.mult).then_inc(S["acc_read"], 1)
                if tick % 2 == 0:
                    next(routing, None)

            interleave(peer, front(G2))
            peer(TICKS)

            for bb in range(NB - NB1):
                b = NB1 + bb
                routing = route(G2, bb + 1)
                x = xn2[:, bb, :]

                def first_dots(q, turn):
                    for k in range(2):
                        r = (2 * q + k) % RB2
                        last = dot((2 * q + k) % 4, r, x, turn + fills[r])
                    last.then_inc(S["dots"], 1)

                def weigh(gr, q, slot):
                    dve.wait_ge(S["gelu"], gr + (TICKS + 1))
                    dve.wait_ge(S["rows_used"], gr + (TICKS - 1))
                    for k in range(2):
                        last = weight((2 * q + k) % 4, gate[:, b, bass.ds(slot + k, 1)])
                    last.then_inc(S["weights"], 1)

                first_dots(0, bb * 16)
                for q in range(1, 17):
                    first_dots(q, bb * 16 + q // 4)
                    weigh(bb * 64 + q - 1, q - 1, 2 * (q - 1))
                    next(routing, None)
                for _ in routing:
                    pass
                if bb + 1 == NB - NB1:
                    for r in range(4):
                        at = slice(32 * r, 32 * r + 32)
                        v.transpose(sT[at, 0, :], eid_s[0:32, at])
                        last = v.transpose(sT[at, 1, :], gate[0:32, NB, at])
                    link(last)
                    v.tensor_copy(gsT[:], sT[:, 1, 0:NS])
                    v.tensor_copy(idxs[:], sT[:, 0, 0:NS]).then_inc(S["idxs_ready"], 1)
                with dve.Fori(0, 5) as m:
                    for q in range(17, 25):
                        first_dots(q, m * 2 + (bb * 16 + q // 4))
                        weigh(m * 8 + (bb * 64 + q - 1), q - 1, m * 16 + 2 * (q - 1))
                for q in range(57, 64):
                    first_dots(q, bb * 16 + q // 4)
                    weigh(bb * 64 + q - 1, q - 1, 2 * (q - 1))
                weigh(bb * 64 + 63, 63, 126)
                dve.wait_ge(S["acc_done"], b + 1)
                v.tensor_tensor(x, bank2(0), gt2[:], ALU.mult).then_inc(S["acc_read"], 1)
            def sample_weight(k):
                dve.wait_ge(S["s_gelu"], k + 1)
                v.tensor_scalar(wmask[:, k, :], eye8[:, k, :], gel[:, k % 4:k % 4 + 1], gsT[:, k:k + 1],
                                ALU.mult, ALU.mult).then_inc(S["s_weights"], 1)

            for k in range(NS):
                dve.wait_ge(s_row[k], 16 * (fills[k] + (NB - NB1) * 16 + 1))
                dve.wait_ge(S["xb_mm"], k + 1)
                v.scalar_tensor_tensor(out=rows[:, k, 0:D], in0=rows[:, k, 0:D], scalar=1.0, in1=bank2(pair(k)),
                                       op0=ALU.mult, op1=ALU.mult, accum_out=act[:, k % 4:k % 4 + 1]
                                       ).then_inc(S["s_dots"], 1)
                if k >= 1:
                    sample_weight(k - 1)
            sample_weight(NS - 1)
            dve.wait_ge(S["x1_back"], 16 * NBT)
            dve.wait_ge(S["acc_read"], NB)
            for b in range(NB):
                xn = xn1[:, b, :] if b < NB1 else xn2[:, b - NB1, :]
                v.tensor_tensor(x1_again(b), x1_again(b), xn, ALU.add).then_inc(S["x2_done"], 1)
            dve.wait_ge(S["s_acc"], 1)
            link(v.tensor_tensor(xn2[0:NS, 4, :], bank2(0)[0:NS, :], gts, ALU.mult))
            v.tensor_tensor(x1_again(NB)[0:NS, :], x1_again(NB)[0:NS, :], xn2[0:NS, 4, :], ALU.add).then_inc(S["x2_done"], 1)
            dve.wait_ge(S["fin_sq"], NBT)
            v.tensor_scalar(stat[:, 0, :], stat[:, 0, :], 1.0 / D, EPS, ALU.mult, ALU.add).then_inc(S["fin_ms"], 1)
            dve.wait_ge(S["fin_root"], 1)
            rsqrt(0, NBT)
            dve.wait_ge(S["gfin_in"], 16)
            for b in range(NBT):
                w = width(b)
                v.scalar_tensor_tensor(out=x1_again(b)[0:w, :], in0=x1_again(b)[0:w, :], scalar=stat[0:w, 2, b:b + 1],
                                       in1=gfin[0:w, :], op0=ALU.mult, op1=ALU.mult).then_inc(S["y_ready"], 1)


def kernel(**inputs):
    import concourse.bacc as bacc
    from concourse.bass_utils import run_bass_kernel_spmd

    a = {k: np.asarray(v) for k, v in inputs.items()}

    def cm(v):
        return v.reshape(-1, P).T

    ins = {
        "x": np.concatenate([a["x_prompt"][0], a["x_sample"][:, 0]], 0),
        "cT": np.concatenate([a["c_prompt"], a["c_sample"]], 0).T.reshape(KC, P, 1 + NS).transpose(1, 0, 2),
        "bada": cm(a["b_ada"][0]),
        "gmix": cm(a["g_mix"][0]),
        "gffn": cm(a["g_ffn"][0]),
        "w_dw": a["w_dw"][0].T.reshape(CC, P, W).transpose(1, 0, 2),
        "cvec": np.stack([cm(a["b_dw"][0]), cm(a["g_cn"][0]), cm(a["b_cn"][0])], 1),
        "keys": np.stack([a["k1"][0].T, a["k2"][0].T], 1),
        "wsT": a["w_s"][0].transpose(2, 0, 1),
        "state_T": a["state_conv"][0].transpose(2, 0, 1).reshape(CC, P, NS, W - 1).transpose(1, 0, 2, 3),
        "b_s": a["b_s"][0],
        "w_s00": a["w_s"][0][:, 0, 0:1],
        "g_v": a["g_v"],
        "b_v": a["b_v"],
        "g_final": a["g_final"][None],
        "w_ada": a["w_ada"][0],
        "w_in": a["w_in"][0],
        "w_conv_out": a["w_conv_out"][0],
        "w_gmlp_out": a["w_gmlp_out"][0],
        "w_out": a["w_out"][0],
        "w_q": a["w_q"][0],
        "experts": np.concatenate([a["u_tab"][0], a["v_tab"][0]], 1),
    }
    scratch = {"x1_rows": (NT, D)}
    outs = {
        "out_y": (NT, D),
        "out_hist_p": (P, CC, W - 1),
        "out_hist_s": (P, CC, NS, W - 1),
        "out_v": (NS, DC),
    }
    nc = bacc.Bacc("TRN2", target_bir_lowering=False, num_devices=1)
    arrays, t = {}, {}
    for name, v in ins.items():
        v = np.ascontiguousarray(v)
        arrays[f"in_{name}"] = v
        t[name] = nc.dram_tensor(f"in_{name}", v.shape, mybir.dt.from_np(v.dtype), kind="ExternalInput").ap()
    for name, shape in outs.items():
        t[name] = nc.dram_tensor(name, shape, mybir.dt.float32, kind="ExternalOutput").ap()
    for name, shape in scratch.items():
        t[name] = nc.dram_tensor(name, shape, mybir.dt.float32, kind="Internal").ap()
    build(nc, t)
    got = run_bass_kernel_spmd(nc, [arrays], core_ids=[0]).results[0]
    y = got["out_y"]
    hist_p = got["out_hist_p"].transpose(2, 1, 0).reshape(1, 1, W - 1, DC)
    hist_s = got["out_hist_s"].transpose(2, 3, 1, 0).reshape(1, NS, W - 1, DC)
    return (y[:NP].reshape(1, NP, D), y[NP:].reshape(NS, 1, D), hist_p, hist_s, got["out_v"].reshape(1, NS, 1, DC))
```

```python
from contextlib import ExitStack

import numpy as np

import concourse.bass as bass
from concourse import mybir

D = 1024
NP = 1024
NS = 8
NT = NP + NS
P = 128
KC = D // P
DC = 512
CC = DC // P
W = 31
NB = NP // P
NBT = NB + 1
H = 8
HD = 64
NCH = 2 * H
TOP = 16
NKEY = 128
EPS = 1e-6
ROWS = [16, 8, 5, 4, 3, 2, 2, 2] + [1] * 8
NC = sum(ROWS)
LOW = -3.0e38
NSLOT = H * TOP
RING = 3
PIECE = 2048
NB1 = 4
GW = 520
RB1, RB2 = 6, 8
TICKS = NB1 * NSLOT
HEAVY = 3
FRONT_TICKS = 500
S_GROUPS = NS // 2
EARLY = 25
ROUTE_PIECES = 10
ROUTE_EXP = [2 * (ROUTE_PIECES * i + 6) for i in range(NB1 - 1)]


class Group:
    pass


def gap(n):
    for _ in range(n):
        yield


def build(nc, t):
    f32, u32 = mybir.dt.float32, mybir.dt.uint32
    ALU, ACT, AX = mybir.AluOpType, mybir.ActivationFunctionType, mybir.AxisListType
    ctx = ExitStack()
    with ctx:
        def sb(name, shape, dt=f32):
            return ctx.enter_context(nc.sbuf_tensor(name, shape, dt))

        def part(area, at, *shape):
            names = "abc"[:len(shape)]
            spec = "p (%s) -> p %s" % (" ".join(names), " ".join(names))
            return area[:, at:at + int(np.prod(shape))].rearrange(spec, **dict(zip(names, shape)))

        big = sb("big", [P, RB1 * 2 * D + KC * GW])
        rows = part(big, 0, RB2, 2 * D)
        nT = part(big, RB1 * 2 * D, KC, GW)
        mod_rows = big[0:1 + NS, 0:6 * D]
        gt1_a = big[:, 6 * D:7 * D]
        sq_a = part(big, 7 * D, NB1, D)
        mbuf = sb("mbuf", [P, KC * GW])
        mT = part(mbuf, 0, KC, GW)
        wring = sb("wring", [P, RING * PIECE])
        AW = 512 + W - 1
        arena = sb("arena", [P, CC * (AW + 2 * GW) + 5 * DC])
        aT = part(arena, 0, CC, AW)
        yT = part(arena, CC * AW, CC, GW)
        v_tm = part(arena, CC * (AW + GW), 5, DC)
        uT = part(arena, CC * (AW + GW) + 5 * DC, CC, GW)
        ysq = part(arena, CC * (AW + GW), CC, GW)
        x_first = part(arena, CC * AW, 5, D)
        eq = part(arena, CC * AW + 5 * D, 2, TOP, NC)
        xn2 = part(arena, 3768, 5, D)
        xn1 = sb("xn1", [P, NB1, D])
        v16 = part(arena, 0, 5, NCH, TOP)
        i16f = part(arena, 5 * NCH * TOP, 5, NCH, TOP)
        i16 = i16f.bitcast(u32)
        rep = part(arena, 10 * NCH * TOP, 4, NKEY)
        w1 = sb("w1", [P, 3600])
        sig, prod = part(w1, 0, 2, 512), part(w1, 1024, 2, 512)
        conv_s = w1[:, 2048:2048 + CC * NS * W].rearrange("p (c s k) -> p c s k", c=CC, s=NS)
        sgt = part(w1, 1024, CC, P)
        rbc = w1[:, 3072:3072 + GW]
        xs = part(w1, 0, 2, D)
        qbuf = part(w1, 0, 2, GW)
        qs = part(w1, 2 * GW, NCH, NS)
        rep_s = part(w1, 2 * GW + NCH * NS, 4, NKEY)
        gts = w1[0:NS, 2 * D:3 * D]
        w2 = sb("w2", [P, H * P + CC * P + 2 * DC])
        wsT = part(w2, 0, H, P)
        bs = part(w2, H * P, CC, P)
        rowv = part(w2, H * P + CC * P, 2, DC)
        gt1_b = w2[:, 0:D]
        full_s = sb("full_s", [P, CC, NS, W])
        hist = sb("hist", [P, CC, W - 1])
        eid = sb("eid", [P, NBT, NSLOT], u32)
        eid_s = sb("eid_s", [P, NSLOT])
        gate = sb("gate", [P, NBT, NSLOT])
        diag = sb("diag", [P, 4, P])
        gt2 = sb("gt2", [P, D])
        ident = sb("ident", [P, P])
        zero = sb("zero", [P, P])
        onesm = sb("onesm", [P, P])
        eye8 = sb("eye8", [P, NS, NS])
        iota = sb("iota", [P, NC])
        cT = sb("cT", [P, KC, 1 + NS])
        sigc = sb("sigc", [P, KC, 1 + NS])
        bada = sb("bada", [P, 48])
        gmix = sb("gmix", [P, KC])
        gffn = sb("gffn", [P, KC])
        mod = sb("mod", [P, 48, 1 + NS])
        scale1 = sb("scale1", [P, KC, 1 + NS])
        scale2 = sb("scale2", [P, KC, 1 + NS])
        wdw = sb("wdw", [P, CC, W])
        cvec = sb("cvec", [P, 3, CC])
        w00 = sb("w00", [P, CC])
        keys = sb("keys", [P, 2, NKEY])
        stat = sb("stat", [P, 4, NBT])
        bnst = sb("bnst", [P, 2, 6])
        mv = sb("mv", [P, NBT, 2])
        vroot = sb("vroot", [P, NBT])
        eps = sb("eps", [P, 1])
        smx = sb("smx", [P, 5 * H])
        act = sb("act", [P, 4])
        gel = sb("gel", [P, 4])
        idx = sb("idx", [P, 16], u32)
        idxs = sb("idxs", [P, NS], u32)
        gsT = sb("gsT", [P, NS])
        sT = sb("sT", [P, 2, 32])
        wmask = sb("wmask", [P, NS, NS])

        ps = ctx.enter_context(nc.psum_tensor("ps", [P, 8, 512], f32))

        def bank2(b):
            return ps[:, b:b + 2, :].rearrange("p b n -> p (b n)")

        def pair(i):
            return 2 + 2 * (i % 3)

        group_names = """x_in sum_sq mean_sq root xs_ready xT_mm nT_done gate_mm lin_mm sig_a a_done
            u_mm u_done v_mm v_stat v_root v_done sg_mm sg_done conv gb_mm ob_mm sig_b mb_done mean_mm yc sq_act
            var_mm std_act yn_done sig_y y_done ga_mm oa_mm sig_g m_done wo_mm x1_done gt_mm gt_done t2b_mm n2_done
            q_mm q_done s_mm s_done sm_diff sm_exp routes tables out_x1""".split()
        S = {f"{n}{g}": ctx.enter_context(nc.semaphore(f"{n}{g}")) for n in group_names for g in (1, 2)}
        for n in """c_in small_in gfin_in consts masked sigmoid_c silu ada_mm ada_row adaT_mm mod_done
                dve_chain pool_chain dots gelu weights rows_used acc_done acc_read hist_kept x_again first_ids
                xb_mm s_dots s_gelu s_weights idx_ready idxs_ready qs_mm
                x1_back x2_done fin_sq fin_ms fin_root y_ready out_y out_hist out_v""".split():
            S[n] = ctx.enter_context(nc.semaphore(n))
        s_piece = [ctx.enter_context(nc.semaphore(f"piece{i}")) for i in range(RING)]
        s_row = [ctx.enter_context(nc.semaphore(f"rows{i}")) for i in range(RB2)]
        fills = [len(range(r, TICKS, RB1)) if r < RB1 else 0 for r in range(RB2)]

        def buffer2(n):
            return (n + TICKS % RB1) % RB2

        def width(b):
            return P if b < NB else NS

        def group(n, blocks, tg, xn, tables):
            g = Group()
            g.n, g.blocks, g.nb, g.tg, g.xn = n, blocks, len(blocks), tg, xn
            g.nt = sum(width(b) for b in blocks)
            g.ng = g.nt // tg
            g.np = 4 * P
            g.S = {k: S[f"{k}{n}"] for k in group_names}
            g.order = list(range(g.nb)) if n == 1 else [0, 1, 2, 4, 3]
            g.cand = part(tables, 0, g.nb * H, NC)
            g.cid = part(tables, g.nb * H * NC, g.nb * H, NC)
            g.posf = part(mbuf, 3200, g.nb * H, TOP) if n == 1 else part(mbuf, 0, g.nb * H, TOP)
            g.crep = part(mbuf, 3200 + 512, H, NC) if n == 1 else part(mbuf, 1024, H, NC)
            g.eq = eq if n == 1 else part(mbuf, 2048, 2, TOP, NC)
            g.sq = sq_a if n == 1 else None
            g.gt1 = gt1_a if n == 1 else gt1_b
            return g

        G1 = group(1, list(range(NB1)), 512, xn1, mbuf)
        G2 = group(2, list(range(NB1, NBT)), 260, xn2, wring)

        def cols(b):
            i = b % 4 if b < NB else 4
            return slice(i * P, i * P + width(b))

        def local(b):
            return b if b < NB1 else b - NB1

        w_in, pieces, first_piece = t["w_in"], [], {}
        ada_piece = []

        def ada_pieces(lo, hi):
            for i in range(lo, hi):
                ada_piece.append(len(pieces))
                pieces.append(("ada", t["w_ada"], i, S["ada_mm"], i + 1))

        ada_pieces(0, 8)
        for g in (G1, G2):
            ng = g.ng
            first_piece[g.n] = len(pieces)
            for half in range(2):
                pieces.append(("in", w_in, 2 + half, g.S["lin_mm"], 2 * ng * (half + 1)))
                pieces.append(("in", w_in, half, g.S["lin_mm"], 2 * ng * (half + 1)))
            for half in range(2):
                pieces.append(("in", w_in, 4 + half, g.S["u_mm"], 2 * ng * (half + 1)))
            for half in range(2):
                pieces.append(("in", w_in, 6 + half, g.S["v_mm"], g.nb))
            if g.n == 1:
                ada_pieces(8, 16)
            for base, wout, done in ((12, t["w_gmlp_out"], "ob_mm"), (8, t["w_conv_out"], "oa_mm")):
                for col in range(4):
                    if col % 2 == 0:
                        pieces.append(("out", wout, col // 2, g.S[done], 2 * ng * (col + 2)))
                    pieces.append(("in", w_in, base + col, g.S[done], 2 * ng * (col + 1)))
                if g.n == 1 and base == 12:
                    ada_pieces(16, 24)
            for i in range(4):
                pieces.append(("wo", t["w_out"], i, g.S["wo_mm"], g.nb * (i + 1)))
            for i in range(8):
                pieces.append(("wq", t["w_q"], i, g.S["q_mm"], 2 * ng * (i + 1)))

        def piece(n):
            k = CC if pieces[n][0] == "out" else KC
            return wring[:, (n % RING) * PIECE:(n % RING + 1) * PIECE].rearrange("p (k n) -> p k n", k=k)

        def norm_steps(g):
            yield from [1] * (g.nb + 7)
            yield from [2] * (2 * g.nb)

        def front_weights(g):
            for work, idle in ((4 * CC * g.ng, 5), (2 * CC * g.ng, 5), (4 * g.nb, 12), (2 * g.nb, 5),
                               (3 * KC * g.ng, 5), (2 * g.ng, 17), (3 * KC * g.ng, 7), (8 * g.nb, 3)):
                if work == 4 * CC * g.ng:
                    yield from norm_steps(g)
                    yield from [1] * 5
                yield from [HEAVY] * work
                yield from [1] * idle
            yield from norm_steps(g)
            yield from [1] * 5
            yield from [HEAVY] * (2 * g.nb)
            yield from [1] * 3
            yield from [HEAVY] * (NCH * (2 * g.ng + 1))
            yield from [1] * (2 * g.ng + 1) * 3
            yield from [1] * 4 + [2] * 36

        def interleave(peer, front):
            weights = list(front_weights(G2))
            total, spent, at = sum(weights), 0, 0
            for tick in range(TICKS):
                peer(tick)
                while at < len(weights) and spent < total * (tick + 1) / FRONT_TICKS:
                    spent += weights[at]
                    at += 1
                    next(front, None)
            for _ in front:
                pass

        taps_per_step = {g.n: -(-CC * W // (2 * CC * g.ng + (4 * g.nb if g.n == 2 else 0) + 3 * KC * g.ng))
                         for g in (G1, G2)}

        def x1_again(b):
            return mbuf[:, b * D:(b + 1) * D] if b < NB1 else wring[:, (b - NB1) * D:(b - NB1 + 1) * D]

        gfin = wring[:, 5 * D:6 * D]
        finals = list(range(NB - 1)) + [NB, NB - 1]
        SMALL_IN = 16 * (4 + CC + 2 * H + 2)

        block = ctx.enter_context(nc.Block())

        @block.sync
        def _(sp):
            for name, dst in (("cT", cT), ("bada", bada), ("gmix", gmix), ("gffn", gffn)):
                sp.dma_start(dst[:], t[name]).then_inc(S["c_in"], 16)
            for b in G1.blocks:
                sp.dma_start(xn1[:, b, :], t["x"][b * P:(b + 1) * P, :]).then_inc(S["x_in1"], 16)

            def load(n):
                kind, src, col, _, _ = pieces[n]
                if n >= RING:
                    done, count = pieces[n - RING][3:]
                    sp.wait_ge(done, count)
                w = 512 if kind == "out" else 256
                sp.dma_start(piece(n), src[:, col * w:(col + 1) * w].rearrange("(k p) n -> p k n", p=P)
                             ).then_inc(s_piece[n % RING], 16)

            for n in range(8):
                load(n)
            sp.dma_start(wdw[:], t["w_dw"]).then_inc(S["small_in"], 16)
            sp.dma_start(cvec[:], t["cvec"]).then_inc(S["small_in"], 16)
            sp.dma_start(keys[:], t["keys"]).then_inc(S["small_in"], 16)
            sp.dma_start(wsT, t["wsT"]).then_inc(S["small_in"], 16)
            for c in range(CC):
                sp.dma_start(full_s[:, c, :, 0:W - 1], t["state_T"][:, c, :, :]).then_inc(S["small_in"], 16)
            for h in range(H):
                at = slice(HD * (h % 2), HD * (h % 2) + HD)
                sp.dma_start(bs[at, h // 2, :], t["b_s"][h:h + 1, :].broadcast_to([HD, P])).then_inc(S["small_in"], 16)
                sp.dma_start(w00[at, h // 2:h // 2 + 1], t["w_s00"][h:h + 1, :].broadcast_to([HD, 1])
                             ).then_inc(S["small_in"], 16)
            for i, name in enumerate(("g_v", "b_v")):
                sp.dma_start(rowv[:, i, :], t[name].broadcast_to([P, DC])).then_inc(S["small_in"], 16)

            def spill(g):
                sp.wait_ge(g.S["x1_done"], 4 * g.nb)
                for b in g.blocks:
                    w = width(b)
                    sp.dma_start(t["x1_rows"][b * P:b * P + w, :], g.xn[0:w, local(b), :]).then_inc(g.S["out_x1"], 16)

            for n in range(8, first_piece[2]):
                load(n)
                if pieces[n][0] == "wq" and pieces[n - 1][0] == "wo":
                    spill(G1)
            sp.wait_ge(S["oa_mm1"], KC * G1.ng)
            sp.wait_ge(S["s_done1"], NCH)
            sp.wait_ge(S["sq_act1"], 1)
            sp.wait_ge(S["tables1"], 1)
            for b in G2.blocks:
                w = width(b)
                sp.dma_start(x_first[0:w, local(b), :], t["x"][b * P:b * P + w, :]).then_inc(S["x_in2"], 16)
            first_wo = max(n for n, p in enumerate(pieces) if p[0] == "wo") - 3
            for n in range(first_piece[2], len(pieces)):
                if n == first_piece[2] + 11:
                    sp.wait_ge(S["a_done2"], CC * G2.ng)
                    sp.dma_start(t["out_hist_p"], aT[:, :, AW - W + 1:AW]).then_inc(S["out_hist"], 16)
                    for c in range(CC):
                        sp.dma_start(t["out_hist_s"][:, c, :, :], full_s[:, c, :, 1:W]).then_inc(S["out_hist"], 16)
                    sp.wait_ge(S["v_done2"], G2.nb)
                    sp.dma_start(t["out_v"], v_tm[0:NS, 4, :]).then_inc(S["out_v"], 16)
                if n == first_wo + 2:
                    sp.wait_ge(S["oa_mm2"], KC * G2.ng)
                    sp.wait_ge(S["out_v"], 16)
                    for b in G2.blocks:
                        w = width(b)
                        sp.dma_start(xn2[0:w, local(b), :], t["x"][b * P:b * P + w, :]).then_inc(S["x_again"], 16)
                if pieces[n][0] == "wq" and pieces[n - 1][0] == "wo":
                    load(n)
                    spill(G2)
                    continue
                load(n)
            sp.wait_ge(S["out_hist"], 16 * (1 + CC))
            sp.wait_ge(S["routes2"], G2.nb)
            for g, area in ((G1, None), (G2, None)):
                sp.wait_ge(g.S["out_x1"], 16 * g.nb)
            for b in range(NBT):
                w = width(b)
                sp.dma_start(x1_again(b)[0:w, :], t["x1_rows"][b * P:b * P + w, :]).then_inc(S["x1_back"], 16)
            sp.dma_start(gfin, t["g_final"].broadcast_to([P, D])).then_inc(S["gfin_in"], 16)
            for n, b in enumerate(finals):
                w = width(b)
                sp.wait_ge(S["y_ready"], n + 1)
                sp.dma_start(t["out_y"][b * P:b * P + w, :], x1_again(b)[0:w, :]).then_inc(S["out_y"], 16)
            sp.wait_ge(S["out_y"], 16 * NBT)

        @block.tensor
        def _(pe):
            mmul = nc.tensor.matmul

            def arrived(n):
                pe.wait_ge(s_piece[n % RING], 16 * (n // RING + 1))

            def ada_turn(n):
                pe.wait_ge(S["ada_row"], n + 1)
                for j in range(2):
                    at = (2 * n + j) * (1 + NS)
                    mm = nc.tensor.transpose(ps[:, 1, at:at + 1 + NS], mod_rows[:, (2 * n + j) * P:(2 * n + j + 1) * P],
                                             ident[0:1 + NS, 0:1 + NS])
                mm.then_inc(S["adaT_mm"], 1)

            def ada(lo, hi):
                for i in range(lo, hi):
                    arrived(ada_piece[i])
                    if i >= 2:
                        pe.wait_ge(S["ada_row"], i - 1)
                    for c in range(KC):
                        mm = mmul(ps[0:1 + NS, 7 * (i % 2), 0:256], cT[:, c, :],
                                  piece(ada_piece[i])[:, c, :], start=(c == 0), stop=(c == KC - 1))
                    mm.then_inc(S["ada_mm"], 1)
                    if i > lo:
                        ada_turn(i - 1)
                ada_turn(hi - 1)

            pe.wait_ge(S["silu"], 1)
            pe.wait_ge(S["consts"], 1)
            ada(0, 8)

            def front(g):
                s, tg, ng, nb = g.S, g.tg, g.ng, g.nb
                n = first_piece[g.n]

                def tiles(n, col, gi, out, done, src=nT, k=KC):
                    for c in range(k):
                        mm = mmul(out, piece(n)[:, c, col:col + P], src[:, c, gi * tg:(gi + 1) * tg],
                                  start=(c == 0), stop=(c == k - 1))
                        if c == k - 1:
                            mm.then_inc(done, 1)
                        if c % 4 == 3:
                            yield

                def norm(turn):
                    yield from gap(nb + 7)
                    for i, b in enumerate(g.blocks):
                        w = width(b)
                        pe.wait_ge(s["xs_ready"], turn * nb + i + 1)
                        if i >= 3:
                            pe.wait_ge(s["nT_done"], turn * nb + i - 2)
                        for c in range(KC):
                            mm = nc.tensor.transpose(bank2(pair(i))[:, c * P:c * P + w], xs[0:w, i % 2, c * P:(c + 1) * P],
                                                     ident[0:w, 0:w])
                        mm.then_inc(s["xT_mm"], 1)
                        yield from gap(2)

                yield from norm(0)
                yield from gap(5)
                pe.wait_ge(s["nT_done"], nb)
                for i in range(CC * ng):
                    c, gi = i // ng, i % ng
                    if i % (2 * ng) == 0:
                        arrived(n)
                        arrived(n + 1)
                    if i >= 3:
                        pe.wait_ge(s["a_done"], i - 2)
                    yield from tiles(n, (c % 2) * P, gi, ps[:, pair(i), 0:tg], s["gate_mm"])
                    yield from tiles(n + 1, (c % 2) * P, gi, ps[:, pair(i) + 1, 0:tg], s["lin_mm"])
                    if i % (2 * ng) == 2 * ng - 1:
                        n += 2
                yield from gap(5)
                pe.wait_ge(s["a_done"], CC * ng)
                for i in range(CC * ng):
                    c, gi = i // ng, i % ng
                    if i % (2 * ng) == 0:
                        arrived(n)
                    if i >= 6:
                        pe.wait_ge(s["u_done"], i - 5)
                    yield from tiles(n, (c % 2) * P, gi, ps[:, 2 + i % 6, 0:tg], s["u_mm"])
                    if i % (2 * ng) == 2 * ng - 1:
                        n += 1
                yield from gap(5)
                pe.wait_ge(s["u_done"], CC * ng)
                arrived(n)
                arrived(n + 1)
                for i, b in enumerate(g.blocks):
                    for half in range(2):
                        for c in range(KC):
                            mm = mmul(ps[0:width(b), 2 + i % 6, half * 256:(half + 1) * 256], nT[:, c, cols(b)],
                                      piece(n + half)[:, c, :], start=(c == 0), stop=(c == KC - 1))
                            if (half, c) == (1, KC - 1):
                                mm.then_inc(s["v_mm"], 1)
                            if c % 4 == 3:
                                yield
                n += 2
                if g.n == 1:
                    ada(8, 16)
                    n += 8
                yield from gap(12)
                pe.wait_ge(s["v_done"], nb)
                pe.wait_ge(S["masked"], 1)
                for i, b in enumerate(g.blocks):
                    if i >= 3:
                        pe.wait_ge(s["sg_done"], i - 2)
                    for c in range(CC):
                        if b < NB:
                            mm = mmul(bank2(pair(i))[:, 256 * c:256 * (c + 1)], v_tm[:, i, c * P:(c + 1) * P],
                                      wsT[:, 2 * c:2 * c + 2, :].rearrange("p h i -> p (h i)"), start=True, stop=True)
                        else:
                            mm = nc.tensor.transpose(ps[:, pair(i), c * NS:(c + 1) * NS], v_tm[0:NS, i, c * P:(c + 1) * P],
                                                     ident[0:NS, 0:NS])
                    mm.then_inc(s["sg_mm"], 1)
                    yield from gap(2)
                yield from gap(5)
                pe.wait_ge(s["sg_done"], nb)

                def branch(n, src, gate_sem, out_sem, done):
                    for i in range(KC * ng):
                        j, gi = i // ng, i % ng
                        if i % (4 * ng) == 0:
                            no = n
                            arrived(no)
                            n += 1
                        if i % (2 * ng) == 0:
                            arrived(n)
                        if i >= 3:
                            pe.wait_ge(s[done], i - 2)
                        yield from tiles(n, (j % 2) * P, gi, ps[:, pair(i), 0:tg], s[gate_sem])
                        yield from tiles(no, (j % 4) * P, gi, ps[:, pair(i) + 1, 0:tg], s[out_sem], src, CC)
                        if i % (2 * ng) == 2 * ng - 1:
                            n += 1
                    yield from gap(5)

                yield from branch(n, uT, "gb_mm", "ob_mm", "mb_done")
                n += 6 if g.n == 2 else 14
                pe.wait_ge(s["conv"], CC * W + (1 if g.n == 2 else 0))
                pe.wait_ge(s["mb_done"], KC * ng)
                for gi in range(ng):
                    for c in range(CC):
                        mm = mmul(ps[:, 2 + gi, 0:tg], onesm[:], yT[:, c, gi * tg:(gi + 1) * tg],
                                  start=(c == 0), stop=(c == CC - 1))
                    mm.then_inc(s["mean_mm"], 1)
                    yield
                if g.n == 1:
                    ada(16, 20)
                yield from gap(6)
                pe.wait_ge(s["sq_act"], ng)
                for gi in range(ng):
                    for c in range(CC):
                        mm = mmul(ps[:, 4 + gi, 0:tg], onesm[:], ysq[:, c, gi * tg:(gi + 1) * tg],
                                  start=(c == 0), stop=(c == CC - 1))
                    mm.then_inc(s["var_mm"], 1)
                    yield
                yield from gap(11)
                if g.n == 1:
                    ada(20, 24)
                pe.wait_ge(s["y_done"], CC)
                yield from branch(n, yT, "ga_mm", "oa_mm", "m_done")
                n += 6
                pe.wait_ge(s["m_done"], KC * ng)
                pe.wait_ge(S["mod_done"], 2)
                for k, bank in ((2, 2), (5, 4)) if g.n == 1 else ((2, None),):
                    for c in range(KC):
                        at = slice(c * P, (c + 1) * P)
                        mm = mmul(bank2(bank or 2)[:, at], mod[:, k * KC + c, 0:1].broadcast_to([P, P]), ident[:],
                                  start=True, stop=True)
                        if g.n == 2:
                            mm = nc.tensor.transpose(bank2(6)[0:NS, at], mod[:, k * KC + c, 1:1 + NS], ident[:])
                mm.then_inc(s["gt_mm"], 1)
                yield from gap(2)
                pe.wait_ge(s["gt_done"], 1)
                for i in range(4 * nb):
                    col, b = i // nb, g.blocks[i % nb]
                    w = width(b)
                    if i % nb == 0:
                        arrived(n + col)
                    if i >= 6:
                        pe.wait_ge(s["x1_done"], i - 5)
                    for c in range(KC):
                        mm = mmul(ps[0:w, 2 + i % 6, 0:256], mT[:, c, cols(b)], piece(n + col)[:, c, :],
                                  start=(c == 0), stop=(c == KC - 1))
                        if c == KC - 1:
                            mm.then_inc(s["wo_mm"], 1)
                        if c % 4 == 3:
                            yield
                n += 4
                yield from gap(3)
                pe.wait_ge(s["x1_done"], 4 * nb)
                yield from norm(1)
                yield from gap(5)
                pe.wait_ge(s["nT_done"], 2 * nb)
                for i, b in enumerate(g.blocks):
                    w = width(b)
                    if i >= 3:
                        pe.wait_ge(s["n2_done"], i - 2)
                    for c in range(KC):
                        mm = nc.tensor.transpose(bank2(pair(i))[0:w, c * P:(c + 1) * P], nT[:, c, cols(b)], ident[:])
                    mm.then_inc(s["t2b_mm"], 1)
                    yield from gap(2)
                yield from gap(3)
                pe.wait_ge(s["n2_done"], nb)
                for ch in range(NCH + 3):
                    if ch < NCH:
                        if ch % 2 == 0:
                            arrived(n + ch // 2)
                        if ch >= 2:
                            pe.wait_ge(s["q_done"], ch - 1)
                        for gi in range(ng):
                            yield from tiles(n + ch // 2, (ch % 2) * P, gi, ps[:, 2 + 2 * (ch % 2) + gi, 0:tg], s["q_mm"])
                    else:
                        yield from gap(2 * ng)
                    if ch >= 2 and ch - 2 < NCH:
                        k = ch - 2
                        pe.wait_ge(s["q_done"], k + 1)
                        if k >= 2:
                            pe.wait_ge(s["s_done"], k - 1)
                        for i in range(4):
                            mm = mmul(ps[:, 6 + k % 2, i * P:(i + 1) * P], qbuf[:, k % 2, i * P:(i + 1) * P],
                                      keys[:, k % 2, :], start=True, stop=True)
                        mm.then_inc(s["s_mm"], 1)
                    yield
                yield from gap(4)
                if g.n == 2:
                    pe.wait_ge(s["q_done"], NCH)
                    for ch in range(NCH):
                        mm = mmul(ps[0:NS, 2 + ch // 4, (ch % 4) * P:(ch % 4 + 1) * P], qs[:, ch, :], keys[:, ch % 2, :],
                                  start=True, stop=True)
                    mm.then_inc(S["qs_mm"], 1)
                    pe.wait_ge(s["s_done"], NCH)
                    for c in range(KC):
                        mm = nc.tensor.transpose(bank2(6)[0:NS, c * P:(c + 1) * P], mod[:, 5 * KC + c, 1:1 + NS], ident[:])
                    mm.then_inc(s["gt_mm"], 1)
                yield from gap(36)

            for _ in front(G1):
                pass

            def open_acc(b):
                if b >= 1:
                    pe.wait_ge(S["acc_read"], b)
                for half in range(2):
                    mmul(ps[:, half, :], zero[:], zero[:, 0:1].broadcast_to([P, 512]), start=True, stop=False)

            def close_acc():
                for half in range(2):
                    mm = mmul(ps[:, half, :], zero[:], zero[:, 0:1].broadcast_to([P, 512]), start=False, stop=True)
                mm.then_inc(S["acc_done"], 1)

            def value(j, r):
                for half in range(2):
                    mm = mmul(ps[:, half, :], diag[:, j, :], rows[:, r, D + 512 * half:D + 512 * (half + 1)],
                              start=False, stop=False)
                return mm

            def peer(tick):
                if tick == 0:
                    return
                n = tick - 1
                if n % NSLOT == 0:
                    open_acc(n // NSLOT)
                pe.wait_ge(S["weights"], n + 1)
                value(n % 4, n % RB1).then_inc(S["rows_used"], 1)
                if n % NSLOT == NSLOT - 1:
                    close_acc()

            interleave(peer, front(G2))
            peer(TICKS)
            def sample_x(k):
                if k >= 3:
                    pe.wait_ge(S["s_dots"], k - 2)
                for half in range(2):
                    mm = mmul(ps[:, pair(k) + half, :], ident[0:NS, k:k + 1].broadcast_to([NS, P]),
                              xn2[0:NS, 4, 512 * half:512 * (half + 1)], start=True, stop=True)
                mm.then_inc(S["xb_mm"], 1)

            def sum_block(turn):
                for half in range(2):
                    mmul(ps[:, half, :], zero[:], zero[:, 0:1].broadcast_to([P, 512]), start=True, stop=False)
                with pe.Fori(0, 8) as m:
                    for q in range(8):
                        pe.wait_ge(S["weights"], turn * 64 + m * 8 + (TICKS + q + 1))
                        value(2 * q % 4, buffer2(2 * q))
                        value((2 * q + 1) % 4, buffer2(2 * q + 1)).then_inc(S["rows_used"], 1)
                close_acc()

            with pe.Fori(0, NB - NB1 - 1) as bb:
                pe.wait_ge(S["acc_read"], bb + NB1)
                sum_block(bb)
            for k in range(3):
                sample_x(k)
            pe.wait_ge(S["acc_read"], NB - 1)
            for k in range(NS):
                pe.wait_ge(S["s_weights"], k + 1)
                for half in range(2):
                    mm = mmul(ps[0:NS, half, :], wmask[:, k, :], rows[:, buffer2(k), D + 512 * half:D + 512 * (half + 1)],
                              start=(k == 0), stop=(k == NS - 1))
                if k % 2 == 1:
                    mm.then_inc(S["rows_used"], 1)
                if k + 3 < NS:
                    sample_x(k + 3)
            pe.wait_ge(S["acc_read"], NB)
            sum_block(NB - NB1 - 1)

        @block.scalar
        def _(act_):
            ac = nc.scalar.activation
            act_.wait_ge(S["c_in"], 64)
            ac(sigc[:], cT[:], ACT.Sigmoid).then_inc(S["sigmoid_c"], 1)

            def ada_rows(lo, hi):
                for i in range(lo, hi):
                    act_.wait_ge(S["ada_mm"], i + 1)
                    ac(mod_rows[:, i * 256:(i + 1) * 256], ps[0:1 + NS, 7 * (i % 2), 0:256], ACT.Copy
                       ).then_inc(S["ada_row"], 1)

            def front(g):
                s, tg, ng, nb = g.S, g.tg, g.ng, g.nb
                if g.n == 2:
                    yield from gap(2)

                def norm(turn):
                    for i, b in enumerate(g.blocks):
                        w = width(b)
                        if g.n == 1:
                            x, out = xn1[0:w, i, :], g.sq[0:w, i, :]
                        else:
                            x = (x_first if turn == 0 else xn2)[0:w, i, :]
                            out = part(big, RB1 * 2 * D, 4, D)[0:w, i % 4, :]
                        if i == 0:
                            act_.wait_ge(S["consts"], 1)
                            act_.wait_ge(s["x_in"], 16 * nb)
                            if turn == 1:
                                act_.wait_ge(s["x1_done"], 4 * nb)
                        if i == 4:
                            act_.wait_ge(s["sum_sq"], turn * nb + 1)
                        ac(out, x, ACT.Square, accum_out=stat[0:w, 0, b:b + 1]).then_inc(s["sum_sq"], 1)
                        yield
                    yield from gap(2)
                    act_.wait_ge(s["mean_sq"], turn + 1)
                    lo, hi = g.blocks[0], g.blocks[-1] + 1
                    ac(stat[:, 1, lo:hi], stat[:, 0, lo:hi], ACT.Sqrt).then_inc(s["root"], 1)
                    if g.n == 1 and turn == 0:
                        ada_rows(0, 8)
                    yield from gap(5 + 2 * nb)

                if g.n == 2:
                    act_.wait_ge(S["q_mm1"], NCH * G1.ng)
                    act_.wait_ge(S["t2b_mm1"], G1.nb)
                yield from norm(0)
                yield from gap(5)
                for i in range(CC * ng):
                    yield from gap(3)
                    act_.wait_ge(s["gate_mm"], i + 1)
                    if i >= 2:
                        act_.wait_ge(s["a_done"], i - 1)
                    elif i == 0:
                        act_.wait_ge(s["xT_mm"], nb)
                    ac(sig[:, i % 2, 0:tg], ps[:, pair(i), 0:tg], ACT.Sigmoid).then_inc(s["sig_a"], 1)
                    yield
                yield from gap(5)
                if g.n == 2:
                    act_.wait_ge(S["routes1"], G1.nb)
                for i in range(CC * ng):
                    c, gi = i // ng, i % ng
                    yield
                    act_.wait_ge(s["u_mm"], i + 1)
                    ac(uT[:, c, gi * tg:(gi + 1) * tg], ps[:, 2 + i % 6, 0:tg], ACT.Copy).then_inc(s["u_done"], 1)
                    yield
                yield from gap(5)
                for i in range(nb + 2):
                    yield
                    if i >= 2:
                        b = g.blocks[i - 2]
                        w = width(b)
                        act_.wait_ge(s["v_stat"], i - 1)
                        ac(vroot[0:w, b:b + 1], mv[0:w, b, 1:2], ACT.Sqrt, bias=eps[0:w, :]).then_inc(s["v_root"], 1)
                    yield from gap(3)
                if g.n == 1:
                    ada_rows(8, 16)
                yield from gap(4 + 2 * nb + 5)

                def gates(gate_sem, sig_sem, done):
                    for i in range(KC * ng):
                        yield from gap(2)
                        act_.wait_ge(s[gate_sem], i + 1)
                        if i >= 2:
                            act_.wait_ge(s[done], i - 1)
                        ac(sig[:, i % 2, 0:tg], ps[:, pair(i), 0:tg], ACT.Sigmoid).then_inc(s[sig_sem], 1)
                        yield
                    yield from gap(5)

                yield from gates("gb_mm", "sig_b", "mb_done")
                yield from gap(ng + 3)
                if g.n == 1:
                    ada_rows(16, 20)
                act_.wait_ge(s["yc"], 1)
                if g.n == 2:
                    act_.wait_ge(S["out_v"], 16)
                for gi in range(ng):
                    at = slice(gi * tg, (gi + 1) * tg)
                    ac(ysq[:, :, at], yT[:, :, at], ACT.Square).then_inc(s["sq_act"], 1)
                    yield
                yield from gap(3)
                act_.wait_ge(s["var_mm"], ng)
                for gi in range(ng):
                    ac(rbc[:, gi * tg:(gi + 1) * tg], ps[:, 4 + gi, 0:tg], ACT.Sqrt, bias=eps[:]).then_inc(s["std_act"], 1)
                yield from gap(4)
                act_.wait_ge(s["yn_done"], 1)
                for c in range(CC):
                    ac(ysq[:, c, 0:g.nt], yT[:, c, 0:g.nt], ACT.Sigmoid, scale=cvec[:, 1, c:c + 1],
                       bias=cvec[:, 2, c:c + 1]).then_inc(s["sig_y"], 1)
                if g.n == 1:
                    ada_rows(20, 24)
                yield from gap(7)
                act_.wait_ge(s["mb_done"], KC * ng)
                yield from gates("ga_mm", "sig_g", "m_done")
                act_.wait_ge(s["gt_mm"], 1)
                if g.n == 1:
                    act_.wait_ge(S["adaT_mm"], 24)
                    ac(gt2[:], bank2(4), ACT.Copy)
                else:
                    act_.wait_ge(s["v_done"], nb)
                    act_.wait_ge(s["sg_done"], nb)
                    ac(gts, bank2(6)[0:NS, :], ACT.Copy)
                ac(g.gt1, bank2(2), ACT.Copy).then_inc(s["gt_done"], 1)
                yield from gap(2)
                yield from gap(8 * nb + 3)
                yield from norm(1)
                yield from gap(5)
                for i, b in enumerate(g.blocks):
                    w = width(b)
                    yield
                    act_.wait_ge(s["t2b_mm"], i + 1)
                    if i == 0:
                        act_.wait_ge(s["out_x1"], 16 * nb)
                    ac(g.xn[0:w, i, :], bank2(pair(i))[0:w, :], ACT.Copy).then_inc(s["n2_done"], 1)
                    yield
                yield from gap(3)
                for ch in range(NCH + 3):
                    yield from gap(2 * ng - 1)
                    if ch < NCH:
                        act_.wait_ge(s["q_mm"], ng * (ch + 1))
                        if ch >= 2:
                            act_.wait_ge(s["s_mm"], ch - 1)
                        for gi in range(ng):
                            last = ac(qbuf[:, ch % 2, gi * tg:(gi + 1) * tg], ps[:, 2 + 2 * (ch % 2) + gi, 0:tg], ACT.Copy)
                        if g.n == 2:
                            last = ac(qs[:, ch, :], ps[:, 3 + 2 * (ch % 2), tg - NS:tg], ACT.Copy)
                        last.then_inc(s["q_done"], 1)
                    yield from gap(2)
                yield from gap(8)
                if g.n == 2:
                    act_.wait_ge(s["gt_mm"], 2)
                    act_.wait_ge(s["x1_done"], 4 * nb)
                    ac(gts, bank2(6)[0:NS, :], ACT.Copy).then_inc(s["gt_done"], 1)
                yield from gap(27)
                next(g.numerators)
                yield from gap(5)

            def numerators(g):
                for turn, i in enumerate(g.order):
                    b = g.blocks[i]
                    act_.wait_ge(g.S["sm_diff"], turn + 1)
                    ac(gate[:, b, :], gate[:, b, :], ACT.Exp).then_inc(g.S["sm_exp"], 1)
                    yield

            for g in (G1, G2):
                g.numerators = numerators(g)
            for _ in front(G1):
                pass

            def peer(tick):
                j = tick % 4
                act_.wait_ge(S["dots"], tick + 1)
                ac(gel[:, j:j + 1], act[:, j:j + 1], ACT.Gelu).then_inc(S["gelu"], 1)
                if tick in ROUTE_EXP:
                    next(G1.numerators)

            interleave(peer, front(G2))
            def gelu(q, at):
                act_.wait_ge(S["dots"], at + 1)
                ac(gel[:, 2 * q:2 * q + 2], act[:, 2 * q:2 * q + 2], ACT.Gelu).then_inc(S["gelu"], 1)

            def square(n):
                b = finals[n]
                w = width(b)
                act_.wait_ge(S["x2_done"], n + 1)
                if n >= 3:
                    act_.wait_ge(S["fin_sq"], n - 2)
                ac(part(arena, 0, 3, D)[0:w, n % 3, :], x1_again(b)[0:w, :], ACT.Square, accum_out=stat[0:w, 0, n:n + 1]
                   ).then_inc(S["fin_sq"], 1)

            def root(turn, lo, hi):
                act_.wait_ge(S["fin_ms"], turn)
                ac(stat[:, 1, lo:hi], stat[:, 0, lo:hi], ACT.Sqrt).then_inc(S["fin_root"], 1)

            for bb in range(NB - NB1):
                last = bb == NB - NB1 - 1
                if last:
                    for k in range(NS):
                        act_.wait_ge(S["s_dots"], k + 1)
                        ac(gel[:, k % 4:k % 4 + 1], act[:, k % 4:k % 4 + 1], ACT.Gelu).then_inc(S["s_gelu"], 1)
                first = TICKS + bb * 64
                for q in range(EARLY + 7):
                    gelu(q % 2, first + q)
                    if not last and q == 6 or bb == NB - NB1 - 2 and q == 6 + ROUTE_PIECES:
                        next(G2.numerators)
                    if last and 2 <= q < 2 + NB:
                        square(q - 2)
                    if last and q == NB + 3:
                        root(1, 0, NB)
                with act_.Fori(0, (64 - EARLY - 7) // 2) as m:
                    for q in range(2):
                        gelu(q, m * 2 + (first + EARLY + 7 + q))
            square(NB)
            root(2, NB, NBT)

        @block.gpsimd
        def _(pool):
            gp = nc.gpsimd
            gp.memset(ident[:], 0.0)
            gp.memset(zero[:], 0.0)
            gp.memset(onesm[:], 1.0 / DC)
            gp.memset(stat[:], 1.0)
            gp.memset(eps[:], EPS)
            gp.iota(iota[:], [[1, NC]], base=0, channel_multiplier=0, allow_small_or_imprecise_dtypes=True)
            gp.memset(eye8[:], 0.0).then_inc(S["pool_chain"], 1)
            pool.wait_ge(S["pool_chain"], 1)
            gp.affine_select(out=eye8[:], in_=eye8[:], compare_op=ALU.not_equal, fill=1.0, base=0,
                             pattern=[[1, NS], [-1, NS]], channel_multiplier=0)
            gp.affine_select(out=ident[:], in_=ident[:], compare_op=ALU.not_equal, fill=1.0, base=0,
                             pattern=[[-1, P]], channel_multiplier=1).then_inc(S["consts"], 1)
            pool.wait_ge(S["small_in"], SMALL_IN)
            gp.affine_select(out=wsT, in_=wsT, compare_op=ALU.is_ge, fill=0.0, base=0,
                             pattern=[[0, H], [1, P]], channel_multiplier=-1).then_inc(S["masked"], 1)

            def fetch(r, index, done):
                gp.indirect_dma_start(rows[:, r, :], None, t["experts"],
                                      bass.IndirectOffsetOnAxis(ap=index, axis=0)).then_inc(done, 16)

            for n in range(TICKS):
                b, slot = n // NSLOT, n % NSLOT
                if slot == 0 and b >= 1:
                    pool.wait_ge(S["routes1"], b + 1)
                if b == 0 and slot % (2 * TOP) == 0:
                    pool.wait_ge(S["first_ids"], slot // (2 * TOP) + 1)
                if n >= RB1:
                    pool.wait_ge(S["rows_used"], n - RB1 + 1)
                fetch(n % RB1, eid[:, b, slot:slot + 1], s_row[n % RB1])
            pool.wait_ge(S["q_mm2"], NCH * G2.ng)
            pool.wait_ge(S["routes2"], 1)
            slots = eid[:].rearrange("p b n -> p (b n)")
            gp.tensor_copy(idx[:, 0:2], slots[:, NB1 * NSLOT:NB1 * NSLOT + 2]).then_inc(S["idx_ready"], 1)
            for bb in range(NB - NB1):
                b = NB1 + bb
                before = TICKS + bb * 64 + (S_GROUPS if b == NB - 1 else 0)
                if b == NB - 1:
                    pool.wait_ge(S["idxs_ready"], 1)
                    for k in range(NS):
                        if k % 2 == 0:
                            pool.wait_ge(S["rows_used"], before - S_GROUPS - RB2 // 2 + k // 2 + 1)
                        fetch(buffer2(k), idxs[:, k:k + 1], s_row[buffer2(k)])

                def eight(m, last=False):
                    for q in range(8):
                        if last and q == 7 and b < NB - 1:
                            pool.wait_ge(S["routes2"], bb + 2 if b < NB - 2 else G2.nb)
                        pool.wait_ge(S["idx_ready"], m * 8 + (bb * 64 + q + 1))
                        pool.wait_ge(S["rows_used"], m * 8 + (before - RB2 // 2 + q + 1))
                        nxt, at = 2 * ((q + 1) % 8), m * 16 + (b * NSLOT + 2 * q + 2)
                        gp.tensor_copy(idx[:, nxt:nxt + 2], slots[:, bass.ds(at, 2)]).then_inc(S["idx_ready"], 1)
                        for k in range(2):
                            r = buffer2(2 * q + k)
                            fetch(r, idx[:, 2 * q + k:2 * q + k + 1], s_row[r])

                with pool.Fori(0, 7) as m:
                    eight(m)
                eight(7, last=True)

        @block.vector
        def _(dve):
            v = nc.vector
            k_ = [0]

            def link(ins):
                k_[0] += 1
                ins.then_inc(S["dve_chain"], 1)
                dve.wait_ge(S["dve_chain"], k_[0])

            def rsqrt(lo, hi):
                sq_, root_, out, tmp = (stat[:, i, lo:hi] for i in range(4))
                link(v.reciprocal(out, root_))
                link(v.tensor_tensor(tmp, out, out, ALU.mult))
                link(v.tensor_tensor(tmp, tmp, sq_, ALU.mult))
                link(v.tensor_scalar(tmp, tmp, -0.5, 1.5, ALU.mult, ALU.add))
                link(v.tensor_tensor(out, out, tmp, ALU.mult))

            dve.wait_ge(S["sigmoid_c"], 1)
            v.tensor_tensor(cT[:], cT[:], sigc[:], ALU.mult).then_inc(S["silu"], 1)

            def modulation(lo, hi, turn):
                dve.wait_ge(S["adaT_mm"], hi // 2)
                link(v.tensor_tensor(mod[:, lo:hi, :],
                                     ps[:, 1, lo * (1 + NS):hi * (1 + NS)].rearrange("p (k n) -> p k n", n=1 + NS),
                                     bada[:, lo:hi].unsqueeze(2).broadcast_to([P, hi - lo, 1 + NS]), ALU.add))
                sc, gg, kk = ((scale1, gmix, 1), (scale2, gffn, 4))[turn]
                v.scalar_tensor_tensor(out=sc[:], in0=mod[:, kk * KC:(kk + 1) * KC, :], scalar=1.0,
                                       in1=gg[:].unsqueeze(2).broadcast_to([P, KC, 1 + NS]),
                                       op0=ALU.add, op1=ALU.mult).then_inc(S["mod_done"], 1)
                dve.wait_ge(S["mod_done"], turn + 1)

            def front(g):
                s, tg, ng, nb = g.S, g.tg, g.ng, g.nb
                lo, hi = g.blocks[0], g.blocks[-1] + 1
                if g.n == 2:
                    yield from gap(4)

                def norm(turn):
                    scale, shift = ((scale1, 0), (scale2, 3))[turn]

                    def scaled(i):
                        w = width(g.blocks[i])
                        if i >= 2:
                            dve.wait_ge(s["xT_mm"], turn * nb + i - 1)
                        x = g.xn if g.n == 1 or turn == 1 else x_first
                        v.tensor_scalar(xs[0:w, i % 2, :], x[0:w, i, :], stat[0:w, 2, lo + i:lo + i + 1], None, ALU.mult
                                        ).then_inc(s["xs_ready"], 1)

                    yield from gap(nb - 1)
                    dve.wait_ge(s["sum_sq"], (turn + 1) * nb)
                    v.tensor_scalar(stat[:, 0, lo:hi], stat[:, 0, lo:hi], 1.0 / D, EPS, ALU.mult, ALU.add
                                    ).then_inc(s["mean_sq"], 1)
                    yield from gap(3)
                    dve.wait_ge(s["root"], turn + 1)
                    rsqrt(lo, hi)
                    yield
                    scaled(0)
                    scaled(1)
                    if g.n == 1 and turn == 0:
                        modulation(0, 2 * KC, 0)
                    yield from gap(4)
                    for i, b in enumerate(g.blocks):
                        dve.wait_ge(s["xT_mm"], turn * nb + i + 1)
                        src = bank2(pair(i))
                        if b < NB:
                            for c in range(KC):
                                last = v.tensor_scalar(nT[:, c, cols(b)], src[:, c * P:(c + 1) * P],
                                                       scale[:, c, 0:1], mod[:, shift * KC + c, 0:1], ALU.mult, ALU.add)
                        else:
                            src = src.rearrange("p (c t) -> p c t", c=KC)[:, :, 0:NS]
                            link(v.tensor_tensor(nT[:, :, cols(b)], src, scale[:, :, 1:1 + NS], ALU.mult))
                            last = v.tensor_tensor(nT[:, :, cols(b)], nT[:, :, cols(b)],
                                                   mod[:, shift * KC:(shift + 1) * KC, 1:1 + NS], ALU.add)
                        last.then_inc(s["nT_done"], 1)
                        yield
                        if i + 2 < nb:
                            scaled(i + 2)
                        yield

                yield from norm(0)
                yield from gap(5)
                dve.wait_ge(S["small_in"], SMALL_IN)
                if g.n == 1:
                    v.memset(aT[:, :, 0:W - 1], 0.0)
                else:
                    v.tensor_copy(aT[:, :, 0:W - 1], hist[:])
                for i in range(CC * ng):
                    c, gi = i // ng, i % ng
                    yield from gap(3)
                    dve.wait_ge(s["sig_a"], i + 1)
                    dve.wait_ge(s["lin_mm"], i + 1)
                    lin = ps[:, pair(i) + 1, :]
                    w = min(tg, g.np - gi * tg)
                    last = v.tensor_tensor(aT[:, c, W - 1 + gi * tg:W - 1 + gi * tg + w], lin[:, 0:w], sig[:, i % 2, 0:w],
                                           ALU.mult)
                    if w < tg:
                        last = v.tensor_tensor(full_s[:, c, :, W - 1:W], lin[:, w:tg].unsqueeze(2),
                                               sig[:, i % 2, w:tg].unsqueeze(2), ALU.mult)
                    last.then_inc(s["a_done"], 1)
                    yield
                dve.wait_ge(s["a_done"], CC * ng)
                if g.n == 1:
                    v.tensor_copy(hist[:], aT[:, :, 512:512 + W - 1]).then_inc(S["hist_kept"], 1)
                else:
                    link(v.tensor_tensor(conv_s, full_s[:], wdw[:].unsqueeze(2).broadcast_to([P, CC, NS, W]), ALU.mult))
                    link(v.tensor_reduce(yT[:, :, 512:GW], conv_s, AX.X, ALU.add))
                    v.tensor_tensor(yT[:, :, 512:GW], yT[:, :, 512:GW], cvec[:, 0, :].unsqueeze(2).broadcast_to([P, CC, NS]),
                                    ALU.add).then_inc(s["conv"], 1)
                before = 1 if g.n == 2 else 0
                taps = [0]

                def conv(count):
                    for n in range(taps[0], min(taps[0] + count, CC * W)):
                        kk, c = n // CC, n % CC
                        y = yT[:, c, 0:512]
                        if kk == 0:
                            ins = v.tensor_scalar(y, aT[:, c, 0:512], wdw[:, c, 0:1], cvec[:, 0, c:c + 1], ALU.mult, ALU.add)
                        else:
                            dve.wait_ge(s["conv"], before + n - CC + 1)
                            ins = v.scalar_tensor_tensor(out=y, in0=aT[:, c, kk:kk + 512], scalar=wdw[:, c, kk:kk + 1],
                                                         in1=y, op0=ALU.mult, op1=ALU.add)
                        ins.then_inc(s["conv"], 1)
                        taps[0] += 1

                def conv_gap(n):
                    for _ in range(n):
                        conv(taps_per_step[g.n])
                        yield

                yield from gap(5)
                yield from conv_gap(2 * CC * ng)
                yield from gap(5)
                for i in range(nb + 2):
                    yield from conv_gap(1) if i < nb and g.n == 2 else gap(1)
                    if i >= 2:
                        b, j = g.blocks[i - 2], i - 2
                        w = width(b)
                        dve.wait_ge(s["v_root"], j + 1)
                        link(v.reciprocal(vroot[0:w, b:b + 1], vroot[0:w, b:b + 1]))
                        link(v.scalar_tensor_tensor(out=v_tm[0:w, j, :], in0=ps[0:w, 2 + j % 6, :], scalar=mv[0:w, b, 0:1],
                                                    in1=rowv[0:w, 0, :], op0=ALU.subtract, op1=ALU.mult))
                        v.scalar_tensor_tensor(out=v_tm[0:w, j, :], in0=v_tm[0:w, j, :], scalar=vroot[0:w, b:b + 1],
                                               in1=rowv[0:w, 1, :], op0=ALU.mult, op1=ALU.add).then_inc(s["v_done"], 1)
                    yield
                    yield from conv_gap(1) if i < nb and g.n == 2 else gap(1)
                    if i < nb:
                        w = width(g.blocks[i])
                        dve.wait_ge(s["v_mm"], i + 1)
                        link(v.bn_stats(bnst[0:w, i % 2, :], ps[0:w, 2 + i % 6, :]))
                        v.bn_aggr(mv[0:w, g.blocks[i], :], bnst[0:w, i % 2, :]).then_inc(s["v_stat"], 1)
                    yield
                yield from gap(4)
                dve.wait_ge(s["u_done"], CC * ng)
                beside_gates = conv_gap if g.n == 2 else gap
                for i, b in enumerate(g.blocks):
                    yield from beside_gates(1)
                    dve.wait_ge(s["sg_mm"], i + 1)
                    if i >= 1:
                        dve.wait_ge(s["sg_done"], i)
                    if b < NB:
                        sg = bank2(pair(i)).rearrange("p (c n) -> p c n", c=CC)
                        for hh in range(2):
                            at = slice(HD * hh, HD * hh + HD)
                            last = v.tensor_tensor(sgt[at, :, :], sg[at, :, P * hh:P * hh + P], bs[at, :, :], ALU.add)
                        link(last)
                        v.tensor_tensor(uT[:, :, cols(b)], uT[:, :, cols(b)], sgt, ALU.mult).then_inc(s["sg_done"], 1)
                    else:
                        vs = ps[:, pair(i), 0:CC * NS].rearrange("p (c s) -> p c s", c=CC)
                        link(v.tensor_tensor(sgt[:, :, 0:NS], vs, w00[:].unsqueeze(2).broadcast_to([P, CC, NS]), ALU.mult))
                        link(v.tensor_tensor(sgt[:, :, 0:NS], sgt[:, :, 0:NS], bs[:, :, 0:1].broadcast_to([P, CC, NS]), ALU.add))
                        v.tensor_tensor(uT[:, :, cols(b)], uT[:, :, cols(b)], sgt[:, :, 0:NS], ALU.mult
                                        ).then_inc(s["sg_done"], 1)
                    yield from beside_gates(1)
                yield from gap(5)
                if g.n == 2:
                    dve.wait_ge(S["routes1"], G1.nb)
                    dve.wait_ge(S["wo_mm1"], 4 * G1.nb)
                for i in range(KC * ng):
                    j, gi = i // ng, i % ng
                    yield from conv_gap(2)
                    dve.wait_ge(s["sig_b"], i + 1)
                    dve.wait_ge(s["ob_mm"], i + 1)
                    v.tensor_tensor(mT[:, j, gi * tg:(gi + 1) * tg], ps[:, pair(i) + 1, 0:tg], sig[:, i % 2, 0:tg], ALU.mult
                                    ).then_inc(s["mb_done"], 1)
                    yield from conv_gap(1)
                conv(CC * W)
                yield from gap(5)
                yield from gap(ng - 1)
                dve.wait_ge(s["mean_mm"], ng)
                for gi in range(ng):
                    y = yT[:, :, gi * tg:(gi + 1) * tg]
                    last = v.tensor_tensor(y, y, ps[:, 2 + gi, 0:tg].unsqueeze(1).broadcast_to([P, CC, tg]), ALU.subtract)
                last.then_inc(s["yc"], 1)
                yield from gap(ng + 6)
                dve.wait_ge(s["std_act"], ng)
                link(v.reciprocal(rbc[:, 0:g.nt], rbc[:, 0:g.nt]))
                dve.wait_ge(s["sq_act"], ng)
                v.tensor_tensor(yT[:, :, 0:g.nt], yT[:, :, 0:g.nt], rbc[:, 0:g.nt].unsqueeze(1).broadcast_to([P, CC, g.nt]),
                                ALU.mult).then_inc(s["yn_done"], 1)
                yield from gap(4)
                for c in range(CC):
                    dve.wait_ge(s["sig_y"], c + 1)
                    y = yT[:, c, 0:g.nt]
                    link(v.tensor_scalar(y, y, cvec[:, 1, c:c + 1], cvec[:, 2, c:c + 1], ALU.mult, ALU.add))
                    v.tensor_tensor(y, y, ysq[:, c, 0:g.nt], ALU.mult).then_inc(s["y_done"], 1)
                    yield
                yield from gap(4)

                if g.n == 1:
                    modulation(2 * KC, 6 * KC, 1)

                chain_at = []

                def add_m(i):
                    j, gi = i // ng, i % ng
                    m = mT[:, j, gi * tg:(gi + 1) * tg]
                    dve.wait_ge(S["dve_chain"], chain_at[i])
                    v.tensor_tensor(m, m, prod[:, i % 2, 0:tg], ALU.add).then_inc(s["m_done"], 1)

                for i in range(KC * ng):
                    yield from gap(2)
                    dve.wait_ge(s["sig_g"], i + 1)
                    dve.wait_ge(s["oa_mm"], i + 1)
                    if i >= 2:
                        dve.wait_ge(s["m_done"], i - 1)
                    k_[0] += 1
                    chain_at.append(k_[0])
                    v.tensor_tensor(prod[:, i % 2, 0:tg], ps[:, pair(i) + 1, 0:tg], sig[:, i % 2, 0:tg], ALU.mult
                                    ).then_inc(S["dve_chain"], 1)
                    add_m(i)
                    yield
                yield from gap(5)
                yield from gap(2)
                dve.wait_ge(s["gt_done"], 1)
                if g.n == 2:
                    dve.wait_ge(S["x_again"], 16 * nb)
                for i in range(4 * nb):
                    col, b = i // nb, g.blocks[i % nb]
                    w = width(b)
                    at = slice(256 * col, 256 * (col + 1))
                    yield
                    dve.wait_ge(s["wo_mm"], i + 1)
                    if i >= 2:
                        dve.wait_ge(s["x1_done"], i - 1)
                    gt_ = g.gt1[:, at] if b < NB else gts[:, at]
                    x = g.xn[0:w, i % nb, at]
                    link(v.tensor_tensor(xs[0:w, i % 2, 0:256], ps[0:w, 2 + i % 6, 0:256], gt_, ALU.mult))
                    v.tensor_tensor(x, x, xs[0:w, i % 2, 0:256], ALU.add).then_inc(s["x1_done"], 1)
                    yield
                yield from gap(3)
                dve.wait_ge(s["x1_done"], 4 * nb)
                yield from norm(1)
                yield from gap(5)
                yield from gap(2 * nb + 3)
                if g.n == 2:
                    dve.wait_ge(S["out_hist"], 16 * (1 + CC))
                    v.memset(v16[:, 4, :, :], 0.0)
                    link(v.memset(i16[:, 4, :, :], 0))

                def top16(scores, out, w, reps):
                    def at(x, o, half):
                        return x[0:w, o[0], o[1], 8 * half:8 * half + 8]
                    for sc, o in zip(scores, out):
                        last = v.max(at(v16, o, 0), sc)
                    link(last)
                    yield
                    for n, (sc, o) in enumerate(zip(scores, out)):
                        last = v.match_replace(reps[0:w, n, :], at(v16, o, 0), sc, LOW)
                    link(last)
                    yield
                    for n, (sc, o) in enumerate(zip(scores, out)):
                        v.max_index(at(i16, o, 0), at(v16, o, 0), sc)
                        last = v.max(at(v16, o, 1), reps[0:w, n, :])
                    link(last)
                    yield
                    for n, o in enumerate(out):
                        last = v.max_index(at(i16, o, 1), at(v16, o, 1), reps[0:w, n, :])
                    last.then_inc(s["s_done"], 1)
                    yield

                for ch in range(NCH + 3):
                    if ch >= 3:
                        k = ch - 3
                        dve.wait_ge(s["s_mm"], k + 1)
                        if k >= 1:
                            dve.wait_ge(s["s_done"], k)
                        yield from top16([ps[:, 6 + k % 2, i * P:(i + 1) * P] for i in range(4)],
                                         [(i, k) for i in range(4)], P, rep)
                    else:
                        yield from gap(2 * ng)
                    yield
                yield from gap(4)
                if g.n == 2:
                    dve.wait_ge(S["qs_mm"], 1)
                    for c in range(4):
                        dve.wait_ge(s["s_done"], NCH + c)
                        yield from top16([ps[0:NS, 2 + c, i * P:(i + 1) * P] for i in range(4)],
                                         [(4, 4 * c + i) for i in range(4)], NS, rep_s)
                    dve.wait_ge(s["s_done"], NCH + 4)
                dve.wait_ge(s["s_done"], NCH)
                dve.wait_ge(s["s_mm"], NCH)
                if g.n == 2:
                    dve.wait_ge(s["q_mm"], NCH * ng)
                link(v.tensor_copy(i16f[:, 0:nb, :, :], i16[:, 0:nb, :, :]))
                vv = v16[:, 0:nb, :, :].rearrange("p b (h f) k -> p (b h) f k", f=2)
                ii = i16f[:, 0:nb, :, :].rearrange("p b (h f) k -> p (b h) f k", f=2)
                at = 0
                for a in range(9):
                    n_ = ROWS[a] if a < 8 else 8

                    def first(x):
                        return x[:, :, 0, a:a + 1].broadcast_to([P, nb * H, n_]) if a < 8 else x[:, :, 0, 8:16]

                    def second(x):
                        return x[:, :, 1, 0:n_] if a < 8 else x[:, :, 1, 0:1].broadcast_to([P, nb * H, n_])

                    v.tensor_tensor(g.cand[:, :, at:at + n_], first(vv), second(vv), ALU.add)
                    last = v.scalar_tensor_tensor(out=g.cid[:, :, at:at + n_], in0=first(ii), scalar=float(NKEY),
                                                  in1=second(ii), op0=ALU.mult, op1=ALU.add)
                    at += n_
                    if a == 8:
                        last.then_inc(s["tables"], 1)
                        dve.wait_ge(s["tables"], 1)
                    yield
                yield from route(g, 0)
                yield

            def route(g, turn):
                s, i = g.S, g.order[turn]
                b = g.blocks[i]
                best = gate[:, b, :].rearrange("p (h k) -> p h k", k=TOP)
                pos = g.posf.bitcast(u32)
                hs = range(H)
                for h in hs:
                    last = v.max(best[:, h, 0:8], g.cand[:, i * H + h, :])
                link(last)
                yield
                for h in hs:
                    last = v.match_replace(g.crep[:, h, :], best[:, h, 0:8], g.cand[:, i * H + h, :], LOW)
                link(last)
                yield
                for h in hs:
                    v.max_index(pos[:, i * H + h, 0:8], best[:, h, 0:8], g.cand[:, i * H + h, :])
                    last = v.max(best[:, h, 8:16], g.crep[:, h, :])
                link(last)
                yield
                for h in hs:
                    last = v.max_index(pos[:, i * H + h, 8:16], best[:, h, 8:16], g.crep[:, h, :])
                link(last)
                link(v.tensor_copy(g.posf[:, i * H:(i + 1) * H, :], pos[:, i * H:(i + 1) * H, :]))
                link(v.tensor_copy(smx[:, 0:H], best[:, :, 0]))
                v.tensor_tensor(best, best, smx[:, 0:H].unsqueeze(2).broadcast_to([P, H, TOP]), ALU.subtract
                                ).then_inc(s["sm_diff"], 1)
                yield
                for hp in range(4):
                    p_ = g.posf[:, i * H + 2 * hp:i * H + 2 * hp + 2, :]
                    c_ = g.cid[:, i * H + 2 * hp:i * H + 2 * hp + 2, :]
                    link(v.tensor_tensor(g.eq.rearrange("p h k n -> p (h k) n"),
                                         p_.rearrange("p h k -> p (h k)").unsqueeze(2).broadcast_to([P, 2 * TOP, NC]),
                                         iota[:].unsqueeze(1).broadcast_to([P, 2 * TOP, NC]), ALU.is_equal))
                    link(v.tensor_tensor(g.eq, g.eq, c_.unsqueeze(2).broadcast_to([P, 2, TOP, NC]), ALU.mult))
                    at = slice(2 * hp * TOP, (2 * hp + 2) * TOP)
                    link(v.tensor_reduce(eid_s[:, at].rearrange("p (h k) -> p h k", k=TOP), g.eq, AX.X, ALU.add))
                    link(v.tensor_copy(eid[:, b, at], eid_s[:, at]))
                    if b == 0:
                        dve.sem_inc(S["first_ids"], 1)
                    yield
                dve.wait_ge(s["sm_exp"], turn + 1)
                link(v.tensor_reduce(smx[:, 0:H], best, AX.X, ALU.add))
                link(v.reciprocal(smx[:, 0:H], smx[:, 0:H]))
                yield
                v.tensor_tensor(best, best, smx[:, 0:H].unsqueeze(2).broadcast_to([P, H, TOP]), ALU.mult
                                ).then_inc(s["routes"], 1)
                dve.wait_ge(s["routes"], turn + 1)
                yield

            for _ in front(G1):
                pass

            def dot(j, r, x, turn):
                dve.wait_ge(s_row[r], turn * 16 + 16)
                return v.scalar_tensor_tensor(out=rows[:, r, 0:D], in0=rows[:, r, 0:D], scalar=1.0, in1=x,
                                              op0=ALU.mult, op1=ALU.mult, accum_out=act[:, j:j + 1])

            def weight(j, gate_):
                return v.tensor_scalar(diag[:, j, :], ident[:], gel[:, j:j + 1], gate_, ALU.mult, ALU.mult)

            routing = (None for i in range(1, NB1) for _ in route(G1, i))

            def peer(tick):
                if tick < TICKS:
                    dot(tick % 4, tick % RB1, xn1[:, tick // NSLOT, :], tick // RB1).then_inc(S["dots"], 1)
                if tick >= 1:
                    n = tick - 1
                    b, slot = n // NSLOT, n % NSLOT
                    dve.wait_ge(S["gelu"], n + 1)
                    if n >= 4:
                        dve.wait_ge(S["rows_used"], n - 3)
                    weight(n % 4, gate[:, b, slot:slot + 1]).then_inc(S["weights"], 1)
                    if slot == NSLOT - 1:
                        dve.wait_ge(S["acc_done"], b + 1)
                        v.tensor_tensor(xn1[:, b, :], bank2(0), gt2[:], ALU.mult).then_inc(S["acc_read"], 1)
                if tick % 2 == 0:
                    next(routing, None)

            interleave(peer, front(G2))
            peer(TICKS)

            def x2(n):
                b = finals[n]
                w = width(b)
                xn = xn1[:, b, :] if b < NB1 else xn2[:, b - NB1, :]
                v.tensor_tensor(x1_again(b)[0:w, :], x1_again(b)[0:w, :], xn[0:w, :], ALU.add).then_inc(S["x2_done"], 1)

            def mean_squares(turn, lo, hi):
                dve.wait_ge(S["fin_sq"], hi)
                v.tensor_scalar(stat[:, 0, lo:hi], stat[:, 0, lo:hi], 1.0 / D, EPS, ALU.mult, ALU.add
                                ).then_inc(S["fin_ms"], 1)

            def y(n):
                b = finals[n]
                w = width(b)
                v.scalar_tensor_tensor(out=x1_again(b)[0:w, :], in0=x1_again(b)[0:w, :], scalar=stat[0:w, 2, n:n + 1],
                                       in1=gfin[0:w, :], op0=ALU.mult, op1=ALU.mult).then_inc(S["y_ready"], 1)

            def early_norm():
                dve.wait_ge(S["x1_back"], 16 * NBT)
                dve.wait_ge(S["gfin_in"], 16)
                dve.wait_ge(S["acc_read"], NB)
                for n in range(NB):
                    x2(n)
                    yield
                yield
                mean_squares(1, 0, NB)
                yield from gap(2)
                dve.wait_ge(S["fin_root"], 1)
                rsqrt(0, NB)
                yield
                for n in range(NB):
                    y(n)
                    yield

            def to_slots():
                for r in range(4):
                    at = slice(32 * r, 32 * r + 32)
                    v.transpose(sT[at, 0, :], eid_s[0:32, at])
                    last = v.transpose(sT[at, 1, :], gate[0:32, NB, at])
                link(last)
                link(v.tensor_copy(gsT[:], sT[:, 1, 0:NS]))
                v.tensor_copy(idxs[:], sT[:, 0, 0:NS]).then_inc(S["idxs_ready"], 1)
                dve.wait_ge(S["idxs_ready"], 1)

            def last_routes():
                yield from route(G2, 3)
                to_slots()
                yield from route(G2, 4)

            def sample_weight(k):
                dve.wait_ge(S["s_gelu"], k + 1)
                v.tensor_scalar(wmask[:, k, :], eye8[:, k, :], gel[:, k % 4:k % 4 + 1], gsT[:, k:k + 1],
                                ALU.mult, ALU.mult).then_inc(S["s_weights"], 1)

            def samples(turn):
                for k in range(NS):
                    r = buffer2(k)
                    dve.wait_ge(s_row[r], 16 * (fills[r] + turn + 1))
                    dve.wait_ge(S["xb_mm"], k + 1)
                    v.scalar_tensor_tensor(out=rows[:, r, 0:D], in0=rows[:, r, 0:D], scalar=1.0, in1=bank2(pair(k)),
                                           op0=ALU.mult, op1=ALU.mult, accum_out=act[:, k % 4:k % 4 + 1]
                                           ).then_inc(S["s_dots"], 1)
                    if k >= 1:
                        sample_weight(k - 1)
                sample_weight(NS - 1)

            for bb in range(NB - NB1):
                b = NB1 + bb
                last_block = b == NB - 1
                if last_block:
                    beside = early_norm()
                else:
                    beside = route(G2, bb + 1) if b < NB - 2 else last_routes()
                x = xn2[:, bb, :]
                turns = bb * 16
                if last_block:
                    samples(turns)
                    turns += 1
                extra = S_GROUPS if last_block else 0

                def first_dots(q, turn):
                    for k in range(2):
                        r = buffer2(2 * q + k)
                        last = dot((2 * q + k) % 4, r, x, turn + fills[r])
                    last.then_inc(S["dots"], 1)

                def weigh(gr, q, slot):
                    dve.wait_ge(S["gelu"], gr + (TICKS + 1))
                    dve.wait_ge(S["rows_used"], gr + (TICKS - 1 + extra))
                    for k in range(2):
                        last = weight((2 * q + k) % 4, gate[:, b, bass.ds(slot + k, 1)])
                    last.then_inc(S["weights"], 1)

                first_dots(0, turns)
                if last_block:
                    dve.wait_ge(S["rows_used"], TICKS + bb * 64 + S_GROUPS)
                    v.tensor_tensor(xn2[0:NS, 4, :], bank2(0)[0:NS, :], gts, ALU.mult).then_inc(S["acc_read"], 1)
                for q in range(1, EARLY):
                    first_dots(q, turns + q // 4)
                    weigh(bb * 64 + q - 1, q - 1, 2 * (q - 1))
                    next(beside, None)
                for _ in beside:
                    pass
                with dve.Fori(0, 4) as m:
                    for q in range(EARLY, EARLY + 8):
                        first_dots(q, m * 2 + (turns + q // 4))
                        weigh(m * 8 + (bb * 64 + q - 1), q - 1, m * 16 + 2 * (q - 1))
                for q in range(57, 64):
                    first_dots(q, turns + q // 4)
                    weigh(bb * 64 + q - 1, q - 1, 2 * (q - 1))
                weigh(bb * 64 + 63, 63, 126)
                dve.wait_ge(S["acc_done"], b + 1)
                v.tensor_tensor(x, bank2(0), gt2[:], ALU.mult).then_inc(S["acc_read"], 1)
            dve.wait_ge(S["acc_read"], NBT)
            x2(NB)
            mean_squares(2, NB, NBT)
            dve.wait_ge(S["fin_root"], 2)
            rsqrt(NB, NBT)
            y(NB)


def kernel(**inputs):
    import concourse.bacc as bacc
    from concourse.bass_utils import run_bass_kernel_spmd

    a = {k: np.asarray(v) for k, v in inputs.items()}

    def cm(v):
        return v.reshape(-1, P).T

    ins = {
        "x": np.concatenate([a["x_prompt"][0], a["x_sample"][:, 0]], 0),
        "cT": np.concatenate([a["c_prompt"], a["c_sample"]], 0).T.reshape(KC, P, 1 + NS).transpose(1, 0, 2),
        "bada": cm(a["b_ada"][0]),
        "gmix": cm(a["g_mix"][0]),
        "gffn": cm(a["g_ffn"][0]),
        "w_dw": a["w_dw"][0].T.reshape(CC, P, W).transpose(1, 0, 2),
        "cvec": np.stack([cm(a["b_dw"][0]), cm(a["g_cn"][0]), cm(a["b_cn"][0])], 1),
        "keys": np.stack([a["k1"][0].T, a["k2"][0].T], 1),
        "wsT": a["w_s"][0].transpose(2, 0, 1),
        "state_T": a["state_conv"][0].transpose(2, 0, 1).reshape(CC, P, NS, W - 1).transpose(1, 0, 2, 3),
        "b_s": a["b_s"][0],
        "w_s00": a["w_s"][0][:, 0, 0:1],
        "g_v": a["g_v"],
        "b_v": a["b_v"],
        "g_final": a["g_final"][None],
        "w_ada": a["w_ada"][0],
        "w_in": a["w_in"][0],
        "w_conv_out": a["w_conv_out"][0],
        "w_gmlp_out": a["w_gmlp_out"][0],
        "w_out": a["w_out"][0],
        "w_q": a["w_q"][0],
        "experts": np.concatenate([a["u_tab"][0], a["v_tab"][0]], 1),
    }
    scratch = {"x1_rows": (NT, D)}
    outs = {
        "out_y": (NT, D),
        "out_hist_p": (P, CC, W - 1),
        "out_hist_s": (P, CC, NS, W - 1),
        "out_v": (NS, DC),
    }
    nc = bacc.Bacc("TRN2", target_bir_lowering=False, num_devices=1)
    arrays, t = {}, {}
    for name, v in ins.items():
        v = np.ascontiguousarray(v)
        arrays[f"in_{name}"] = v
        t[name] = nc.dram_tensor(f"in_{name}", v.shape, mybir.dt.from_np(v.dtype), kind="ExternalInput").ap()
    for name, shape in outs.items():
        t[name] = nc.dram_tensor(name, shape, mybir.dt.float32, kind="ExternalOutput").ap()
    for name, shape in scratch.items():
        t[name] = nc.dram_tensor(name, shape, mybir.dt.float32, kind="Internal").ap()
    build(nc, t)
    got = run_bass_kernel_spmd(nc, [arrays], core_ids=[0]).results[0]
    y = got["out_y"]
    hist_p = got["out_hist_p"].transpose(2, 1, 0).reshape(1, 1, W - 1, DC)
    hist_s = got["out_hist_s"].transpose(2, 3, 1, 0).reshape(1, NS, W - 1, DC)
    return (y[:NP].reshape(1, NP, D), y[NP:].reshape(NS, 1, D), hist_p, hist_s, got["out_v"].reshape(1, NS, 1, DC))
```
